# Optimizing a Trainium2 kernel written in Bass

```python
import jax
import jax.numpy as jnp
from jax import lax
import numpy as np
import jax, jax.numpy as jnp

D_MODEL = 1024
BATCH = 1
SEQ = 512
DEPTH = 2

N_MIXERS = 2
N_A_LAYERS = (DEPTH + 1) // 2
N_B_LAYERS = DEPTH // 2

HG_EXPAND = 128
HG_HEADS = D_MODEL // HG_EXPAND
HG_KDIM = HG_EXPAND
HG_VDIM = D_MODEL // HG_HEADS
HG_CHUNK = 32

ATT_HEAD_DIM = 128
ATT_HEADS = D_MODEL // ATT_HEAD_DIM
DILATED_GROUPS = ((128, 1), (512, 4), (2048, 16))
N_GROUPS = len(DILATED_GROUPS)
ATT_QKV_COLS = N_GROUPS * 3 * ATT_HEADS * ATT_HEAD_DIM
ROPE_THETA = 500000.0
ROPE_DIM = ATT_HEAD_DIM // 4

D_FF = -(-(8 * D_MODEL) // (3 * 256)) * 256

NORM_EPS = 1e-6


def rms_norm(x, g):
    xf = x.astype(jnp.float32)
    y = xf * lax.rsqrt(jnp.mean(xf * xf, axis=-1, keepdims=True) + NORM_EPS)
    return (y * g.astype(jnp.float32)).astype(x.dtype)

def apply_partial_rope(t, cos, sin):
    half = ROPE_DIM // 2
    t1 = t[..., :half]
    t2 = t[..., half:ROPE_DIM]
    return jnp.concatenate([t1 * cos - t2 * sin, t2 * cos + t1 * sin, t[..., ROPE_DIM:]], axis=-1)

def hgrn2_mixer(u, w_in, lb, norm_g, w_out):
    B, S, _ = u.shape
    H, K, C = HG_HEADS, HG_KDIM, HG_CHUNK
    proj = (u @ w_in).astype(jnp.float32).reshape(B, S, 4, H, K)
    q_raw, f_raw, v, g = proj[:, :, 0], proj[:, :, 1], proj[:, :, 2], proj[:, :, 3]
    lb = lb.astype(jnp.float32).reshape(H, K)
    log_f = jnp.log(lb + (1.0 - lb) * jax.nn.sigmoid(f_raw))
    k = (1.0 - lb) * jax.nn.sigmoid(-f_raw)
    q = jax.nn.silu(q_raw)
    NC = S // C
    rs = lambda t: t.reshape(B, NC, C, H, t.shape[-1])
    q, k, v, log_f = rs(q), rs(k), rs(v), rs(log_f)
    b = jnp.cumsum(log_f, axis=2)
    q_dec = q * jnp.exp(b)
    k_inv = k * jnp.exp(-b)
    causal = jnp.tril(jnp.ones((C, C), dtype=bool))
    a = jnp.einsum('bnchk,bnshk->bnhcs', q_dec, k_inv)
    a = jnp.where(causal, a, 0.0)
    o_intra = jnp.einsum('bnhcs,bnshv->bnchv', a, v)
    b_last = b[:, :, -1:]
    k_end = k * jnp.exp(b_last - b)
    chunk_decay = jnp.exp(b_last[:, :, 0])

    def step(state, xs):
        q_c, k_c, v_c, dec = xs
        o_c = jnp.einsum('bchk,bhkv->bchv', q_c, state)
        state = dec[..., None] * state + jnp.einsum('bchk,bchv->bhkv', k_c, v_c)
        return state, o_c

    xs = (jnp.moveaxis(q_dec, 1, 0), jnp.moveaxis(k_end, 1, 0),
          jnp.moveaxis(v, 1, 0), jnp.moveaxis(chunk_decay, 1, 0))
    state0 = jnp.zeros((B, H, K, HG_VDIM), jnp.float32)
    _, o_inter = lax.scan(step, state0, xs)
    o = (o_intra + jnp.moveaxis(o_inter, 0, 1)).reshape(B, S, H, HG_VDIM)
    o = o * lax.rsqrt(jnp.mean(o * o, axis=-1, keepdims=True) + NORM_EPS)
    o = o * norm_g.astype(jnp.float32).reshape(H, HG_VDIM)
    o = o.reshape(B, S, D_MODEL) * jax.nn.silu(g.reshape(B, S, D_MODEL))
    return o.astype(u.dtype) @ w_out

def dilated_group_attention(q, k, v, window, dilation):
    B, S, H, Dh = q.shape
    L = S // dilation
    n_win = window // dilation
    blk = n_win
    nb = -(-L // blk)
    Lp = nb * blk

    def gather(t):
        t = t.reshape(B, L, dilation, H, Dh).transpose(0, 2, 1, 3, 4).reshape(B * dilation, L, H, Dh)
        t = jnp.pad(t, ((0, 0), (0, Lp - L), (0, 0), (0, 0)))
        return t.reshape(B * dilation, nb, blk, H, Dh)

    def with_prev(t):
        prev = jnp.pad(t, ((0, 0), (1, 0), (0, 0), (0, 0), (0, 0)))[:, :-1]
        return jnp.concatenate([prev, t], axis=2)

    qb = gather(q)
    kw = with_prev(gather(k))
    vw = with_prev(gather(v))
    s = jnp.einsum('bnqhd,bnkhd->bnhqk', qb, kw)
    qi = jnp.arange(blk)[:, None]
    ki = jnp.arange(2 * blk)[None, :]
    dist = blk + qi - ki
    band = (dist >= 0) & (dist <= n_win)
    has_prev = (jnp.arange(nb)[:, None, None] > 0) | (ki >= blk)[None]
    valid = band[None] & has_prev
    s = jnp.where(valid[None, :, None], s, -jnp.inf)
    m = jnp.max(s, axis=-1, keepdims=True)
    p = jnp.exp(s - m)
    z = jnp.sum(p, axis=-1, keepdims=True)
    o = jnp.einsum('bnhqk,bnkhd->bnqhd', p, vw) / jnp.swapaxes(z, 2, 3)
    lse = jnp.swapaxes((m + jnp.log(z))[..., 0], 2, 3)

    def scatter_back(t):
        rest = t.shape[3:]
        t = t.reshape(B, dilation, Lp, *rest)[:, :, :L]
        return jnp.moveaxis(t, 1, 2).reshape(B, S, *rest)

    return scatter_back(o), scatter_back(lse)

def dilated_attention_mixer(u, cos, sin, w_in, w_out):
    B, S, _ = u.shape
    proj = (u @ w_in).astype(jnp.float32).reshape(B, S, N_GROUPS, 3, ATT_HEADS, ATT_HEAD_DIM)
    scale = ATT_HEAD_DIM ** -0.5
    outs = []
    lses = []
    for gi, (window, dilation) in enumerate(DILATED_GROUPS):
        q = apply_partial_rope(proj[:, :, gi, 0], cos, sin) * scale
        k = apply_partial_rope(proj[:, :, gi, 1], cos, sin)
        v = proj[:, :, gi, 2]
        o_g, lse_g = dilated_group_attention(q, k, v, window, dilation)
        outs.append(o_g)
        lses.append(lse_g)
    wts = jax.nn.softmax(jnp.stack(lses, axis=0), axis=0)
    o = jnp.einsum('gbsh,gbshd->bshd', wts, jnp.stack(outs, axis=0))
    return o.reshape(B, S, D_MODEL).astype(u.dtype) @ w_out

def swiglu_ffn(u, w_in, w_out):
    gate, up = jnp.split(u @ w_in, 2, axis=-1)
    return (jax.nn.silu(gate) * up) @ w_out

def first_inputs(seed: int = 0) -> dict:
    key = jax.random.key(seed)
    ks = jax.random.split(key, 16)
    D = D_MODEL
    nrm = jax.random.normal
    x = nrm(ks[0], (BATCH, SEQ, D), jnp.float32)
    c = nrm(ks[1], (BATCH, D), jnp.float32)
    offset = jax.random.randint(ks[2], (BATCH, 1), 0, 1024, dtype=jnp.int32)
    positions = offset + jnp.arange(SEQ, dtype=jnp.int32)[None, :]
    ada_w = nrm(ks[3], (DEPTH, D, 6 * D), jnp.float32) * (0.5 * D ** -0.5)
    ada_b = nrm(ks[4], (DEPTH, 6 * D), jnp.float32) * 0.02
    norm_g = 1.0 + 0.05 * nrm(ks[5], (DEPTH, 4, D), jnp.float32)
    hgrn_w_in = nrm(ks[6], (N_A_LAYERS, D, 4 * D), jnp.float32) * D ** -0.5
    hgrn_lower_bounds = 1.0 + 0.5 * nrm(ks[7], (N_A_LAYERS, D), jnp.float32)
    hgrn_norm_g = 1.0 + 0.05 * nrm(ks[8], (N_A_LAYERS, D), jnp.float32)
    hgrn_w_out = nrm(ks[9], (N_A_LAYERS, D, D), jnp.float32) * D ** -0.5
    attn_w_in = nrm(ks[10], (N_B_LAYERS, D, ATT_QKV_COLS), jnp.float32) * D ** -0.5
    attn_w_out = nrm(ks[11], (N_B_LAYERS, D, D), jnp.float32) * D ** -0.5
    ffn_w_in = nrm(ks[12], (DEPTH, D, 2 * D_FF), jnp.float32) * D ** -0.5
    ffn_w_out = nrm(ks[13], (DEPTH, D_FF, D), jnp.float32) * D_FF ** -0.5
    return {'x': x, 'c': c, 'positions': positions, 'ada_w': ada_w, 'ada_b': ada_b,
            'norm_g': norm_g, 'hgrn_w_in': hgrn_w_in, 'hgrn_lower_bounds': hgrn_lower_bounds,
            'hgrn_norm_g': hgrn_norm_g, 'hgrn_w_out': hgrn_w_out, 'attn_w_in': attn_w_in,
            'attn_w_out': attn_w_out, 'ffn_w_in': ffn_w_in, 'ffn_w_out': ffn_w_out}

def first_block(x, c, positions, ada_w, ada_b, norm_g, hgrn_w_in, hgrn_lower_bounds,
              hgrn_norm_g, hgrn_w_out, attn_w_in, attn_w_out, ffn_w_in, ffn_w_out):
    cond = jax.nn.silu(c)
    inv_freq = ROPE_THETA ** (-jnp.arange(0, ROPE_DIM, 2, dtype=jnp.float32) / ROPE_DIM)
    ang = positions.astype(jnp.float32)[..., None] * inv_freq
    cos = jnp.cos(ang)[:, :, None, :]
    sin = jnp.sin(ang)[:, :, None, :]
    lbs = jnp.cumsum(jax.nn.softmax(hgrn_lower_bounds.astype(jnp.float32), axis=0), axis=0)
    lbs = lbs - lbs[0:1]
    h = x
    for layer in range(DEPTH):
        mod = (cond @ ada_w[layer] + ada_b[layer])[:, None, :]
        sh1, sc1, g1, sh2, sc2, g2 = jnp.split(mod, 6, axis=-1)
        u = rms_norm(h, norm_g[layer, 0]) * (1.0 + sc1) + sh1
        idx = layer // N_MIXERS
        if layer % N_MIXERS == 0:
            y = hgrn2_mixer(u, hgrn_w_in[idx], lbs[idx], hgrn_norm_g[idx], hgrn_w_out[idx])
        else:
            y = dilated_attention_mixer(u, cos, sin, attn_w_in[idx], attn_w_out[idx])
        h = h + (1.0 + g1) * rms_norm(y, norm_g[layer, 1])
        u = rms_norm(h, norm_g[layer, 2]) * (1.0 + sc2) + sh2
        y = swiglu_ffn(u, ffn_w_in[layer], ffn_w_out[layer])
        h = h + (1.0 + g2) * rms_norm(y, norm_g[layer, 3])
    return h


ATT_HEADS_2 = 8
ATT_KV_HEADS = 2
ATT_HEAD_DIM_2 = 64
ATT_GROUP = ATT_HEADS_2 // ATT_KV_HEADS
WINDOW = 128
ATT_BLOCK = 128
ROPE_DIM_2 = ATT_HEAD_DIM_2 // 4
M_HEADS = 4
M_QK_DIM = 64
M_V_DIM = 128
M_CHUNK = 64
D_FF_2 = 4 * D_MODEL
EPS = 1e-6

ATT_Q_W = ATT_HEADS_2 * ATT_HEAD_DIM_2
ATT_KV_W = ATT_KV_HEADS * ATT_HEAD_DIM_2
M_QK_W = M_HEADS * M_QK_DIM
M_V_W = M_HEADS * M_V_DIM
IN_WIDTHS = (ATT_Q_W, ATT_KV_W, ATT_KV_W, M_QK_W, M_QK_W, M_V_W, M_V_W, 2 * M_HEADS, 2 * D_MODEL)
D_IN = sum(IN_WIDTHS)


def rmsnorm(x, gain):
    x32 = x.astype(jnp.float32)
    inv = lax.rsqrt(jnp.mean(x32 * x32, axis=-1, keepdims=True) + EPS)
    return (x32 * inv).astype(x.dtype) * gain

def rope_tables(seq_len):
    pos = jnp.arange(seq_len, dtype=jnp.float32)
    inv_freq = ROPE_THETA ** (-jnp.arange(0, ROPE_DIM_2, 2, dtype=jnp.float32) / ROPE_DIM_2)
    ang = pos[:, None] * inv_freq[None, :]
    return jnp.cos(ang), jnp.sin(ang)

def partial_rope(x, cos, sin):
    half = ROPE_DIM_2 // 2
    x1 = x[..., :half].astype(jnp.float32)
    x2 = x[..., half:ROPE_DIM_2].astype(jnp.float32)
    c = cos[None, :, None, :]
    s = sin[None, :, None, :]
    return jnp.concatenate([(x1 * c - x2 * s).astype(x.dtype),
                            (x2 * c + x1 * s).astype(x.dtype),
                            x[..., ROPE_DIM_2:]], axis=-1)

def sliding_window_attention(q, k, v, sinks):
    B, S, _, hd = q.shape
    nb = S // ATT_BLOCK
    qb = q.reshape(B, nb, ATT_BLOCK, ATT_KV_HEADS, ATT_GROUP, hd)

    def with_prev(t):
        tb = t.reshape(B, nb, ATT_BLOCK, ATT_KV_HEADS, hd)
        prev = jnp.pad(tb, ((0, 0), (1, 0), (0, 0), (0, 0), (0, 0)))[:, :-1]
        return jnp.concatenate([prev, tb], axis=2)

    kb, vb = with_prev(k), with_prev(v)
    scores = jnp.einsum('bnqhgd,bnkhd->bnhgqk', qb, kb).astype(jnp.float32) * (hd ** -0.5)
    blk = jnp.arange(nb)[:, None, None]
    qpos = blk * ATT_BLOCK + jnp.arange(ATT_BLOCK)[None, :, None]
    kpos = (blk - 1) * ATT_BLOCK + jnp.arange(2 * ATT_BLOCK)[None, None, :]
    valid = (kpos >= 0) & (kpos <= qpos) & (qpos - kpos < WINDOW)
    scores = jnp.where(valid[None, :, None, None], scores, -jnp.inf)
    sink = sinks.astype(jnp.float32).reshape(ATT_KV_HEADS, ATT_GROUP)[None, None, :, :, None, None]
    m = jnp.maximum(jnp.max(scores, axis=-1, keepdims=True), sink)
    p = jnp.exp(scores - m)
    probs = (p / (jnp.sum(p, axis=-1, keepdims=True) + jnp.exp(sink - m))).astype(v.dtype)
    out = jnp.einsum('bnhgqk,bnkhd->bnqhgd', probs, vb)
    return out.reshape(B, S, ATT_HEADS_2 * hd)

def mlstm_chunkwise(q, k, v, i_pre, f_pre):
    f32 = jnp.float32
    B, S, H, dk = q.shape
    dv = v.shape[-1]
    L = M_CHUNK
    nc = S // L

    def chunks(t):
        return t.astype(f32).reshape(B, nc, L, H, -1).transpose(0, 1, 3, 2, 4)

    q = chunks(q) * (dk ** -0.5)
    k = chunks(k)
    v = chunks(v)
    log_f = jax.nn.log_sigmoid(f_pre.astype(f32)).reshape(B, nc, L, H).transpose(0, 1, 3, 2)
    log_i = i_pre.astype(f32).reshape(B, nc, L, H).transpose(0, 1, 3, 2)
    b = jnp.cumsum(log_f, axis=-1)
    g = b[..., -1]

    w_end = g[..., None] - b + log_i
    m_loc = jnp.max(w_end, axis=-1)
    e = jnp.exp(w_end - m_loc[..., None])
    dC = jnp.einsum('bnhlv,bnhlk->bnhvk', v * e[..., None], k)
    dn = jnp.einsum('bnhl,bnhlk->bnhk', e, k)

    def step(carry, inp):
        C, n, m = carry
        dC_c, dn_c, g_c, m_loc_c = inp
        m_new = jnp.maximum(g_c + m, m_loc_c)
        a = jnp.exp(g_c + m - m_new)
        s = jnp.exp(m_loc_c - m_new)
        C_new = a[..., None, None] * C + s[..., None, None] * dC_c
        n_new = a[..., None] * n + s[..., None] * dn_c
        return (C_new, n_new, m_new), (C, n, m)

    init = (jnp.zeros((B, H, dv, dk), f32), jnp.zeros((B, H, dk), f32), jnp.zeros((B, H), f32))
    xs = (jnp.moveaxis(dC, 1, 0), jnp.moveaxis(dn, 1, 0), jnp.moveaxis(g, 1, 0), jnp.moveaxis(m_loc, 1, 0))
    _, (C_prev, n_prev, m_prev) = lax.scan(step, init, xs)
    C_prev = jnp.moveaxis(C_prev, 0, 1)
    n_prev = jnp.moveaxis(n_prev, 0, 1)
    m_prev = jnp.moveaxis(m_prev, 0, 1)

    causal = jnp.tril(jnp.ones((L, L), dtype=bool))
    log_d = jnp.where(causal, b[..., :, None] - b[..., None, :] + log_i[..., None, :], -jnp.inf)
    log_inter = b + m_prev[..., None]
    m_t = jnp.maximum(log_inter, jnp.max(log_d, axis=-1))
    w = jnp.exp(log_d - m_t[..., None]) * jnp.einsum('bnhlk,bnhsk->bnhls', q, k)
    a_inter = jnp.exp(log_inter - m_t)
    num = jnp.einsum('bnhls,bnhsv->bnhlv', w, v) + a_inter[..., None] * jnp.einsum('bnhvk,bnhlk->bnhlv', C_prev, q)
    den = jnp.sum(w, axis=-1) + a_inter * jnp.einsum('bnhk,bnhlk->bnhl', n_prev, q)
    h = num / jnp.maximum(jnp.abs(den), jnp.exp(-m_t))[..., None]
    return h.transpose(0, 1, 3, 2, 4).reshape(B, S, H, dv)

def hybrid_layer(x, cos, sin, norm_mix, w_in, att_q_norm, att_k_norm, att_sinks, m_gate_bias,
                 m_head_norm, w_att_branch, w_m_branch, w_out, norm_ffn, w_ff1, w_ff2):
    B, S, _ = x.shape
    h = rmsnorm(x, norm_mix)
    z = h @ w_in
    splits = [int(s) for s in np.cumsum(IN_WIDTHS)[:-1]]
    q_a, k_a, v_a, q_m, k_m, v_m, o_m, if_m, gates = jnp.split(z, splits, axis=-1)

    q_a = partial_rope(rmsnorm(q_a.reshape(B, S, ATT_HEADS_2, ATT_HEAD_DIM_2), att_q_norm), cos, sin)
    k_a = partial_rope(rmsnorm(k_a.reshape(B, S, ATT_KV_HEADS, ATT_HEAD_DIM_2), att_k_norm), cos, sin)
    v_a = v_a.reshape(B, S, ATT_KV_HEADS, ATT_HEAD_DIM_2)
    att = sliding_window_attention(q_a, k_a, v_a, att_sinks)

    i_pre, f_pre = jnp.split(if_m + m_gate_bias, 2, axis=-1)
    hm = mlstm_chunkwise(q_m.reshape(B, S, M_HEADS, M_QK_DIM),
                         k_m.reshape(B, S, M_HEADS, M_QK_DIM),
                         v_m.reshape(B, S, M_HEADS, M_V_DIM), i_pre, f_pre).astype(x.dtype)
    hm = rmsnorm(hm, m_head_norm.reshape(M_HEADS, M_V_DIM)).reshape(B, S, M_V_W)
    hm = hm * jax.nn.sigmoid(o_m)

    g_a, g_m = jnp.split(gates, 2, axis=-1)
    mixed = jax.nn.sigmoid(g_a) * (att @ w_att_branch) + jax.nn.sigmoid(g_m) * (hm @ w_m_branch)
    x = x + mixed @ w_out

    u = jax.nn.relu(rmsnorm(x, norm_ffn) @ w_ff1)
    return x + (u * u) @ w_ff2

def second_inputs(seed: int = 0) -> dict:
    key = jax.random.key(seed)
    ks = jax.random.split(key, 16)
    nrm = jax.random.normal
    f32 = jnp.float32
    x = nrm(ks[0], (BATCH, SEQ, D_MODEL), f32)
    norm_mix = 1.0 + 0.02 * nrm(ks[1], (DEPTH, D_MODEL), f32)
    w_in = nrm(ks[2], (DEPTH, D_MODEL, D_IN), f32) * D_MODEL ** -0.5
    att_q_norm = 1.0 + 0.02 * nrm(ks[3], (DEPTH, ATT_HEAD_DIM_2), f32)
    att_k_norm = 1.0 + 0.02 * nrm(ks[4], (DEPTH, ATT_HEAD_DIM_2), f32)
    att_sinks = 0.5 * nrm(ks[5], (DEPTH, ATT_HEADS_2), f32)
    i_bias = -1.0 + 0.1 * nrm(ks[6], (DEPTH, M_HEADS), f32)
    f_bias = 3.0 + 0.5 * nrm(ks[7], (DEPTH, M_HEADS), f32)
    m_gate_bias = jnp.concatenate([i_bias, f_bias], axis=-1)
    m_head_norm = 1.0 + 0.02 * nrm(ks[8], (DEPTH, M_V_W), f32)
    w_att_branch = nrm(ks[9], (DEPTH, ATT_Q_W, D_MODEL), f32) * ATT_Q_W ** -0.5
    w_m_branch = nrm(ks[10], (DEPTH, M_V_W, D_MODEL), f32) * M_V_W ** -0.5
    w_out = nrm(ks[11], (DEPTH, D_MODEL, D_MODEL), f32) * D_MODEL ** -0.5
    norm_ffn = 1.0 + 0.02 * nrm(ks[12], (DEPTH, D_MODEL), f32)
    w_ff1 = nrm(ks[13], (DEPTH, D_MODEL, D_FF_2), f32) * D_MODEL ** -0.5
    w_ff2 = nrm(ks[14], (DEPTH, D_FF_2, D_MODEL), f32) * D_FF_2 ** -0.5
    return {"x": x, "norm_mix": norm_mix, "w_in": w_in, "att_q_norm": att_q_norm,
            "att_k_norm": att_k_norm, "att_sinks": att_sinks, "m_gate_bias": m_gate_bias,
            "m_head_norm": m_head_norm, "w_att_branch": w_att_branch, "w_m_branch": w_m_branch,
            "w_out": w_out, "norm_ffn": norm_ffn, "w_ff1": w_ff1, "w_ff2": w_ff2}

def second_block(x, norm_mix, w_in, att_q_norm, att_k_norm, att_sinks, m_gate_bias, m_head_norm,
              w_att_branch, w_m_branch, w_out, norm_ffn, w_ff1, w_ff2):
    cos, sin = rope_tables(x.shape[1])
    for layer in range(DEPTH):
        x = hybrid_layer(x, cos, sin, norm_mix[layer], w_in[layer], att_q_norm[layer],
                         att_k_norm[layer], att_sinks[layer], m_gate_bias[layer],
                         m_head_norm[layer], w_att_branch[layer], w_m_branch[layer],
                         w_out[layer], norm_ffn[layer], w_ff1[layer], w_ff2[layer])
    return x


def setup_inputs(seed=0):
    out = dict(first_inputs(seed))
    for name, value in second_inputs(seed + 1).items():
        if name != "x":
            out[name + "_2"] = value
    return out


def reference(
    x, c, positions, ada_w, ada_b, norm_g, hgrn_w_in, hgrn_lower_bounds, hgrn_norm_g,
    hgrn_w_out, attn_w_in, attn_w_out, ffn_w_in, ffn_w_out, norm_mix_2, w_in_2, att_q_norm_2,
    att_k_norm_2, att_sinks_2, m_gate_bias_2, m_head_norm_2, w_att_branch_2, w_m_branch_2,
    w_out_2, norm_ffn_2, w_ff1_2, w_ff2_2,
):
    x = first_block(
        x, c, positions, ada_w, ada_b, norm_g, hgrn_w_in, hgrn_lower_bounds, hgrn_norm_g,
        hgrn_w_out, attn_w_in, attn_w_out, ffn_w_in, ffn_w_out,
    )
    return second_block(
        x, norm_mix_2, w_in_2, att_q_norm_2, att_k_norm_2, att_sinks_2, m_gate_bias_2,
        m_head_norm_2, w_att_branch_2, w_m_branch_2, w_out_2, norm_ffn_2, w_ff1_2, w_ff2_2,
    )


_drawn_inputs = setup_inputs


def setup_inputs(seed=0):
    import zlib

    import numpy as np

    out = dict(_drawn_inputs(seed))
    spreads = {}
    factors = {'norm_mix_2': 6.487,
     'att_q_norm_2': 8.0,
     'att_k_norm_2': 8.0,
     'att_sinks_2': 34.363,
     'm_head_norm_2': 8.0,
     'norm_ffn_2': 3.713}
    for name, (base, spread) in spreads.items():
        noise = np.random.default_rng([zlib.crc32(name.encode()), seed]).standard_normal(out[name].shape)
        drawn = base * np.exp(spread * noise) if base else spread * noise
        out[name] = jnp.asarray(drawn.astype(out[name].dtype))
    for name, factor in factors.items():
        out[name] = (out[name] * factor).astype(out[name].dtype)
    return out
```

```python
import concourse.bass as bass
import numpy as np
from concourse import mybir
from contextlib import ExitStack

F32 = mybir.dt.float32
F32R = mybir.dt.float32r
BF16 = mybir.dt.bfloat16
U16 = mybir.dt.uint16
I32 = mybir.dt.int32
ACT = mybir.ActivationFunctionType
ALU = mybir.AluOpType
AX = mybir.AxisListType.X

P = 128
S = 512
D = 1024
KT = D // P
TB = S // P
NEG = -1.0e30
EPS = 1e-6

HG_HEADS, HG_CHUNK = 8, 32
ATT_HEADS, GROUPS = 8, 3
ATT_SCALE = 128 ** -0.5
ROPE_THETA = 500000.0
FF1 = 2816
FF1_TILES = (12, 10)
SW_HEADS, SW_DIM = 8, 64
M_HEADS, M_CHUNK, M_DK = 4, 64, 64
FF2 = 4096
Z = {"q_a": 0, "k_a": 512, "v_a": 640, "q_m": 768, "k_m": 1024, "v_m": 1280, "o_m": 1792, "if": 2304, "gate": 2312}
ADA_BLOCKS = 12
ADA_FIRST = 5


def constants():
    r = np.arange(P)
    f = {}
    f["ident"] = np.eye(P)
    f["ones"] = np.ones((P, P))
    f["half"] = (r[:, None] // 64 == r[None, :] // 64)
    s, c = r[:, None], r[None, :]
    mask32 = (s // HG_CHUNK == c // HG_CHUNK) & (s <= c)
    inv = ROPE_THETA ** (-np.arange(0, 32, 2, dtype=np.float32) / np.float32(32))
    freq = np.zeros((P, 1), np.float32)
    freq[:32, 0] = np.tile(inv.astype(np.float32), 2)
    f["freq"] = freq
    sign = np.zeros((P, 1))
    sign[:16], sign[16:32] = -1, 1
    f["sign"] = sign
    q8 = np.zeros((P, 2))
    q8[:64, 0] = q8[64:, 1] = M_DK ** -0.5
    f["q8"] = q8
    first = {k: np.asarray(v, np.float32) for k, v in f.items()}

    g = {"mask32": mask32}
    inv2 = ROPE_THETA ** (-np.arange(0, 16, 2, dtype=np.float32) / np.float32(16))
    ang = np.arange(S, dtype=np.float32)[None, :] * inv2.astype(np.float32)[:, None]
    cos2, sin2 = np.ones((P, S)), np.zeros((P, S))
    for h in (0, 64):
        cos2[h:h + 8] = cos2[h + 8:h + 16] = np.cos(ang)
        sin2[h:h + 8], sin2[h + 8:h + 16] = -np.sin(ang), np.sin(ang)
    g["cos2"], g["sin2"] = cos2, sin2
    sel = []
    for kv in range(2):
        for half in range(2):
            m = np.zeros((P, P))
            m[kv * 64 + np.arange(64), half * 64 + np.arange(64)] = 1
            sel.append(m)
    g["selk"] = np.concatenate(sel, 1)
    sel4 = np.zeros((P, M_HEADS, P))
    for h in range(M_HEADS):
        sel4[h, h] = 1
    g["sel4"] = sel4.reshape(P, -1)
    second = {k: np.asarray(v, np.float32) for k, v in g.items()}

    q, k = r[:, None], r[None, :]
    n = lambda ok: np.where(ok, 0.0, NEG)
    off1, off2 = n((q - k) % 4 == 0), n((q - k) % 16 == 0)
    d1, d2 = n(((q - k) % 4 == 0) & (k <= q)), n(((q - k) % 16 == 0) & (k <= q))
    causal = n(k <= q)
    prev0 = n(k >= q)
    m = {"dil": np.concatenate([off1, off1, off1, d1, off2, off2, off2, d2, prev0, causal], 1)}
    prevw = n(k > q)
    full = np.full((P, P), NEG)
    m["sw"] = np.concatenate([full, causal, prevw, causal, prevw, causal, prevw, causal], 1)
    md = n((q // M_CHUNK == k // M_CHUNK) & (q <= k))
    m["ml"] = np.tile(md, (1, TB))
    m["identb"] = np.eye(P)
    masks = {k2: (np.ascontiguousarray(v, np.float32).view(np.uint32) >> 16).astype(np.uint16) for k2, v in m.items()}
    return first, second, masks


def pack(parts):
    at, where = 0, {}
    for k, v in parts.items():
        where[k] = (at, at + v.shape[1])
        at += v.shape[1]
    return np.ascontiguousarray(np.concatenate(list(parts.values()), 1)), where


class Counts:

    def __init__(self, eng):
        self.eng, self.seen, self.given = eng, {}, {}

    def take(self, sem, n=1):
        self.seen[sem] = self.seen.get(sem, 0) + n
        self.eng.wait_ge(sem, self.seen[sem])

    def skip(self, sem, n):
        self.seen[sem] = self.seen.get(sem, 0) + n

    def at(self, sem):
        return self.seen.get(sem, 0)

    def give(self, ins, sem, n=1):
        ins.then_inc(sem, n)
        self.given[sem] = self.given.get(sem, 0) + n

    def made(self, sem, n):
        self.given[sem] = self.given.get(sem, 0) + n

    def own(self, sem):
        self.eng.wait_ge(sem, self.given[sem])


def gemm_plan():
    plan, order = {}, []

    def add(name, blocks, ktiles, evictor):
        chunks = -(-ktiles // 4)
        order.append(name)
        plan[name] = dict(blocks=blocks, chunks=chunks, ktiles=ktiles, evictor=evictor)

    def ffn1(l):
        for half, n in enumerate(FF1_TILES):
            add(f"ffn_in{l}{half}", n // 2, KT, "dve")
            add(f"ffn_out{l}{half}", 2, n, "dve")

    add("hg_q", 2, KT, "act")
    add("hg_f", 2, KT, "act")
    add("hg_v", 2, KT, "act")
    add("hg_g", 2, KT, "act")
    add("hg_out", 2, KT, "dve")
    ffn1(0)
    add("at_v", 6, KT, "act")
    for p in range(4):
        add(f"at_qk{p}", 3, KT, "dve")
    add("at_out", 2, KT, "dve")
    ffn1(1)
    for l in range(2):
        add(f"z{l}", 5, KT, "act")
        add(f"zg{l}", 4, KT, "act")
        add(f"br{l}", 4, 4, "dve")
        add(f"mo{l}", 2, KT, "dve")
        for half in range(2):
            add(f"ff_in{l}{half}", 4, KT, "act")
            add(f"ff_out{l}{half}", 2, 16, "dve")
    c = t = inner = 0
    freed = {"act": 4, "dve": 4}
    for name in order:
        g = plan[name]
        g.update(c0=c, t0=t, inner0=inner, mine=freed[g["evictor"]], other=freed["dve" if g["evictor"] == "act" else "act"])
        c += g["blocks"] * g["chunks"]
        inner += g["blocks"] * (g["chunks"] - 1)
        t += 4 * g["blocks"]
        freed[g["evictor"]] += 4 * g["blocks"]
    return plan, order, c


def build(nc, a, out, where1, where2, where3, stop=None, probe=None):
    plan, order, n_chunks = gemm_plan()
    if stop is not None:
        order = order[:order.index(stop) + 1]
        n_chunks = plan[stop]["c0"] + plan[stop]["blocks"] * plan[stop]["chunks"]
    ctx = ExitStack()

    def sb(name, shape, dt=F32, stack=None):
        return (stack or ctx).enter_context(nc.sbuf_tensor(name, shape, dt))

    def sem(name):
        return ctx.enter_context(nc.semaphore(name))

    with ctx:
        hT = sb("hT", [P, KT, S])
        yT = sb("yT", [P, KT, S])
        u_hi, u_lo = sb("u_hi", [P, KT, S], F32R), sb("u_lo", [P, KT, S], F32R)
        raw = [sb(f"raw{i}", [P, 4, 512]) for i in range(2)]
        w_hi = [sb(f"w_hi{i}", [P, 4, 512], F32R) for i in range(2)]
        w_lo = [sb(f"w_lo{i}", [P, 4, 512], F32R) for i in range(2)]
        tmp = sb("tmp", [P, 8, S])
        con1 = sb("con1", [P, max(v[1] for v in where1.values())])
        cols_a, cols_b = sb("cols_a", [P, P]), sb("cols_b", [P, P])
        mod, mix, cond, lbc = sb("mod", [P, 96]), sb("mix", [P, 64]), sb("cond", [P, KT]), sb("lbc", [P, 4, KT])
        sinks, gbias, stat, mcol = sb("sinks", [P, 16]), sb("gbias", [4, 4]), sb("stat", [P, 32]), sb("mcol", [P, 64])
        with ExitStack() as room:
            masks = sb("masks", [P, max(v[1] for v in where3.values())], U16, room)
            cosT, sinT = sb("cosT", [P, S], F32, room), sb("sinT", [P, S], F32, room)
            sel4, selk = sb("sel4", [P, 512], F32, room), sb("selk", [P, 4, P], F32, room)
        ada_raw = sb("ada_raw", [P, 2, 4, 512])
        ada_room = ExitStack()
        acc, mask32 = sb("acc", [P, 512], F32, ada_room), sb("mask32_sb", [P, P], F32, ada_room)
        with ExitStack() as room:
            hg_q, hg_f, hg_g = (sb(n, [P, 8, S], F32, room) for n in ("hg_q", "hg_f", "hg_g"))
            hg_v = sb("hg_v", [P, TB, D], F32, room)
        with ExitStack() as room:
            hid_hi, hid_lo = (sb(n, [P, FF1_TILES[0], S], F32R, room) for n in ("hid_hi", "hid_lo"))
            silu_g, hid_f = (sb(n, [P, 2, S], F32, room) for n in ("silu_g", "hid_f"))
        ada_room.close()
        with ExitStack() as room:
            at_v = sb("at_v", [P, TB, GROUPS * D], F32, room)
            at_qk = sb("at_qk", [P, GROUPS, 4, S], F32, room)
        with ExitStack() as room:
            gate = sb("gate", [P, 16, S], F32, room)
            with ExitStack() as sub:
                z_km, z_vm = sb("z_km", [P, TB, 256], F32, sub), sb("z_vm", [P, TB, 512], F32, sub)
                z_om, z_if = sb("z_om", [P, 4, S], F32, sub), sb("z_if", [M_HEADS, 2, S], F32, sub)
                with ExitStack() as sub2:
                    z_q = sb("z_q", [P, 4, S], F32, sub2)
                    vpad = sb("vpad", [P, TB, 2, 2, P], F32, sub2)
                with ExitStack() as sub2:
                    row = sb("row", [M_HEADS, 4, S], F32, sub2)
                    m_state = sb("m_state", [P, 7, 256], F32, sub2)
                    srow = sb("srow", [M_HEADS, 8, 8], F32, sub2)
            with ExitStack() as sub:
                mx_hi, mx_lo = (sb(n, [P, KT, S], F32R, sub) for n in ("mx_hi", "mx_lo"))
        with ExitStack() as room:
            ff_hi, ff_lo = (sb(n, [P, 16, S], F32R, room) for n in ("ff_hi", "ff_lo"))
            relu_f, sq_f = (sb(n, [P, 2, S], F32, room) for n in ("relu_f", "sq_f"))
        hg_state = yT[:, 0:4, :].rearrange("p a (b c) -> p (a b) c", c=P)
        z_k = yT[:, 4:5, :]
        z_qm = yT[:, 6:8, :]

        G = ctx.enter_context(nc.psum_tensor("G", [P, 4, 512], F32))
        X = ctx.enter_context(nc.psum_tensor("X", [P, 4, 512], F32))

        s_raw = [sem("raw_landed0"), sem("raw_landed1")]
        s_hi, s_lo = sem("w_hi_ready"), sem("w_lo_ready")
        s_inner, s_tile = sem("inner_chunk_used"), sem("tile_summed")
        s_free = {"act": sem("act_freed_tile"), "dve": sem("dve_freed_tile")}
        s_in, s_con, s_con2 = sem("inputs_landed"), sem("masks_landed"), sem("rope_tables_landed")
        s_ada = [sem("ada_landed0"), sem("ada_landed1")]
        s_astep, s_asum, s_mod = sem("ada_product_added"), sem("ada_summed"), sem("mod_ready")
        s_dve, s_act = sem("dve_order"), sem("act_order")
        s_sq, s_sqd, s_std = sem("square_ready"), sem("square_summed"), sem("std_ready")
        s_h, s_n, s_uhi, s_u = sem("h_tile_ready"), sem("normed_tile_ready"), sem("u_hi_ready"), sem("u_ready")
        s_silu, s_ff, s_fhi, s_fr = sem("silu_ready"), sem("hidden_ready"), sem("hidden_hi_ready"), sem("hidden_split")
        d2p, d2a = sem("dve_made_for_pe"), sem("dve_made_for_act")
        a2d, a2p = sem("act_made_for_dve"), sem("act_made_for_pe")
        p2d, p2a = sem("pe_made_for_dve"), sem("pe_made_for_act")
        s_rope1, s_res, s_out = sem("first_rope_done"), sem("result_ready"), sem("result_written")

        c1 = lambda k: con1[:, where1[k][0]:where1[k][1]]
        ident, ones, half, freq, sign, q8 = (c1(k) for k in ("ident", "ones", "half", "freq", "sign", "q8"))
        mk = lambda k, lo, hi: masks[:, where3[k][0] + lo:where3[k][0] + hi].bitcast(BF16)
        identb = mk("identb", 0, P)
        rhs_a, rows_b = tmp[:, 0, 0:P], tmp[:, 0, P:2 * P]
        flat = lambda t: t.rearrange("p a s -> p (a s)")
        x_view = flat(yT[:, :, :]).rearrange("p (b n) -> p b n", b=TB)
        Xf = flat(X[:, :, :])
        LBC, HNG, MHN = 104, 112, 120
        NMIX, NFFN, QN, KN = 64, 80, 96, 98
        A1, C1, A2, C2 = 0, 8, 16, 24
        blk = lambda j: slice(j * P, (j + 1) * P)
        PASSES = ((0, 0), (0, 1), (1, 0))

        def rolled(name):
            g = plan[name]
            return g["chunks"] % 2 == 0 and name not in ("z0", "z1", "at_v") and name != order[-1]

        def blocks(eng, name):
            if rolled(name):
                with eng.Fori(0, plan[name]["blocks"]) as b:
                    yield b
            else:
                yield from range(plan[name]["blocks"])

        def slot_of(name, b, s):
            g = plan[name]
            return (s if rolled(name) else b * g["chunks"] + s) % 2

        def half_count(name, b, s, ahead):
            g = plan[name]
            if rolled(name):
                return b * (g["chunks"] // 2) + (g["c0"] + s + ahead) // 2
            return (g["c0"] + b * g["chunks"] + s + ahead) // 2

        def source(name, s, b, k0, k1):
            rows = lambda w: w.rearrange("(t p) n -> p t n", p=P)[:, k0:k1, :]
            one = lambda w, n=512, off=0: [(0, rows(w)[:, :, bass.ds(b * 512 + off, n)])]
            if name in ("hg_q", "hg_f", "hg_v", "hg_g"):
                return one(a["hgrn_w_in"][0], off=D * ("hg_q", "hg_f", "hg_v", "hg_g").index(name))
            if name == "hg_out":
                return one(a["hgrn_w_out"][0])
            if name == "at_out":
                return one(a["attn_w_out"][0])
            if name == "at_v":
                return [(0, rows(a["attn_w_in"][0])[:, :, (b // 2) * 3 * D + 2 * D + (b % 2) * 512:][:, :, 0:512])]
            if name.startswith("at_qk"):
                w, p = rows(a["attn_w_in"][0]), int(name[-1])
                return [(256 * i, w[:, :, bass.ds(b * 3 * D + (i * D + p * 256), 256)]) for i in range(2)]
            if name.startswith("ffn_in"):
                l, base = int(name[-2]), int(name[-1]) * FF1_TILES[0] * P
                w = rows(a["ffn_w_in"][l])
                return [(256 * i, w[:, :, bass.ds(b * 256 + (i * FF1 + base), 256)]) for i in range(2)]
            if name.startswith("ffn_out"):
                return one(a["ffn_w_out"][int(name[-2])])
            if name.startswith("zg"):
                return one(a["w_in_2"][int(name[-1])], off=Z["gate"])
            if name.startswith("z"):
                return one(a["w_in_2"][int(name[-1])], n=512 if b < 4 else 264)
            if name.startswith("br"):
                w = a["w_att_branch_2" if b < 2 else "w_m_branch_2"][int(name[-1])]
                return [(0, rows(w)[:, :, (b % 2) * 512:(b % 2) * 512 + 512])]
            if name.startswith("mo"):
                return one(a["w_out_2"][int(name[-1])])
            if name.startswith("ff_in"):
                return one(a["w_ff1_2"][int(name[-2])], off=int(name[-1]) * 2048)
            return one(a["w_ff2_2"][int(name[-2])])

        def first_row_tile(name):
            if name.startswith("ffn_out"):
                return int(name[-1]) * FF1_TILES[0]
            return int(name[-1]) * 16 if name.startswith("ff_out") else 0

        block = ctx.enter_context(nc.Block())

        @block.sync
        def _(sp):
            def chunk(name, s, b):
                g = plan[name]
                nk, k0 = min(4, g["ktiles"] - 4 * s), first_row_tile(name) + 4 * s
                slot = slot_of(name, b, s)
                if name.startswith(("at_qk", "ffn_in")):
                    for col, src in source(name, s, b, k0, k0 + nk):
                        sp.dma_start(raw[slot][:, 0:nk, col:col + 256], src).then_inc(s_raw[slot], 16)
                else:
                    for i in range(2):
                        (_, src), = source(name, s, b, k0 + i * nk // 2, k0 + (i + 1) * nk // 2)
                        sp.dma_start(raw[slot][:, i * nk // 2:(i + 1) * nk // 2, 0:src.shape[-1]],
                                     src).then_inc(s_raw[slot], 16)

            small = [(con1[:, :], a["con1"]),
                     (mask32[:, :], a["con2"][:, where2["mask32"][0]:where2["mask32"][1]]),
                     (rhs_a[0:96, :], a["ada_b"].rearrange("l (c p) -> (l c) p", p=P)),
                     (rhs_a[96:104, :], a["c"].rearrange("o (c p) -> (o c) p", p=P)),
                     (rhs_a[104:112, :], a["hgrn_lower_bounds"].rearrange("o (c p) -> (o c) p", p=P)),
                     (rhs_a[112:120, :], a["hgrn_norm_g"].rearrange("o (c p) -> (o c) p", p=P)),
                     (rhs_a[120:128, :], a["m_head_norm_2"].rearrange("o (c p) -> (o c) p", p=P)),
                     (rows_b[0:64, :], a["norm_g"].rearrange("l q (c p) -> (l q c) p", p=P)),
                     (rows_b[64:80, :], a["norm_mix_2"].rearrange("l (c p) -> (l c) p", p=P)),
                     (rows_b[80:96, :], a["norm_ffn_2"].rearrange("l (c p) -> (l c) p", p=P))]
            for r0, nm in ((QN, "att_q_norm_2"), (KN, "att_k_norm_2")):
                small += [(rows_b[r0:r0 + 2, 64 * i:64 * i + 64], a[nm]) for i in range(2)]
            small += [(sinks[:, :], a["att_sinks_2"].rearrange("l h -> (l h)").partition_broadcast(P))]
            for dst, src in small:
                sp.dma_start(dst, src).then_inc(s_in, 16)
            with nc.allow_non_contiguous_dma(reason="sixteen gate biases"):
                for l in range(2):
                    for i in range(2):
                        sp.dma_start(gbias[:, 2 * l + i:2 * l + i + 1],
                                     a["m_gate_bias_2"][l:l + 1, 4 * i:4 * i + 4].rearrange("o h -> h o")).then_inc(s_in, 16)
            sp.dma_start(x_view, a["x"][0].rearrange("(b p) n -> p b n", p=P)).then_inc(s_in, 16)
            for name in order:
                g = plan[name]
                if name == "at_v":
                    sp.wait_ge(s_mod, 2 * ADA_BLOCKS)
                    sp.dma_start(masks[:, :], a["masks"]).then_inc(s_con, 16)
                    sp.dma_start(sel4[:, :], a["con2"][:, where2["sel4"][0]:where2["sel4"][1]]).then_inc(s_con, 16)
                    sp.dma_start(flat(selk[:, :, :]), a["con2"][:, where2["selk"][0]:where2["selk"][1]]).then_inc(s_con, 16)
                    sp.dma_start(sinT[:, :].bitcast(I32), a["positions"][0].partition_broadcast(P)).then_inc(s_con, 16)
                if name == "z0":
                    sp.wait_ge(s_rope1, 1)
                    sp.dma_start(cosT[:, :], a["con2"][:, where2["cos2"][0]:where2["cos2"][1]]).then_inc(s_con2, 16)
                    sp.dma_start(sinT[:, :], a["con2"][:, where2["sin2"][0]:where2["sin2"][1]]).then_inc(s_con2, 16)
                if name == order[0]:
                    for s in range(2):
                        chunk(name, s, 0)
                    with sp.Fori(1, g["blocks"]) as b:
                        for s in range(2):
                            sp.wait_ge(s_lo, 2 * b + (s - 1))
                            chunk(name, s, b)
                    continue
                for b in blocks(sp, name):
                    for s in range(g["chunks"]):
                        sp.wait_ge(s_lo, b * g["chunks"] + (g["c0"] + s - 1))
                        chunk(name, s, b)
            sp.wait_ge(s_res, 8)
            sp.dma_start(out[0].rearrange("(b p) n -> p b n", p=P), x_view).then_inc(s_out, 16)
            sp.wait_ge(s_out, 16)

        @block.gpsimd
        def _(pool):
            for l in range(2):
                w = a["ada_w"][l].rearrange("(s k p) n -> s p k n", p=P, k=4)

                def load(b):
                    for s in range(2):
                        if l or not isinstance(b, int):
                            pool.wait_ge(s_astep, b * 8 + (8 * ADA_BLOCKS * l - 8 + 4 * (s + 1)))
                        pool.dma_start(ada_raw[:, s, :, :], w[s][:, :, bass.ds(b * 512, 512)]).then_inc(s_ada[s], 16)

                if l == 0:
                    load(0)
                with pool.Fori(1 - l, ADA_BLOCKS) as b:
                    load(b)

        NORM_TMP = dict(sq=0, t=2, uf=4, std=6, rstd=7)
        n_eps = 1

        @block.scalar
        def _(act):
            n = Counts(act)
            sc = nc.scalar

            def split(name, b, s):
                g = plan[name]
                if isinstance(b, int) and g["c0"] + b * g["chunks"] + s + 2 >= n_chunks:
                    return
                slot = slot_of(name, b, s)
                act.wait_ge(s_raw[slot], half_count(name, b, s, 2) * 32 + 32)
                if s < g["chunks"] - 1:
                    act.wait_ge(s_inner, b * (g["chunks"] - 1) + (g["inner0"] + s + 1))
                else:
                    act.wait_ge(s_tile, b * 4 + (g["t0"] + 4))
                sc.copy(w_hi[slot][:, :, :], raw[slot][:, :, :]).then_inc(s_hi, 1)

            def linear(name, evict):
                g = plan[name]
                for b in blocks(act, name):
                    for s in range(g["chunks"] - 1):
                        split(name, b, s)
                    evict(g, b)
                    split(name, b, g["chunks"] - 1)

            def evicted(g, b, m, *instructions):
                act.wait_ge(s_tile, b * 4 + (g["t0"] + m + 1))
                for f in instructions[:-1]:
                    f()
                instructions[-1]().then_inc(s_free["act"], 1)

            def nothing(g, b):
                pass

            def norm(ready, src, n_mean=D):
                for k in range(KT):
                    ready(k)
                    if k >= 2:
                        n.take(s_sqd)
                    n.give(sc.activation(tmp[:, k % 2, :], src[:, k, :], ACT.Square), s_sq)
                n.take(s_sqd, 2)
                n.give(sc.activation(tmp[:, 6, :], X[:, 0, :], ACT.Sqrt, bias=EPS, scale=1.0 / n_mean), s_std)

            def to_u(scale, shift=None):
                for k in range(KT):
                    n.take(s_n)
                    if k >= 2:
                        n.take(s_u)
                    kw = dict(scale=scale(k), bias=0.0 if shift is None else shift(k))
                    sc.activation(tmp[:, 4 + k % 2, :], tmp[:, 2 + k % 2, :], ACT.Identity, **kw)
                    n.give(sc.activation(u_hi[:, k, :], tmp[:, 2 + k % 2, :], ACT.Identity, **kw), s_uhi)
                n.take(s_u, 2)

            def split_tiles(src, hi, s_done, ready=None):
                for k in range(KT):
                    if ready:
                        ready(k)
                    n.give(sc.copy(hi[:, k, :], src[:, k, :]), s_done)

            def freed_by_dve(name):
                g = plan[name]
                return lambda k: act.wait_ge(s_free["dve"], g["mine"] + k + 1)

            n.take(d2a)
            n.give(sc.activation(cond[:, :], cols_a[:, 96:104], ACT.Silu), a2d)
            n.give(sc.activation(lbc[:, 1, :], lbc[:, 0, :], ACT.Exp), a2d)
            for s in range(2):
                act.wait_ge(s_raw[s], 32)
                sc.copy(w_hi[s][:, :, :], raw[s][:, :, :]).then_inc(s_hi, 1)
            sc.sem_inc(s_free["act"], 4)

            def first_norm(l, q, ready, src):
                norm(ready, src)
                to_u(lambda k: mix[:, 32 * l + 16 * q + k:32 * l + 16 * q + k + 1],
                     lambda k: mod[:, 48 * l + 24 * q + k:48 * l + 24 * q + k + 1])

            def h_ready(k):
                n.take(s_h)

            def hgrn():
                for h in range(HG_HEADS):
                    sc.activation(tmp[:, 0, :], hg_f[:, h, :], ACT.Sigmoid)
                    n.give(sc.activation(tmp[:, 1, :], hg_f[:, h, :], ACT.Sigmoid, scale=-1.0), a2d)
                    n.take(p2a)
                    n.give(sc.copy(tmp[:, 0, :], X[:, 1, :]), a2p)
                    n.take(p2a)
                    n.give(sc.activation(tmp[:, 1, :], X[:, 0, :], ACT.Square), a2p)
                    n.take(p2a)
                    n.give(sc.activation(tmp[:, 2, :], X[:, 1, :], ACT.Sqrt, bias=EPS, scale=1.0 / P), a2d)
                n.take(d2a)

            def attention(p):
                Pb, PTb = flat(tmp[:, 0:3, :]), flat(tmp[:, 3:6, :])
                for hh in range(2):
                    for i in range(TB):
                        w, w0 = (i + 1) * P, 256 if i else P
                        n.take(d2a)
                        sc.activation(Pb[:, 0:2 * w].rearrange("p (a n) -> p a n", a=2), X[:, 0:2, 0:w], ACT.Exp,
                                      bias=stat[:, 2:3], scale=ATT_SCALE, accum_out=stat[:, 3:4])
                        n.give(sc.activation(Pb[:, 2 * w:2 * w + w0], X[:, 2, 0:w0], ACT.Exp,
                                             bias=stat[:, 2:3], scale=ATT_SCALE, accum_out=stat[:, 4:5]), a2d)
                        n.take(p2a)
                        n.give(sc.copy(PTb[:, 0:2 * w + w0], Xf[:, 0:2 * w + w0]), a2p)
                    n.take(p2a)
                    n.give(sc.copy(yT[:, 2 * p + hh, :], X[:, 3, :]), s_act)

            def window_attention(l):
                n.give(sc.activation(tmp[:, 4, :], z_k[:, 0, :], ACT.Square), a2p)
                n.take(p2a)
                n.give(sc.activation(tmp[:, 4, :], X[:, 0, :], ACT.Sqrt, bias=EPS, scale=1.0 / SW_DIM), a2d)
                n.take(d2a)
                n.give(sc.activation(tmp[:, 4:8, :], z_q[:, :, :], ACT.Square), a2p)
                n.take(p2a)
                n.give(sc.activation(tmp[:, 4:8, :], X[:, :, :], ACT.Sqrt, bias=EPS, scale=1.0 / SW_DIM), a2d)
                n.take(p2a)
                n.give(sc.copy(tmp[:, 0:4, :], X[:, :, :]), a2p)
                Pb, PTb = flat(tmp[:, 4:6, :]), flat(tmp[:, 6:8, :])
                for h in range(SW_HEADS):
                    sink = sinks[:, 8 * l + h:8 * l + h + 1]
                    n.take(d2a)
                    for i in range(TB):
                        sc.activation(Pb[:, 256 * i:256 * i + 256], X[:, i // 2, 256 * (i % 2):256 * (i % 2) + 256], ACT.Exp,
                                      bias=stat[:, 8 + i:9 + i], scale=SW_DIM ** -0.5, accum_out=stat[:, 12 + i:13 + i])
                    n.give(sc.activation(stat[:, 16:20], stat[:, 8:12], ACT.Exp, bias=sink), a2d)
                    n.take(p2a)
                    n.give(sc.copy(PTb[:, 0:7 * P], Xf[:, 0:7 * P]), a2p)
                    if h % 2:
                        n.take(p2a)
                        n.give(sc.copy(yT[:, h // 2, :], X[:, 2, :]), s_act)

            def mlstm(l):
                gi, gf = z_if[:, 0, :], z_if[:, 1, :]
                n.own(s_free["act"])
                n.give(sc.activation(row[:, 0, :], gf, ACT.Abs), s_act)
                n.own(s_act)
                n.give(sc.activation(row[:, 0, :], row[:, 0, :], ACT.Exp, scale=-1.0), s_act)
                n.own(s_act)
                n.give(sc.activation(row[:, 0, :], row[:, 0, :], ACT.Ln, bias=1.0), a2d)
                n.take(d2a)
                sc.activation(row[:, 1, :], row[:, 1, :], ACT.Exp)
                sc.activation(row[:, 0, :], row[:, 0, :], ACT.Exp)
                sc.activation(row[:, 3, :], row[:, 3, :], ACT.Exp, scale=-1.0)
                n.give(sc.activation(srow[:, 6, :], srow[:, 5, :], ACT.Exp), a2p)
                for h in range(M_HEADS):
                    if h % 2 == 0:
                        n.take(p2a)
                        n.give(sc.copy(tmp[:, 4, :], X[:, 0, :]), a2p)
                    n.take(p2a)
                    for j in range(TB):
                        ins = sc.activation(tmp[:, 0, blk(j)], X[:, 1, blk(j)], ACT.Exp,
                                            bias=mcol[:, 4 * j + h:4 * j + h + 1])
                    n.give(ins, a2d)
                    n.take(p2a)
                    n.give(sc.activation(tmp[:, 6, :], X[:, 1, :], ACT.Abs), a2d)
                    n.take(d2a)
                    n.give(sc.activation(tmp[:, 6, :], tmp[:, 5, :], ACT.Square), a2p)
                    n.take(p2a)
                    n.give(sc.activation(tmp[:, 7, :], X[:, 3, :], ACT.Sqrt, bias=EPS, scale=1.0 / P), a2d)
                n.take(d2a)

            first_norm(0, 0, h_ready, hT)

            for name in order:
                l = int(name[-2]) if name.startswith(("ffn", "ff_")) else 0
                if name == "hg_q":
                    linear(name, lambda g, b: [evicted(g, b, m, lambda: sc.activation(hg_q[:, b * 4 + m, :], G[:, m, :], ACT.Silu)) for m in range(4)])
                elif name == "hg_f":
                    linear(name, lambda g, b: [evicted(g, b, m, lambda: sc.copy(hg_f[:, b * 4 + m, :], G[:, m, :])) for m in range(4)])
                elif name == "hg_v":
                    linear(name, lambda g, b: [evicted(g, b, m, lambda: sc.copy(hg_v[:, m, bass.ds(b * 512, 512)], G[:, m, :])) for m in range(4)])
                elif name == "hg_g":
                    linear(name, lambda g, b: [evicted(g, b, m, lambda: sc.activation(hg_g[:, b * 4 + m, :], G[:, m, :], ACT.Silu)) for m in range(4)])
                    n.made(s_free["act"], plan["hg_g"]["mine"] + 8)
                    n.own(s_free["act"])
                    hgrn()
                    split_tiles(hg_g, u_hi, s_uhi)
                elif name == "hg_out":
                    linear(name, nothing)
                    norm(freed_by_dve(name), yT)
                    first_norm(0, 1, h_ready, hT)
                elif name.startswith("ffn_in"):
                    def gates(g, b):
                        for m in range(2):
                            act.wait_ge(s_tile, b * 4 + (g["t0"] + m + 1))
                            act.wait_ge(s_free["dve"], b * 4 + (g["mine"] - 1 + m))
                            sc.activation(silu_g[:, m, :], G[:, m, :], ACT.Silu).then_inc(s_silu, 1)
                        for m in range(2):
                            act.wait_ge(s_free["dve"], b * 4 + (g["mine"] + 3 + m))
                            sc.copy(hid_hi[:, b * 2 + m, :], hid_f[:, m, :]).then_inc(s_fhi, 1)
                    linear(name, gates)
                elif name.startswith("ffn_out"):
                    linear(name, nothing)
                    if name[-1] == "1":
                        norm(freed_by_dve(name), yT)
                        if l == 0:
                            first_norm(1, 0, h_ready, hT)
                        else:
                            norm(h_ready, hT)
                            to_u(lambda k: cols_b[:, NMIX + k:NMIX + k + 1])
                elif name == "at_v":
                    linear(name, lambda g, b: [evicted(g, b, m, lambda: sc.copy(at_v[:, m, b * 512:b * 512 + 512], G[:, m, :])) for m in range(4)])
                    n.take(d2a)
                    n.give(sc.activation(sinT[:, :], tmp[:, 2, :], ACT.Sin), a2d)
                    n.give(sc.activation(tmp[:, 3, :], tmp[:, 2, :], ACT.Abs), s_act)
                    n.own(s_act)
                    n.give(sc.activation(cosT[:, :], tmp[:, 3, :], ACT.Sin, scale=-1.0, bias=float(np.pi / 2)), a2d)
                elif name.startswith("at_qk"):
                    linear(name, nothing)
                    attention(int(name[-1]))
                    if name[-1] == "3":
                        n.own(s_act)
                        split_tiles(yT, u_hi, s_uhi)
                elif name == "at_out":
                    linear(name, nothing)
                    norm(freed_by_dve(name), yT)
                    first_norm(1, 1, h_ready, hT)
                elif name.startswith("zg"):
                    linear(name, lambda g, b: [evicted(g, b, m, lambda: sc.activation(gate[:, b * 4 + m, :], G[:, m, :], ACT.Sigmoid)) for m in range(4)])
                    l = int(name[-1])
                    n.made(s_free["act"], plan[name]["mine"] + 16 - n.given.get(s_free["act"], 0))
                    n.own(s_free["act"])
                    window_attention(l)
                    mlstm(l)
                    n.own(s_act)
                    split_tiles(yT, u_hi, s_uhi)
                elif name.startswith("z"):
                    n.take(d2a)
                    zl = int(name[-1])

                    def z_evict(g, b):
                        if b == 0:
                            for m in range(4):
                                evicted(g, b, m, lambda: sc.copy(z_q[:, m, :], G[:, m, :]))
                        elif b == 1:
                            evicted(g, b, 0, lambda: sc.copy(z_k[:, 0, :], G[:, 0, :]))
                            v = G[:, 1, :].rearrange("p (j v d) -> p j v d", j=TB, v=2)
                            evicted(g, b, 1, lambda: sc.copy(vpad[:, :, :, 0, 0:64], v), lambda: sc.copy(vpad[:, :, :, 1, 64:128], v))
                            for m in (2, 3):
                                evicted(g, b, m, lambda: sc.copy(z_qm[:, m - 2, :], G[:, m, :]))
                        elif b == 2:
                            for m in range(4):
                                evicted(g, b, m, lambda: sc.copy(z_km[:, m, :], G[:, m, 0:256]),
                                        lambda: sc.copy(z_vm[:, m, 0:256], G[:, m, 256:512]))
                        elif b == 3:
                            for m in range(2):
                                evicted(g, b, m, lambda: sc.copy(z_vm[:, 2 * m:2 * m + 2, 256:512],
                                                                 G[:, m, :].rearrange("p (j d) -> p j d", j=2)))
                            for m in (2, 3):
                                evicted(g, b, m, lambda: sc.activation(z_om[:, m - 2, :], G[:, m, :], ACT.Sigmoid))
                        else:
                            for m in range(2):
                                evicted(g, b, m, lambda: sc.activation(z_om[:, 2 + m, :], G[:, m, :], ACT.Sigmoid))
                            for m in (2, 3):
                                evicted(g, b, m, lambda: sc.activation(z_if[:, m - 2, :], G[0:4, m, :], ACT.Identity,
                                                                       bias=gbias[:, 2 * zl + m - 2:2 * zl + m - 1]))
                    linear(name, z_evict)
                elif name.startswith("br"):
                    linear(name, nothing)
                    for k in range(KT):
                        n.take(d2a)
                        n.give(sc.copy(mx_hi[:, k, :], gate[:, k, :]), s_uhi)
                elif name.startswith("mo"):
                    linear(name, nothing)
                    l = int(name[-1])
                    norm(freed_by_dve(name), hT)
                    to_u(lambda k: cols_b[:, NFFN + 8 * l + k:NFFN + 8 * l + k + 1])
                elif name.startswith("ff_in"):
                    gff = n.at(s_ff)

                    def relu2(g, b):
                        def hi(m):
                            act.wait_ge(s_ff, b * 4 + (gff + 2 + m + 1))
                            sc.copy(ff_hi[:, b * 4 + m, :], sq_f[:, m % 2, :]).then_inc(s_fhi, 1)
                        for m in range(4):
                            act.wait_ge(s_ff, b * 4 + (gff + m + 1))
                            evicted(g, b, m, lambda: sc.activation(relu_f[:, m % 2, :], G[:, m, :], ACT.Relu))
                            if m >= 1:
                                hi(m - 1)
                        hi(3)
                    linear(name, relu2)
                    n.skip(s_ff, 16)
                elif name.startswith("ff_out"):
                    linear(name, nothing)
                    if name == "ff_out01":
                        norm(freed_by_dve(name), hT)
                        to_u(lambda k: cols_b[:, NMIX + 8 + k:NMIX + 8 + k + 1])

        @block.vector
        def _(dve):
            n = Counts(dve)
            v = nc.vector
            tt, ts, stt = v.tensor_tensor, v.tensor_scalar, v.scalar_tensor_tensor

            def link(ins):
                n.give(ins, s_dve)
                n.own(s_dve)

            def split(name, b, s):
                g = plan[name]
                if isinstance(b, int) and g["c0"] + b * g["chunks"] + s + 2 >= n_chunks:
                    return
                slot = slot_of(name, b, s)
                dve.wait_ge(s_hi, b * g["chunks"] + (g["c0"] + s + 3))
                tt(w_lo[slot][:, :, :], raw[slot][:, :, :], w_hi[slot][:, :, :].bitcast(F32), ALU.subtract).then_inc(s_lo, 1)

            def linear(name, evict, ada=None):
                g = plan[name]
                for b in blocks(dve, name):
                    for s in range(g["chunks"] - 1):
                        split(name, b, s)
                    if ada is not None:
                        ada_products(b + ada)
                    evict(g, b)
                    if ada is not None:
                        ada_add(b + ada)
                    split(name, b, g["chunks"] - 1)

            def evicted(g, b, m, f):
                dve.wait_ge(s_tile, b * 4 + (g["t0"] + m + 1))
                f().then_inc(s_free["dve"], 1)

            def nothing(g, b):
                pass

            def ada_products(i):
                for s in range(2):
                    dve.wait_ge(s_ada[s], i * 16 + 16)
                    for k in range(4):
                        c = cond[:, 4 * s + k:4 * s + k + 1]
                        if s == k == 0:
                            ins = ts(acc[:, :], ada_raw[:, 0, 0, :], c, None, ALU.mult)
                        else:
                            dve.wait_ge(s_astep, i * 8 + (4 * s + k))
                            ins = stt(acc[:, :], ada_raw[:, s, k, :], c, acc[:, :], ALU.mult, ALU.add)
                        ins.then_inc(s_astep, 1)

            def ada_add(i):
                dve.wait_ge(s_asum, i + 1)
                tt(mod[:, bass.ds(i * 4, 4)], X[:, 3, 0:4], cols_a[:, bass.ds(i * 4, 4)], ALU.add).then_inc(s_mod, 1)

            def norm_tail():
                n.take(s_std)
                link(v.reciprocal(tmp[:, 7, :], tmp[:, 6, :]))

            def to_u(src):
                def lo(k):
                    n.take(s_uhi)
                    n.give(tt(u_lo[:, k, :], tmp[:, 4 + k % 2, :], u_hi[:, k, :].bitcast(F32), ALU.subtract), s_u)
                for k in range(KT):
                    n.give(tt(tmp[:, 2 + k % 2, :], src[:, k, :], tmp[:, 7, :], ALU.mult), s_n)
                    if k >= 1:
                        lo(k - 1)
                lo(KT - 1)

            def split_lo(src, hi, lo, s_done):
                for k in range(KT):
                    n.take(s_done)
                    n.give(tt(lo[:, k, :], src[:, k, :], hi[:, k, :].bitcast(F32), ALU.subtract), s_u)

            def add_to_h(l, q):
                norm_tail()
                n.give(tt(tmp[:, 2, :], yT[:, 0, :], tmp[:, 7, :], ALU.mult), s_dve)
                for k in range(KT):
                    if k + 1 < KT:
                        if k:
                            n.own(s_h)
                        n.give(tt(tmp[:, 2 + (k + 1) % 2, :], yT[:, k + 1, :], tmp[:, 7, :], ALU.mult), s_dve)
                        dve.wait_ge(s_dve, n.given[s_dve] - 1)
                    else:
                        n.own(s_dve)
                    c = mix[:, 32 * l + 16 * q + 8 + k:32 * l + 16 * q + 9 + k]
                    n.give(stt(hT[:, k, :], tmp[:, 2 + k % 2, :], c, hT[:, k, :], ALU.mult, ALU.add), s_h)

            def mixing(l, q):
                m0, c0, g0 = 48 * l + 24 * q, 32 * l + 16 * q, 32 * l + 16 * q
                stt(mix[:, c0:c0 + 8], mod[:, m0 + 8:m0 + 16], 1.0, cols_b[:, g0:g0 + 8], ALU.add, ALU.mult)
                return stt(mix[:, c0 + 8:c0 + 16], mod[:, m0 + 16:m0 + 24], 1.0, cols_b[:, g0 + 8:g0 + 16], ALU.add, ALU.mult)

            v.sem_inc(s_free["dve"], 4)
            v.sem_inc(s_ff, 2)
            v.sem_inc(s_fr, 2)
            n.take(p2d)
            v.tensor_copy(cols_a[:, :], X[:, 0, 0:P])
            link(v.tensor_copy(cols_b[:, 0:100], X[:, 1, 0:100]))
            n.give(tt(lbc[:, 0, :], cols_a[:, LBC:LBC + 8], cols_a[:, LBC:LBC + 8], ALU.subtract), d2a)
            for k in range(KT):
                n.take(p2d)
                n.give(v.tensor_copy(hT[:, k, :], (G if k < 4 else X)[:, k % 4, :]), s_h)
            n.take(a2d, 2)
            link(v.reciprocal(lbc[:, 2, :], lbc[:, 1, :]))
            link(tt(lbc[:, 1, :], lbc[:, 1, :], lbc[:, 2, :], ALU.mult))
            link(tt(lbc[:, 0, :], lbc[:, 1, :], lbc[:, 1, :], ALU.subtract))
            link(ts(lbc[:, 1, :], lbc[:, 0, :], -1.0, 1.0, ALU.mult, ALU.add))
            for s in range(2):
                dve.wait_ge(s_hi, s + 1)
                tt(w_lo[s][:, :, :], raw[s][:, :, :], w_hi[s][:, :, :].bitcast(F32), ALU.subtract).then_inc(s_lo, 1)
            for i in range(ADA_FIRST):
                ada_products(i)
                ada_add(i)
            dve.wait_ge(s_mod, ADA_FIRST)
            link(stt(mix[:, 0:8], mod[:, 8:16], 1.0, cols_b[:, 0:8], ALU.add, ALU.mult))
            norm_tail()
            to_u(hT)

            def hgrn():
                F, K, F1, Dc, Di, Ke, At = (tmp[:, i, :] for i in (2, 1, 3, 4, 5, 6, 7))
                dve.wait_ge(s_free["act"], plan["hg_g"]["mine"] + 8)
                link(v.memset(F1, 0.0))
                for h in range(HG_HEADS):
                    n.take(a2d)
                    ts(F, tmp[:, 0, :], lbc[:, 1, h:h + 1], lbc[:, 0, h:h + 1], ALU.mult, ALU.add)
                    link(ts(Ke, K, lbc[:, 1, h:h + 1], None, ALU.mult))
                    link(v.tensor_copy(F1[:, ::HG_CHUNK], F[:, ::HG_CHUNK]))
                    link(v.memset(F[:, ::HG_CHUNK], 0.0))
                    link(v.tensor_tensor_scan(Dc, F, F1, 0.0, ALU.mult, ALU.add))
                    v.reciprocal(Di, Dc)
                    link(tt(hg_q[:, h, :], hg_q[:, h, :], Dc, ALU.mult))
                    n.give(tt(hg_f[:, h, :], Ke, Di, ALU.mult), d2p)
                    n.own(d2p)
                    last = Dc[:, HG_CHUNK - 1::HG_CHUNK].unsqueeze(2).broadcast_to([P, 16, HG_CHUNK])
                    n.give(tt(Ke.rearrange("p (n c) -> p n c", c=HG_CHUNK), hg_f[:, h, :].rearrange("p (n c) -> p n c", c=HG_CHUNK),
                              last, ALU.mult), d2p)
                    n.take(p2d)
                    n.give(tt(At.rearrange("p (j c) -> p j c", j=TB), X[:, 0, :].rearrange("p (j c) -> p j c", j=TB),
                              mask32[:, :].unsqueeze(1).broadcast_to([P, TB, P]), ALU.mult), d2p)
                    n.take(p2d)
                    link(v.tensor_copy(hg_state[:, 1, :], X[:, 2, 0:P]))
                    for c in range(1, 15):
                        ins = stt(hg_state[:, c + 1, :], hg_state[:, c, :], Dc[:, 32 * c + 31:32 * c + 32],
                                  X[:, (2, 3, 0, 1)[c % 4], blk(c // 4)], ALU.mult, ALU.add)
                        if c < 14:
                            link(ins)
                    n.give(ins, d2p)
                    n.take(a2d)
                    link(v.reciprocal(Di, F))
                    link(tt(Ke, X[:, 0, :], Di, ALU.mult))
                    n.give(stt(hg_g[:, h, :], Ke, cols_a[:, HNG + h:HNG + h + 1], hg_g[:, h, :], ALU.mult, ALU.mult), d2a if h == 7 else s_dve)
                    n.own(d2a if h == 7 else s_dve)
                split_lo(hg_g, u_hi, u_lo, s_uhi)

            def rope_tables():
                n.take(s_con, 64)
                two_pi = 2 * np.pi
                c_a = float(np.float32(6.28125))
                c_b = float((np.array([two_pi - c_a], np.float32).view(np.uint32) & np.uint32(0xFFFFF000)).view(np.float32)[0])
                c_c = float(np.float32(two_pi - c_a - c_b))
                magic = float(1.5 * 2 ** 23)
                link(v.tensor_copy(tmp[:, 0, :], sinT[:, :].bitcast(I32)))
                link(ts(tmp[:, 0, :], tmp[:, 0, :], freq, None, ALU.mult))
                link(ts(tmp[:, 1, :], tmp[:, 0, :], float(1 / two_pi), magic, ALU.mult, ALU.add))
                link(ts(tmp[:, 1, :], tmp[:, 1, :], -magic, None, ALU.add))
                for c in (c_a, c_b, c_c):
                    link(stt(tmp[:, 0, :], tmp[:, 1, :], -c, tmp[:, 0, :], ALU.mult, ALU.add))
                n.give(ts(tmp[:, 2, :], tmp[:, 0, :], 3.1415925, -3.1415925, ALU.min, ALU.max), d2a)
                n.take(a2d)
                link(ts(sinT[:, :], sinT[:, :], sign, None, ALU.mult))
                n.take(a2d)

            def rope(x, rot, mask, parts, tiles):
                wide = lambda t: t[0:parts, :].unsqueeze(1).broadcast_to([parts, tiles, S])
                link(v.stream_shuffle(rot, x, mask))
                tt(rot, rot, wide(sinT), ALU.mult)
                link(tt(x, x, wide(cosT), ALU.mult))
                return tt(x, x, rot, ALU.add)

            def attention(p):
                swap = [(i + 16) % 32 for i in range(32)]
                for g in range(GROUPS):
                    link(rope(at_qk[0:32, g, :, :], tmp[0:32, 0:4, :], swap, 32, 4))
                v.sem_inc(d2p, 1)
                n.made(d2p, 1)
                Pb = flat(tmp[:, 0:3, :])
                for hh in range(2):
                    for i in range(TB):
                        w, w0 = (i + 1) * P, 256 if i else P
                        n.take(p2d)
                        v.tensor_reduce(stat[:, 0:1], X[:, 0:2, 0:w], mybir.AxisListType.XY, ALU.max)
                        link(v.tensor_reduce(stat[:, 1:2], X[:, 2, 0:w0], AX, ALU.max))
                        n.give(ts(stat[:, 2:3], stat[:, 0:1], stat[:, 1:2], -ATT_SCALE, ALU.max, ALU.mult), d2a)
                        n.take(a2d)
                        link(tt(stat[:, 5:6], stat[:, 3:4], stat[:, 4:5], ALU.add))
                        link(v.reciprocal(stat[:, 6:7], stat[:, 5:6]))
                        n.give(ts(Pb[:, 0:2 * w + w0], Pb[:, 0:2 * w + w0], stat[:, 6:7], None, ALU.mult), d2p)

            def window_attention(l):
                swap = [i + 8 if i < 8 else i - 8 if i < 16 else i for i in range(32)]
                if l == 0:
                    n.take(s_con2, 32)
                for z, k, gain in ((z_k, 1, KN), (z_q, 4, QN)):
                    n.take(a2d)
                    ra = tmp[:, 4:4 + k, :]
                    link(v.reciprocal(ra, ra))
                    for t in range(k):
                        ins = stt(z[:, t, :], z[:, t, :], cols_b[:, gain + l:gain + l + 1], ra[:, t, :], ALU.mult, ALU.mult)
                    link(ins)
                    n.give(rope(z[:, 0:k, :], ra, swap, P, k), d2a if k == 1 else d2p)
                Pb = flat(tmp[:, 4:6, :]).rearrange("p (i k) -> p i k", i=TB)
                for h in range(SW_HEADS):
                    sink = sinks[:, 8 * l + h:8 * l + h + 1]
                    n.take(p2d)
                    link(v.tensor_reduce(stat[:, 0:4], Xf[:, 0:1024].rearrange("p (i k) -> p i k", i=TB), AX, ALU.max))
                    link(ts(stat[:, 4:8], stat[:, 0:4], SW_DIM ** -0.5, sink, ALU.mult, ALU.max))
                    n.give(ts(stat[:, 8:12], stat[:, 4:8], -1.0, None, ALU.mult), d2a)
                    n.take(a2d)
                    link(tt(stat[:, 20:24], stat[:, 12:16], stat[:, 16:20], ALU.add))
                    link(v.reciprocal(stat[:, 24:28], stat[:, 20:24]))
                    n.give(tt(Pb, Pb, stat[:, 24:28].unsqueeze(2).broadcast_to([P, TB, 256]), ALU.mult), d2p)

            def mlstm(l):
                R = [row[:, i, :] for i in range(4)]
                gi, gf = z_if[:, 0, :], z_if[:, 1, :]
                ch = lambda t: t.rearrange("p (n c) -> p n c", c=M_CHUNK)
                wide = lambda t: t.unsqueeze(2).broadcast_to([M_HEADS, 8, M_CHUNK])
                n.take(a2d)
                link(ts(R[1], gf, 0.0, None, ALU.min))
                v.memset(R[3], 1.0)
                link(tt(gf, R[1], R[0], ALU.subtract))
                link(v.memset(R[3][:, ::M_CHUNK], 0.0))
                link(v.tensor_tensor_scan(R[0], R[3], gf, 0.0, ALU.mult, ALU.add))
                g = srow[:, 0, :]
                v.tensor_copy(g, R[0][:, M_CHUNK - 1::M_CHUNK])
                link(tt(gi, gi, R[0], ALU.subtract))
                link(tt(ch(R[1]), ch(gi), wide(g), ALU.add))
                link(v.tensor_reduce(srow[:, 1, :], ch(R[1]), AX, ALU.max))
                v.memset(srow[:, 3, 0:1], 0.0)
                link(v.tensor_tensor_scan(srow[:, 2, :], g, srow[:, 1, :], 0.0, ALU.add, ALU.max))
                link(v.tensor_copy(srow[:, 3, 1:8], srow[:, 2, 0:7]))
                tt(ch(R[1]), ch(R[1]), wide(srow[:, 2, :]), ALU.subtract)
                tt(srow[:, 4, :], g, srow[:, 3, :], ALU.add)
                v.tensor_copy(R[2], gi)
                link(v.memset(R[3], 0.0))
                tt(srow[:, 5, :], srow[:, 4, :], srow[:, 2, :], ALU.subtract)
                v.memset(R[3][:, ::M_CHUNK], -3.0e38)
                link(tt(R[2][:, ::M_CHUNK], gi[:, ::M_CHUNK], srow[:, 3, :], ALU.max))
                link(v.tensor_tensor_scan(gf, R[3], R[2], 0.0, ALU.add, ALU.max))
                ts(R[2], gf, -1.0, None, ALU.mult)
                link(tt(R[3], R[0], gf, ALU.add))
                n.give(tt(ch(R[0]), wide(srow[:, 3, :]), ch(gf), ALU.subtract), d2a)
                n.take(p2d)
                n.give(v.tensor_copy(mcol[:, :], X[:, 0, 0:64]), d2p)
                n.own(d2p)
                for h in range(M_HEADS):
                    pr, hf = h // 2, h % 2
                    qpad, qs, ke = tmp[:, 1, :], tmp[:, 2, :], tmp[:, 3, :]
                    ts(qpad, z_qm[:, pr, :], q8[:, hf:hf + 1], None, ALU.mult)
                    for j in range(TB):
                        ins = ts(ke[:, blk(j)], z_km[:, j, pr * P:(pr + 1) * P], mcol[:, 16 + 4 * j + h:17 + 4 * j + h], None, ALU.mult)
                    n.give(ins, d2p)
                    n.take(p2d)
                    n.take(a2d)
                    n.give(tt(tmp[:, 0, :], tmp[:, 0, :], X[:, 2, :], ALU.mult), d2p)
                    n.take(p2d)
                    n.give(tt(qs, qpad, X[:, 3, :], ALU.mult), d2p)
                    n.take(p2d)
                    link(v.tensor_copy(m_state[:, 0, :], X[:, 0, 0:256]))
                    for c in range(1, 7):
                        ins = stt(m_state[:, c, :], m_state[:, c - 1, :], mcol[:, 32 + 8 * h + c:33 + 8 * h + c],
                                  X[:, 2 * (c % 2) + c // 4, 256 * (c // 2 % 2):256 * (c // 2 % 2) + 256], ALU.mult, ALU.add)
                        if c < 6:
                            link(ins)
                    n.give(ins, d2p)
                    n.take(a2d)
                    link(tt(tmp[:, 6, :], tmp[:, 6, :], X[:, 2, :], ALU.max))
                    link(v.reciprocal(tmp[:, 7, :], tmp[:, 6, :]))
                    n.give(tt(tmp[:, 5, :], X[:, 0, :], tmp[:, 7, :], ALU.mult), d2a)
                    n.take(a2d)
                    link(v.reciprocal(tmp[:, 6, :], tmp[:, 7, :]))
                    link(stt(tmp[:, 5, :], tmp[:, 5, :], cols_a[:, MHN + 4 * l + h:MHN + 4 * l + h + 1], tmp[:, 6, :], ALU.mult, ALU.mult))
                    n.give(tt(yT[:, 4 + h, :], tmp[:, 5, :], z_om[:, h, :], ALU.mult), d2a if h == 3 else s_dve)
                    n.own(d2a if h == 3 else s_dve)
                split_lo(yT, u_hi, u_lo, s_uhi)

            def copy_out(g, b):
                for m in range(4):
                    evicted(g, b, m, lambda: v.tensor_copy(yT[:, b * 4 + m, :], G[:, m, :]))

            def add_out(dst):
                def f(g, b):
                    for m in range(4):
                        evicted(g, b, m, lambda: tt(dst[:, b * 4 + m, :], dst[:, b * 4 + m, :], G[:, m, :], ALU.add))
                return f

            for name in order:
                if name in ("hg_q", "hg_f", "hg_v", "hg_g"):
                    linear(name, nothing, ada=ADA_FIRST + 2 * ("hg_q", "hg_f", "hg_v", "hg_g").index(name))
                    if name == "hg_g":
                        hgrn()
                elif name == "hg_out":
                    linear(name, copy_out)
                    mixing(0, 0)
                    link(mixing(0, 1))
                    add_to_h(0, 0)
                    norm_tail()
                    to_u(hT)
                elif name.startswith("ffn_in"):
                    l, hf = int(name[-2]), int(name[-1])
                    fr, fhi, silu = n.at("fr"), n.at("fhi"), n.at("silu")

                    def product(g, b):
                        for m in range(2):
                            dve.wait_ge(s_silu, b * 2 + (silu + m + 1))
                            v.sem_inc(s_free["dve"], 1)
                        for m in range(2):
                            dve.wait_ge(s_fr, b * 2 + (fr + 2))
                            evicted(g, b, 2 + m, lambda: tt(hid_f[:, m, :], silu_g[:, m, :], G[:, 2 + m, :], ALU.mult))
                        for m in range(2):
                            dve.wait_ge(s_fhi, b * 2 + (fhi + m + 1))
                            dve.wait_ge(s_free["dve"], b * 4 + (g["mine"] + 3 + m))
                            tt(hid_lo[:, b * 2 + m, :], hid_f[:, m, :], hid_hi[:, b * 2 + m, :].bitcast(F32), ALU.subtract).then_inc(s_fr, 1)
                    linear(name, product, ada=(ADA_FIRST + 8 + 6 * hf) if l == 0 else None)
                    for q in ("fr", "fhi", "silu"):
                        n.skip(q, 2 * plan[name]["blocks"])
                elif name.startswith("ffn_out"):
                    l, hf = int(name[-2]), int(name[-1])
                    if hf == 0:
                        linear(name, copy_out)
                    else:
                        linear(name, add_out(yT))
                        if l == 0:
                            dve.wait_ge(s_mod, 24)
                            mixing(1, 0)
                            link(mixing(1, 1))
                        add_to_h(l, 1)
                        norm_tail()
                        to_u(hT)
                elif name == "at_v":
                    linear(name, nothing)
                    rope_tables()
                elif name.startswith("at_qk"):
                    def qk(g, b):
                        for m in range(4):
                            evicted(g, b, m, lambda: v.tensor_copy(at_qk[:, b, m, :], G[:, m, :]))
                    linear(name, qk)
                    dve.wait_ge(s_free["dve"], plan[name]["mine"] + 12)
                    attention(int(name[-1]))
                    if name[-1] == "3":
                        v.sem_inc(s_rope1, 1)
                        split_lo(yT, u_hi, u_lo, s_uhi)
                elif name == "at_out":
                    linear(name, copy_out)
                    add_to_h(1, 0)
                    norm_tail()
                    to_u(hT)
                elif name.startswith("zg"):
                    linear(name, nothing)
                    window_attention(int(name[-1]))
                    mlstm(int(name[-1]))
                elif name.startswith("z"):
                    n.give(v.memset(vpad[:, :, :, :, :].rearrange("p a b c d -> p (a b c d)"), 0.0), d2a)
                    linear(name, nothing)
                elif name.startswith("br"):
                    def branch(g, b):
                        for m in range(4):
                            t = b * 4 + m
                            evicted(g, b, m, lambda: tt(gate[:, t, :], gate[:, t, :], G[:, m, :], ALU.mult))
                    linear(name, branch)
                    dve.wait_ge(s_free["dve"], plan[name]["mine"] + 16)
                    for k in range(KT):
                        n.give(tt(gate[:, k, :], gate[:, k, :], gate[:, 8 + k, :], ALU.add), d2a)
                    for k in range(KT):
                        n.take(s_uhi)
                        n.give(tt(mx_lo[:, k, :], gate[:, k, :], mx_hi[:, k, :].bitcast(F32), ALU.subtract), s_u)
                elif name.startswith("mo"):
                    linear(name, add_out(hT))
                    norm_tail()
                    to_u(hT)
                elif name.startswith("ff_in"):
                    fr, fhi = n.at("fr"), n.at("fhi")
                    gff = n.at("ff")

                    def square(g, b):
                        def lo(m):
                            dve.wait_ge(s_fhi, b * 4 + (fhi + m + 1))
                            tt(ff_lo[:, b * 4 + m, :], sq_f[:, m % 2, :], ff_hi[:, b * 4 + m, :].bitcast(F32), ALU.subtract).then_inc(s_fr, 1)
                        for m in range(4):
                            dve.wait_ge(s_free["act"], b * 4 + (g["mine"] + m + 1))
                            dve.wait_ge(s_fr, b * 4 + (fr + 2 + m - 1))
                            tt(sq_f[:, m % 2, :], relu_f[:, m % 2, :], relu_f[:, m % 2, :], ALU.mult).then_inc(s_ff, 1)
                            if m >= 1:
                                lo(m - 1)
                        lo(3)
                    linear(name, square)
                    n.skip("fr", 16)
                    n.skip("fhi", 16)
                elif name.startswith("ff_out"):
                    linear(name, add_out(hT))
                    if name == "ff_out01":
                        norm_tail()
                        to_u(hT)
            for q in range(8):
                n.take(p2d)
                v.tensor_copy(x_view[:, q // 2, (q % 2) * 512:(q % 2) * 512 + 512], (G if q < 4 else X)[:, q % 4, :]).then_inc(s_res, 1)

        @block.tensor
        def _(pe):
            n = Counts(pe)
            mm, tr = nc.tensor.matmul, nc.tensor.transpose

            def linear(name, x_hi, x_lo, tiles=None, ada=None, x0=lambda b: 0):
                g = plan[name]
                other = "dve" if g["evictor"] == "act" else "act"
                pe.wait_ge(s_free[other], g["other"])
                for b in blocks(pe, name):
                    for s in range(g["chunks"]):
                        slot = slot_of(name, b, s)
                        pe.wait_ge(s_lo, b * g["chunks"] + (g["c0"] + s + 1))
                        nk = min(4, g["ktiles"] - 4 * s)
                        w, xs = (w_hi[slot], w_lo[slot]), (x_hi, x_lo)
                        for m in range(4):
                            if s == 0:
                                pe.wait_ge(s_free[g["evictor"]], b * 4 + (g["mine"] + m - 3))
                            spec = tiles(b, m) if tiles else None
                            last_k = g["ktiles"] - 1
                            for part in (spec if isinstance(spec, list) else [None]):
                                for k in range(nk):
                                    kk = 4 * s + k
                                    for iw, ix in PASSES:
                                        first = kk == 0 and (iw, ix) == (0, 0) and (part is None or part is spec[0])
                                        last = kk == last_k and (iw, ix) == (1, 0)
                                        if part is None:
                                            c0, c1_ = spec or (m * P, m * P + P)
                                            ins = mm(G[0:c1_ - c0, m, :], w[iw][:, k, c0:c1_], xs[ix][:, x0(b) + kk, :],
                                                     start=first, stop=last, skip_group_check=True)
                                        else:
                                            tok, (c0, c1_), (o0, o1) = part
                                            ins = mm(G[:, m, o0:o1], xs[ix][:, kk, blk(tok)], w[iw][:, k, c0:c1_],
                                                     start=first, stop=last, skip_group_check=True)
                            if s == g["chunks"] - 1:
                                ins.then_inc(s_tile, 1)
                            elif m == 3:
                                ins.then_inc(s_inner, 1)
                    if ada is not None:
                        ada_sum(b + ada)

            def ada_sum(i):
                pe.wait_ge(s_astep, i * 8 + 8)
                if not isinstance(i, int) or i > 0:
                    pe.wait_ge(s_mod, i)
                for q in range(4):
                    ins = mm(X[:, 3, q:q + 1], acc[:, blk(q)], ones[:, 0:1], start=True, stop=True, skip_group_check=True)
                ins.then_inc(s_asum, 1)

            def norm():
                for k in range(KT):
                    n.take(s_sq)
                    n.give(mm(X[:, 0, :], ones, tmp[:, k % 2, :], start=k == 0, stop=k == KT - 1), s_sqd)

            def transposes(out_bank, src, count, sem_, dst0=0):
                for j in range(count):
                    ins = tr(out_bank[:, blk(dst0 + j)], src(j), ident)
                if sem_ is not None:
                    n.give(ins, sem_)
                return ins

            n.take(s_in, 16 * 20)
            tr(X[:, 0, 0:P], rhs_a, ident)
            n.give(tr(X[:, 1, 0:100], rows_b[0:100, :], ident[0:100, 0:100]), p2d)
            for k in range(KT):
                if k == 4:
                    n.take(s_h, 1)
                transposes((G if k < 4 else X)[:, k % 4, :], lambda j: x_view[:, j, blk(k)], TB, p2d)
            for i in range(ADA_FIRST):
                if i == 0:
                    n.take(s_h, 7)
                ada_sum(i)

            norm()

            def hgrn():
                kT = tmp[:, 0, :]
                for h in range(HG_HEADS):
                    n.take(d2p)
                    for j in range(TB):
                        ins = mm(X[:, 0, blk(j)], hg_f[:, h, blk(j)], hg_q[:, h, blk(j)], start=True, stop=True, skip_group_check=True)
                    n.give(ins, p2d)
                    n.take(d2p)
                    transposes(X[:, 1, :], lambda j: tmp[:, 6, blk(j)], TB, p2a)
                    n.take(a2p)
                    n.take(d2p)
                    for c in range(15):
                        r = slice(32 * (c % 4), 32 * (c % 4) + 32)
                        ins = mm(X[:, (2, 3, 0, 1)[c % 4], blk(c // 4)], kT[r, blk(c // 4)], hg_v[r, c // 4, blk(h)],
                                 start=True, stop=True, skip_group_check=True)
                    n.give(ins, p2d)
                    n.take(d2p)
                    for j in range(TB):
                        mm(X[:, 0, blk(j)], hg_v[:, j, blk(h)], tmp[:, 7, blk(j)], start=j == 0, stop=False, skip_group_check=True)
                    for c in range(1, 16):
                        ins = mm(X[:, 0, 32 * c:32 * c + 32], hg_state[:, c, :], hg_q[:, h, 32 * c:32 * c + 32],
                                 start=False, stop=c == 15, skip_group_check=True)
                    n.give(ins, p2a)
                    n.take(a2p)
                    n.give(mm(X[:, 1, :], ones, tmp[:, 1, :], start=True, stop=True), p2a)

            def attention(p):
                Pb, PTb = flat(tmp[:, 0:3, :]), flat(tmp[:, 3:6, :])
                n.take(d2p)
                for hh in range(2):
                    h = 2 * p + hh
                    q = [at_qk[:, g, hh, :] for g in range(GROUPS)]
                    k = [at_qk[:, g, 2 + hh, :] for g in range(GROUPS)]
                    for i in range(TB):
                        w, w0 = (i + 1) * P, 256 if i else P
                        for bank, (g, lo, hi) in enumerate(((1, 512 - w, 512), (2, 1024 - w, 1024), (0, 1280 - w0, 1280))):
                            o = X[:, bank, 0:hi - lo]
                            mm(o, identb, mk("dil", lo, hi), start=True, stop=False)
                            ins = mm(o, q[g][:, blk(i)], k[g][:, (i + 1) * P - (hi - lo):(i + 1) * P], start=False, stop=True)
                        n.give(ins, p2d)
                        n.take(d2p)
                        nb = 2 * (i + 1) + w0 // P
                        transposes(Xf, lambda j: Pb[:, blk(j)], nb, p2a)
                        n.take(a2p)
                        where = [(1, j) for j in range(i + 1)] + [(2, j) for j in range(i + 1)] + [(0, j) for j in range(max(i - 1, 0), i + 1)]
                        for t, (g, j) in enumerate(where):
                            ins = mm(X[:, 3, blk(i)], at_v[:, j, g * D + h * P:g * D + (h + 1) * P], PTb[:, blk(t)],
                                     start=i == 0 and t == 0, stop=t == nb - 1, skip_group_check=True)
                    n.give(ins, p2a)

            def window_attention(l):
                n.take(a2p)
                n.give(mm(X[:, 0, :], half, tmp[:, 4, :], start=True, stop=True), p2a)
                n.take(a2p)
                for t in range(4):
                    ins = mm(X[:, t, :], half, tmp[:, 4 + t, :], start=True, stop=True)
                n.give(ins, p2a)
                n.take(d2p)
                for t in range(4):
                    ins = mm(X[:, t, :], selk[:, t, :], z_k[:, 0, :], start=True, stop=True)
                n.give(ins, p2a)
                n.take(a2p)
                Pb, PTb = flat(tmp[:, 4:6, :]), flat(tmp[:, 6:8, :])
                for h in range(SW_HEADS):
                    t, hf, kv = h // 2, h % 2, h // 4
                    kp = tmp[:, 2 * kv + hf, :]
                    for bank in range(2):
                        mm(X[:, bank, :], identb, mk("sw", 512 * bank, 512 * bank + 512), start=True, stop=False, skip_group_check=True)
                    for i in range(TB):
                        c0 = 256 * (i % 2)
                        lo = (i - 1) * P if i else 0
                        o = X[:, i // 2, c0 + (0 if i else P):c0 + 256]
                        ins = mm(o, z_q[:, t, blk(i)], kp[:, lo:(i + 1) * P], start=False, stop=True, skip_group_check=True)
                    n.give(ins, p2d)
                    n.take(d2p)
                    transposes(Xf, lambda j: Pb[:, blk(j + 1)], 7, p2a)
                    n.take(a2p)
                    for j in range(7):
                        i, cur = (j + 1) // 2, (j + 1) % 2
                        ins = mm(X[:, 2, blk(i)], vpad[:, i if cur else i - 1, kv, hf, :], PTb[:, blk(j)],
                                 start=hf == 0 and j == 0, stop=hf == 1, skip_group_check=True)
                    if hf:
                        n.give(ins, p2a)

            def mlstm(l):
                gi = z_if[:, 0, :]
                n.take(a2p)
                for j in range(TB):
                    mm(X[:, 0, 4 * j:4 * j + 4], gi[:, blk(j)], ident[0:4, 0:4], start=j == 0, stop=True, skip_group_check=True)
                    mm(X[:, 0, 16 + 4 * j:20 + 4 * j], row[:, 1, blk(j)], ident[0:4, 0:4], start=False, stop=True, skip_group_check=True)
                for h in range(M_HEADS):
                    ins = mm(X[:, 0, 32 + 8 * h:40 + 8 * h], sel4[0:4, blk(h)], srow[:, 6, :], start=False, stop=True, skip_group_check=True)
                n.give(ins, p2d)
                n.take(d2p)
                for h in range(M_HEADS):
                    pr = h // 2
                    sel = sel4[0:4, blk(h)]
                    if h % 2 == 0:
                        transposes(X[:, 0, :], lambda j: z_km[:, j, pr * P:(pr + 1) * P], TB, p2a)
                        n.take(a2p)
                    n.take(d2p)
                    mm(X[:, 1, :], identb, mk("ml", 0, 512), start=True, stop=False)
                    n.give(mm(X[:, 1, :], sel, row[:, 2, :], start=False, stop=True), p2a)
                    for j in range(TB):
                        ins = mm(X[:, 2, blk(j)], tmp[:, 4, blk(j)], tmp[:, 1, blk(j)], start=True, stop=True, skip_group_check=True)
                    n.give(ins, p2d)
                    n.give(mm(X[:, 3, :], sel, row[:, 0, :], start=True, stop=True), p2d)
                    n.take(d2p, 2)
                    for c in range(7):
                        r = slice(64 * (c % 2), 64 * (c % 2) + 64)
                        bank, o = 2 * (c % 2) + c // 4, 256 * (c // 2 % 2)
                        mm(X[:, bank, o:o + P], tmp[r, 3, blk(c // 2)], z_vm[r, c // 2, blk(h)], start=True, stop=True, skip_group_check=True)
                        ins = mm(X[:, bank, o + P:o + 256], tmp[r, 3, blk(c // 2)], ones[r, :], start=True, stop=True, skip_group_check=True)
                    n.give(ins, p2d)
                    n.take(d2p)
                    for j in range(TB):
                        mm(X[:, 0, blk(j)], z_vm[:, j, blk(h)], tmp[:, 0, blk(j)], start=j == 0, stop=False, skip_group_check=True)
                    mm(X[:, 1, :], ones, tmp[:, 0, :], start=True, stop=False, skip_group_check=True)
                    for c in range(1, 8):
                        cs = slice(64 * c, 64 * c + 64)
                        for bank in range(2):
                            mm(X[:, bank, cs], m_state[:, c - 1, blk(bank)], tmp[:, 2, cs], start=False, stop=c == 7, skip_group_check=True)
                    n.give(mm(X[:, 2, :], sel, row[:, 3, :], start=True, stop=True), p2a)
                    n.take(a2p)
                    n.give(mm(X[:, 3, :], ones, tmp[:, 6, :], start=True, stop=True), p2a)

            u_ready = lambda: n.take(s_u, KT)
            n.skip(s_fr, 2)
            fr = [0]

            def token_tiles(b, m):
                return [(m, (0, 512), (0, 512))]

            def z_tiles(b, m):
                if b == 1 and m == 1:
                    return [(j, (P, 2 * P), (j * P, (j + 1) * P)) for j in range(TB)]
                if b == 2:
                    return [(m, (0, 512), (0, 512))]
                if b == 3 and m < 2:
                    return [(2 * m + j, (0, 256), (256 * j, 256 * j + 256)) for j in range(2)]
                if b == 4 and m >= 2:
                    return (256 + 4 * (m - 2), 260 + 4 * (m - 2))
                return None

            for name in order:
                if name in ("hg_q", "hg_f", "hg_v", "hg_g"):
                    if name == "hg_q":
                        u_ready()
                    linear(name, u_hi, u_lo, token_tiles if name == "hg_v" else None,
                           ada=ADA_FIRST + 2 * ("hg_q", "hg_f", "hg_v", "hg_g").index(name))
                    if name == "hg_g":
                        hgrn()
                elif name in ("hg_out", "at_out"):
                    u_ready()
                    linear(name, u_hi, u_lo)
                    norm()
                    norm()
                elif name.startswith("ffn_in"):
                    l, hf = int(name[-2]), int(name[-1])
                    if hf == 0:
                        u_ready()
                    linear(name, u_hi, u_lo, ada=(ADA_FIRST + 8 + 6 * hf) if l == 0 else None)
                    n.take(s_fr, FF1_TILES[hf])
                elif name.startswith("ffn_out"):
                    linear(name, hid_hi, hid_lo)
                    if name[-1] == "1":
                        norm()
                        norm()
                elif name == "at_v":
                    u_ready()
                    linear(name, u_hi, u_lo, token_tiles)
                elif name.startswith("at_qk"):
                    linear(name, u_hi, u_lo)
                    attention(int(name[-1]))
                elif name.startswith("zg"):
                    linear(name, u_hi, u_lo)
                    window_attention(int(name[-1]))
                    mlstm(int(name[-1]))
                elif name.startswith("z"):
                    u_ready()
                    linear(name, u_hi, u_lo, z_tiles)
                elif name.startswith("br"):
                    u_ready()
                    linear(name, u_hi, u_lo, x0=lambda b: 0 if b < 2 else 4)
                elif name.startswith("mo"):
                    u_ready()
                    linear(name, mx_hi, mx_lo)
                    norm()
                elif name.startswith("ff_in"):
                    if name[-1] == "0":
                        u_ready()
                    linear(name, u_hi, u_lo)
                    n.take(s_fr, 16)
                elif name.startswith("ff_out"):
                    linear(name, ff_hi, ff_lo)
                    if name == "ff_out01":
                        norm()
            for e in ("act", "dve"):
                pe.wait_ge(s_free[e], sum(4 * plan[x]["blocks"] for x in order if plan[x]["evictor"] == e) + 4)
            for q in range(8):
                bank = (G if q < 4 else X)[:, q % 4, :]
                transposes(bank, lambda j: hT[:, 4 * (q % 2) + j, blk(q // 2)], 4, p2d)

    return plan


NAMES = ["x", "c", "positions", "ada_w", "ada_b", "norm_g", "hgrn_w_in", "hgrn_lower_bounds", "hgrn_norm_g",
         "hgrn_w_out", "attn_w_in", "attn_w_out", "ffn_w_in", "ffn_w_out", "norm_mix_2", "w_in_2", "att_q_norm_2",
         "att_k_norm_2", "att_sinks_2", "m_gate_bias_2", "m_head_norm_2", "w_att_branch_2", "w_m_branch_2",
         "w_out_2", "norm_ffn_2", "w_ff1_2", "w_ff2_2"]


def make(nc, inputs, stop=None):
    first, second, m = constants()
    con1, where1 = pack(first)
    con2, where2 = pack(second)
    masks, where3 = pack(m)
    arrays = {f"in_{k}": np.ascontiguousarray(inputs[k]) for k in NAMES}
    arrays.update(in_con1=con1, in_con2=con2, in_masks=masks)
    aps = {}
    for k, v in arrays.items():
        aps[k[3:]] = nc.dram_tensor(k, v.shape, mybir.dt.from_np(v.dtype), kind="ExternalInput").ap()
    out = nc.dram_tensor("out", (1, S, D), F32, kind="ExternalOutput").ap()
    build(nc, aps, out, where1, where2, where3, stop)
    return arrays


def kernel(**inputs):
    import concourse.bacc as bacc
    from concourse.bass_utils import run_bass_kernel_spmd

    nc = bacc.Bacc("TRN2", target_bir_lowering=False, num_devices=1, dynamic_dma_scratch_size=4096)
    arrays = make(nc, inputs)
    r = run_bass_kernel_spmd(nc, [arrays], core_ids=[0])
    return r.results[0]["out"]
```

```python
import concourse.bass as bass
import numpy as np
from concourse import mybir
from contextlib import ExitStack

F32 = mybir.dt.float32
F32R = mybir.dt.float32r
BF16 = mybir.dt.bfloat16
U16 = mybir.dt.uint16
I32 = mybir.dt.int32
ACT = mybir.ActivationFunctionType
ALU = mybir.AluOpType
AX = mybir.AxisListType.X

P = 128
S = 512
D = 1024
KT = D // P
TB = S // P
NEG = -1.0e30
EPS = 1e-6

HG_HEADS, HG_CHUNK = 8, 32
ATT_HEADS, GROUPS = 8, 3
ATT_SCALE = 128 ** -0.5
ROPE_THETA = 500000.0
FF1 = 2816
FF1_TILES = (12, 10)
SW_HEADS, SW_DIM = 8, 64
M_HEADS, M_CHUNK, M_DK = 4, 64, 64
FF2 = 4096
Z = {"q_a": 0, "k_a": 512, "v_a": 640, "q_m": 768, "k_m": 1024, "v_m": 1280, "o_m": 1792, "if": 2304, "gate": 2312}
ADA_BLOCKS = 12
ADA_FIRST = 4


def constants():
    r = np.arange(P)
    f = {}
    f["ident"] = np.eye(P)
    f["ones"] = np.ones((P, P))
    f["half"] = (r[:, None] // 64 == r[None, :] // 64)
    s, c = r[:, None], r[None, :]
    mask32 = (s // HG_CHUNK == c // HG_CHUNK) & (s <= c)
    inv = ROPE_THETA ** (-np.arange(0, 32, 2, dtype=np.float32) / np.float32(32))
    freq = np.zeros((P, 1), np.float32)
    freq[:32, 0] = np.tile(inv.astype(np.float32), 2)
    f["freq"] = freq
    sign = np.zeros((P, 1))
    sign[:16], sign[16:32] = -1, 1
    f["sign"] = sign
    q8 = np.zeros((P, 2))
    q8[:64, 0] = q8[64:, 1] = M_DK ** -0.5
    f["q8"] = q8
    first = {k: np.asarray(v, np.float32) for k, v in f.items()}

    g = {"mask32": mask32}
    inv2 = ROPE_THETA ** (-np.arange(0, 16, 2, dtype=np.float32) / np.float32(16))
    ang = np.arange(S, dtype=np.float32)[None, :] * inv2.astype(np.float32)[:, None]
    cos2, sin2 = np.ones((P, S)), np.zeros((P, S))
    for h in (0, 64):
        cos2[h:h + 8] = cos2[h + 8:h + 16] = np.cos(ang)
        sin2[h:h + 8], sin2[h + 8:h + 16] = -np.sin(ang), np.sin(ang)
    g["cos2"], g["sin2"] = cos2, sin2
    sel = []
    for kv in range(2):
        for half in range(2):
            m = np.zeros((P, P))
            m[kv * 64 + np.arange(64), half * 64 + np.arange(64)] = 1
            sel.append(m)
    g["selk"] = np.concatenate(sel, 1)
    sel4 = np.zeros((P, M_HEADS, P))
    for h in range(M_HEADS):
        sel4[h, h] = 1
    g["sel4"] = sel4.reshape(P, -1)
    second = {k: np.asarray(v, np.float32) for k, v in g.items()}

    q, k = r[:, None], r[None, :]
    n = lambda ok: np.where(ok, 0.0, NEG)
    off1, off2 = n((q - k) % 4 == 0), n((q - k) % 16 == 0)
    d1, d2 = n(((q - k) % 4 == 0) & (k <= q)), n(((q - k) % 16 == 0) & (k <= q))
    causal = n(k <= q)
    prev0 = n(k >= q)
    m = {"dil": np.concatenate([off1, off1, off1, d1, off2, off2, off2, d2, prev0, causal], 1)}
    prevw = n(k > q)
    full = np.full((P, P), NEG)
    m["sw"] = np.concatenate([full, causal, prevw, causal, prevw, causal, prevw, causal], 1)
    md = n((q // M_CHUNK == k // M_CHUNK) & (q <= k))
    m["ml"] = np.tile(md, (1, TB))
    m["identb"] = np.eye(P)
    masks = {k2: (np.ascontiguousarray(v, np.float32).view(np.uint32) >> 16).astype(np.uint16) for k2, v in m.items()}
    return first, second, masks


def pack(parts):
    at, where = 0, {}
    for k, v in parts.items():
        where[k] = (at, at + v.shape[1])
        at += v.shape[1]
    return np.ascontiguousarray(np.concatenate(list(parts.values()), 1)), where


class Counts:

    def __init__(self, eng):
        self.eng, self.seen, self.given = eng, {}, {}

    def take(self, sem, n=1):
        self.seen[sem] = self.seen.get(sem, 0) + n
        self.eng.wait_ge(sem, self.seen[sem])

    def skip(self, sem, n):
        self.seen[sem] = self.seen.get(sem, 0) + n

    def at(self, sem):
        return self.seen.get(sem, 0)

    def give(self, ins, sem, n=1):
        ins.then_inc(sem, n)
        self.given[sem] = self.given.get(sem, 0) + n

    def made(self, sem, n):
        self.given[sem] = self.given.get(sem, 0) + n

    def own(self, sem):
        self.eng.wait_ge(sem, self.given[sem])


def gemm_plan():
    plan, order = {}, []

    def add(name, blocks, ktiles, evictor):
        chunks = -(-ktiles // 4)
        order.append(name)
        plan[name] = dict(blocks=blocks, chunks=chunks, ktiles=ktiles, evictor=evictor)

    def ffn1(l):
        for half, n in enumerate(FF1_TILES):
            add(f"ffn_in{l}{half}", n // 2, KT, "dve")
            add(f"ffn_out{l}{half}", 2, n, "dve")

    add("hg_q", 2, KT, "act")
    add("hg_f", 2, KT, "act")
    add("hg_v", 2, KT, "act")
    add("hg_g", 2, KT, "act")
    add("hg_out", 2, KT, "dve")
    ffn1(0)
    add("at_v", 6, KT, "act")
    for p in range(4):
        add(f"at_qk{p}", 3, KT, "dve")
    add("at_out", 2, KT, "dve")
    ffn1(1)
    for l in range(2):
        add(f"z{l}", 5, KT, "act")
        add(f"zg{l}", 4, KT, "act")
        add(f"br{l}", 4, 4, "dve")
        add(f"mo{l}", 2, KT, "dve")
        for half in range(2):
            add(f"ff_in{l}{half}", 4, KT, "act")
            add(f"ff_out{l}{half}", 2, 16, "dve")
    c = t = inner = 0
    freed = {"act": 4, "dve": 4}
    for name in order:
        g = plan[name]
        g.update(c0=c, t0=t, inner0=inner, mine=freed[g["evictor"]], other=freed["dve" if g["evictor"] == "act" else "act"])
        c += g["blocks"] * g["chunks"]
        inner += g["blocks"] * (g["chunks"] - 1)
        t += 4 * g["blocks"]
        freed[g["evictor"]] += 4 * g["blocks"]
    return plan, order, c


def build(nc, a, out, where1, where2, where3, stop=None, probe=None):
    plan, order, n_chunks = gemm_plan()
    if stop is not None:
        order = order[:order.index(stop) + 1]
        n_chunks = plan[stop]["c0"] + plan[stop]["blocks"] * plan[stop]["chunks"]
    ctx = ExitStack()

    def sb(name, shape, dt=F32, stack=None):
        return (stack or ctx).enter_context(nc.sbuf_tensor(name, shape, dt))

    def sem(name):
        return ctx.enter_context(nc.semaphore(name))

    with ctx:
        hT = sb("hT", [P, KT, S])
        yT = sb("yT", [P, KT, S])
        u_hi, u_lo = sb("u_hi", [P, KT, S], F32R), sb("u_lo", [P, KT, S], F32R)
        raw = [sb(f"raw{i}", [P, 4, 512]) for i in range(2)]
        w_hi = [sb(f"w_hi{i}", [P, 4, 512], F32R) for i in range(2)]
        w_lo = [sb(f"w_lo{i}", [P, 4, 512], F32R) for i in range(2)]
        tmp = sb("tmp", [P, 8, S])
        con1 = sb("con1", [P, max(v[1] for v in where1.values())])
        cols_a, cols_b = sb("cols_a", [P, P]), sb("cols_b", [P, P])
        mod, mix, cond, lbc = sb("mod", [P, 96]), sb("mix", [P, 64]), sb("cond", [P, KT]), sb("lbc", [P, 4, KT])
        sinks, gbias, stat = sb("sinks", [P, 16]), sb("gbias", [4, 4]), sb("stat", [P, 24])
        rstd = sb("rstd", [P, 2, TB])
        with ExitStack() as room:
            masks = sb("masks", [P, max(v[1] for v in where3.values())], U16, room)
            cosT, sinT = sb("cosT", [P, S], F32, room), sb("sinT", [P, S], F32, room)
            sel4, selk = sb("sel4", [P, 512], F32, room), sb("selk", [P, 4, P], F32, room)
        ada_raw = sb("ada_raw", [P, 2, 4, 512])
        ada_room = ExitStack()
        acc, mask32 = sb("acc", [P, 512], F32, ada_room), sb("mask32_sb", [P, P], F32, ada_room)
        with ExitStack() as room:
            hg_q, hg_f, hg_g = (sb(n, [P, 8, S], F32, room) for n in ("hg_q", "hg_f", "hg_g"))
            hg_v = sb("hg_v", [P, TB, D], F32, room)
            decay = sb("decay", [P, HG_HEADS, S // HG_CHUNK], F32, room)
        with ExitStack() as room:
            hid_hi, hid_lo = (sb(n, [P, FF1_TILES[0], S], F32R, room) for n in ("hid_hi", "hid_lo"))
            silu_g, hid_f = (sb(n, [P, 2, S], F32, room) for n in ("silu_g", "hid_f"))
        ada_room.close()
        with ExitStack() as room:
            at_v = sb("at_v", [P, TB, GROUPS * D], F32, room)
            at_qk = sb("at_qk", [P, GROUPS, 4, S], F32, room)
        with ExitStack() as room:
            gate = sb("gate", [P, 16, S], F32, room)
            with ExitStack() as sub:
                z_km, z_vm = sb("z_km", [P, TB, 256], F32, sub), sb("z_vm", [P, TB, M_HEADS, P + 1], F32, sub)
                z_om, z_if = sb("z_om", [P, 4, S], F32, sub), sb("z_if", [M_HEADS, 2, S], F32, sub)
                with ExitStack() as sub2:
                    z_q = sb("z_q", [P, 4, S], F32, sub2)
                    vpad = sb("vpad", [P, TB, 2, 2, P], F32, sub2)
                with ExitStack() as sub2:
                    row = sb("row", [M_HEADS, 4, S], F32, sub2)
                    m_state = sb("m_state", [P, 7, P + 1], F32, sub2)
                    srow = sb("srow", [M_HEADS, 8, 8], F32, sub2)
            with ExitStack() as sub:
                mx_hi, mx_lo = (sb(n, [P, KT, S], F32R, sub) for n in ("mx_hi", "mx_lo"))
        with ExitStack() as room:
            ff_hi, ff_lo = (sb(n, [P, 16, S], F32R, room) for n in ("ff_hi", "ff_lo"))
            relu_f, sq_f = (sb(n, [P, 2, S], F32, room) for n in ("relu_f", "sq_f"))
        hg_state = yT[:, 0:4, :].rearrange("p a (b c) -> p (a b) c", c=P)
        z_k = yT[:, 4:5, :]
        tmpf = tmp.rearrange("p a s -> p (a s)")
        att_p, att_pt = tmpf[:, 0:1280], [tmpf[:, 1280:2560], tmpf[:, 2560:3840]]
        win_p, win_pt = tmpf[:, 2048:3072], [tmpf[:, 3072:4096], yT[:, 4:6, :].rearrange("p a s -> p (a s)")]
        mcol = mod[:, 0:80]
        z_qm = yT[:, 6:8, :]

        G = ctx.enter_context(nc.psum_tensor("G", [P, 4, 512], F32))
        X = ctx.enter_context(nc.psum_tensor("X", [P, 4, 512], F32))

        s_raw = [sem("raw_landed0"), sem("raw_landed1")]
        s_hi, s_lo = sem("w_hi_ready"), sem("w_lo_ready")
        s_inner, s_tile = sem("inner_chunk_used"), sem("tile_summed")
        s_free = {"act": sem("act_freed_tile"), "dve": sem("dve_freed_tile")}
        s_in, s_con, s_con2 = sem("inputs_landed"), sem("masks_landed"), sem("rope_tables_landed")
        s_ada = [sem("ada_landed0"), sem("ada_landed1")]
        s_astep, s_asum, s_mod = sem("ada_product_added"), sem("ada_summed"), sem("mod_ready")
        s_dve, s_act = sem("dve_order"), sem("act_order")
        s_sq, s_sqd, s_std = sem("square_ready"), sem("square_summed"), sem("std_ready")
        s_diag, s_spread = sem("rstd_on_diagonal"), sem("rstd_spread")
        s_h, s_n, s_uhi, s_u = sem("h_tile_ready"), sem("normed_tile_ready"), sem("u_hi_ready"), sem("u_ready")
        s_silu, s_ff, s_fhi, s_fr = sem("silu_ready"), sem("hidden_ready"), sem("hidden_hi_ready"), sem("hidden_split")
        d2p, d2a = sem("dve_made_for_pe"), sem("dve_made_for_act")
        a2d, a2p = sem("act_made_for_dve"), sem("act_made_for_pe")
        p2d, p2a = sem("pe_made_for_dve"), sem("pe_made_for_act")
        hs = {k: sem("hgrn_" + k) for k in ("scores", "masked", "k_end", "k_end_transposed", "k_end_copied", "updates",
                                            "states", "output", "squares", "output_copied", "sums", "std", "diagonal", "spread", "done")}
        ms = {k: sem("mlstm_" + k) for k in ("columns", "columns_copied", "k_transposed", "k_copied", "exponents", "weights_exp",
                                             "q_alone", "k_end", "scores", "decay", "weights", "q_decayed", "updates", "states",
                                             "output", "squares", "variance", "std", "normed", "transposed", "done")}
        s_rope1, s_res, s_out = sem("first_rope_done"), sem("result_ready"), sem("result_written")

        c1 = lambda k: con1[:, where1[k][0]:where1[k][1]]
        ident, ones, half, freq, sign, q8 = (c1(k) for k in ("ident", "ones", "half", "freq", "sign", "q8"))
        mk = lambda k, lo, hi: masks[:, where3[k][0] + lo:where3[k][0] + hi].bitcast(BF16)
        identb = mk("identb", 0, P)
        rhs_a, rows_b = tmp[:, 0, 0:P], tmp[:, 0, P:2 * P]
        flat = lambda t: t.rearrange("p a s -> p (a s)")
        x_view = flat(yT[:, :, :]).rearrange("p (b n) -> p b n", b=TB)
        Xf = flat(X[:, :, :])
        out_view = X[:, 2:4, :].rearrange("p b (i c) -> p (b i) c", c=256)
        banks, banksf = (X, G), (Xf, flat(G[:, :, :]))
        LBC, HNG, MHN = 104, 112, 120
        NMIX, NFFN, QN, KN = 64, 80, 96, 98
        A1, C1, A2, C2 = 0, 8, 16, 24
        blk = lambda j: slice(j * P, (j + 1) * P)
        PASSES = ((0, 0), (0, 1), (1, 0))

        def att_blocks(t):
            i = t % TB
            return 2 * (i + 1) + (2 if i else 1)

        def rolled(name):
            g = plan[name]
            return g["chunks"] % 2 == 0 and name not in ("hg_out", "z0", "z1", "at_v") and name != order[-1]

        def m_bank(c):
            return (2, c // 2) if c % 2 else (c // 6, c // 2 % 3)

        def decay_heads(name, b):
            first = {"hg_f": -2, "hg_v": 2, "hg_g": 6}[name] + 2 * b
            return range(first, first + 2) if 0 <= first < HG_HEADS else ()

        def with_ada(name, b):
            return name != "hg_out" or b == 1

        def blocks(eng, name, loop=True):
            if rolled(name) and loop:
                with eng.Fori(0, plan[name]["blocks"]) as b:
                    yield b
            else:
                yield from range(plan[name]["blocks"])

        def slot_of(name, b, s):
            g = plan[name]
            return (s if rolled(name) else b * g["chunks"] + s) % 2

        def half_count(name, b, s, ahead):
            g = plan[name]
            if rolled(name):
                return b * (g["chunks"] // 2) + (g["c0"] + s + ahead) // 2
            return (g["c0"] + b * g["chunks"] + s + ahead) // 2

        def source(name, s, b, k0, k1):
            rows = lambda w: w.rearrange("(t p) n -> p t n", p=P)[:, k0:k1, :]
            one = lambda w, n=512, off=0: [(0, rows(w)[:, :, bass.ds(b * 512 + off, n)])]
            if name in ("hg_q", "hg_f", "hg_v", "hg_g"):
                return one(a["hgrn_w_in"][0], off=D * ("hg_q", "hg_f", "hg_v", "hg_g").index(name))
            if name == "hg_out":
                return one(a["hgrn_w_out"][0])
            if name == "at_out":
                return one(a["attn_w_out"][0])
            if name == "at_v":
                return [(0, rows(a["attn_w_in"][0])[:, :, (b // 2) * 3 * D + 2 * D + (b % 2) * 512:][:, :, 0:512])]
            if name.startswith("at_qk"):
                w, p = rows(a["attn_w_in"][0]), int(name[-1])
                return [(256 * i, w[:, :, bass.ds(b * 3 * D + (i * D + p * 256), 256)]) for i in range(2)]
            if name.startswith("ffn_in"):
                l, base = int(name[-2]), int(name[-1]) * FF1_TILES[0] * P
                w = rows(a["ffn_w_in"][l])
                return [(256 * i, w[:, :, bass.ds(b * 256 + (i * FF1 + base), 256)]) for i in range(2)]
            if name.startswith("ffn_out"):
                return one(a["ffn_w_out"][int(name[-2])])
            if name.startswith("zg"):
                return one(a["w_in_2"][int(name[-1])], off=Z["gate"])
            if name.startswith("z"):
                return one(a["w_in_2"][int(name[-1])], n=512 if b < 4 else 264)
            if name.startswith("br"):
                w = a["w_att_branch_2" if b < 2 else "w_m_branch_2"][int(name[-1])]
                return [(0, rows(w)[:, :, (b % 2) * 512:(b % 2) * 512 + 512])]
            if name.startswith("mo"):
                return one(a["w_out_2"][int(name[-1])])
            if name.startswith("ff_in"):
                return one(a["w_ff1_2"][int(name[-2])], off=int(name[-1]) * 2048)
            return one(a["w_ff2_2"][int(name[-2])])

        def first_row_tile(name):
            if name.startswith("ffn_out"):
                return int(name[-1]) * FF1_TILES[0]
            return int(name[-1]) * 16 if name.startswith("ff_out") else 0

        block = ctx.enter_context(nc.Block())

        @block.sync
        def _(sp):
            def chunk(name, s, b):
                g = plan[name]
                nk, k0 = min(4, g["ktiles"] - 4 * s), first_row_tile(name) + 4 * s
                slot = slot_of(name, b, s)
                if name.startswith(("at_qk", "ffn_in")):
                    for col, src in source(name, s, b, k0, k0 + nk):
                        sp.dma_start(raw[slot][:, 0:nk, col:col + 256], src).then_inc(s_raw[slot], 16)
                else:
                    for i in range(2):
                        (_, src), = source(name, s, b, k0 + i * nk // 2, k0 + (i + 1) * nk // 2)
                        sp.dma_start(raw[slot][:, i * nk // 2:(i + 1) * nk // 2, 0:src.shape[-1]],
                                     src).then_inc(s_raw[slot], 16)

            small = [(con1[:, :], a["con1"]),
                     (mask32[:, :], a["con2"][:, where2["mask32"][0]:where2["mask32"][1]]),
                     (rhs_a[0:96, :], a["ada_b"].rearrange("l (c p) -> (l c) p", p=P)),
                     (rhs_a[96:104, :], a["c"].rearrange("o (c p) -> (o c) p", p=P)),
                     (rhs_a[104:112, :], a["hgrn_lower_bounds"].rearrange("o (c p) -> (o c) p", p=P)),
                     (rhs_a[112:120, :], a["hgrn_norm_g"].rearrange("o (c p) -> (o c) p", p=P)),
                     (rhs_a[120:128, :], a["m_head_norm_2"].rearrange("o (c p) -> (o c) p", p=P)),
                     (rows_b[0:64, :], a["norm_g"].rearrange("l q (c p) -> (l q c) p", p=P)),
                     (rows_b[64:80, :], a["norm_mix_2"].rearrange("l (c p) -> (l c) p", p=P)),
                     (rows_b[80:96, :], a["norm_ffn_2"].rearrange("l (c p) -> (l c) p", p=P))]
            for r0, nm in ((QN, "att_q_norm_2"), (KN, "att_k_norm_2")):
                small += [(rows_b[r0:r0 + 2, 64 * i:64 * i + 64], a[nm]) for i in range(2)]
            small += [(sinks[:, :], a["att_sinks_2"].rearrange("l h -> (l h)").partition_broadcast(P))]
            for dst, src in small:
                sp.dma_start(dst, src).then_inc(s_in, 16)
            with nc.allow_non_contiguous_dma(reason="sixteen gate biases"):
                for l in range(2):
                    for i in range(2):
                        sp.dma_start(gbias[:, 2 * l + i:2 * l + i + 1],
                                     a["m_gate_bias_2"][l:l + 1, 4 * i:4 * i + 4].rearrange("o h -> h o")).then_inc(s_in, 16)
            sp.dma_start(x_view, a["x"][0].rearrange("(b p) n -> p b n", p=P)).then_inc(s_in, 16)
            for name in order:
                g = plan[name]
                if name == "at_v":
                    sp.wait_ge(s_mod, 2 * ADA_BLOCKS)
                    sp.dma_start(masks[:, :], a["masks"]).then_inc(s_con, 16)
                    sp.dma_start(sel4[:, :], a["con2"][:, where2["sel4"][0]:where2["sel4"][1]]).then_inc(s_con, 16)
                    sp.dma_start(flat(selk[:, :, :]), a["con2"][:, where2["selk"][0]:where2["selk"][1]]).then_inc(s_con, 16)
                    sp.dma_start(sinT[:, :].bitcast(I32), a["positions"][0].partition_broadcast(P)).then_inc(s_con, 16)
                if name == "z0":
                    sp.wait_ge(s_rope1, 1)
                    sp.dma_start(cosT[:, :], a["con2"][:, where2["cos2"][0]:where2["cos2"][1]]).then_inc(s_con2, 16)
                    sp.dma_start(sinT[:, :], a["con2"][:, where2["sin2"][0]:where2["sin2"][1]]).then_inc(s_con2, 16)
                if name == order[0]:
                    for s in range(2):
                        chunk(name, s, 0)
                    with sp.Fori(1, g["blocks"]) as b:
                        for s in range(2):
                            sp.wait_ge(s_lo, 2 * b + (s - 1))
                            chunk(name, s, b)
                    continue
                for b in blocks(sp, name):
                    for s in range(g["chunks"]):
                        sp.wait_ge(s_lo, b * g["chunks"] + (g["c0"] + s - 1))
                        chunk(name, s, b)
            sp.wait_ge(s_res, 8)
            sp.dma_start(out[0].rearrange("(b p) n -> p b n", p=P), x_view).then_inc(s_out, 16)
            sp.wait_ge(s_out, 16)

        @block.gpsimd
        def _(pool):
            for l in range(2):
                w = a["ada_w"][l].rearrange("(s k p) n -> s p k n", p=P, k=4)

                def load(b):
                    for s in range(2):
                        if l or not isinstance(b, int):
                            pool.wait_ge(s_astep, b * 8 + (8 * ADA_BLOCKS * l - 8 + 4 * (s + 1)))
                        pool.dma_start(ada_raw[:, s, :, :], w[s][:, :, bass.ds(b * 512, 512)]).then_inc(s_ada[s], 16)

                if l == 0:
                    load(0)
                with pool.Fori(1 - l, ADA_BLOCKS) as b:
                    load(b)

        NORM_TMP = dict(sq=0, t=2, uf=4, std=6, rstd=7)
        n_eps = 1

        @block.scalar
        def _(act):
            n = Counts(act)
            sc = nc.scalar

            def split(name, b, s):
                g = plan[name]
                if isinstance(b, int) and g["c0"] + b * g["chunks"] + s + 2 >= n_chunks:
                    return
                slot = slot_of(name, b, s)
                act.wait_ge(s_raw[slot], half_count(name, b, s, 2) * 32 + 32)
                if s < g["chunks"] - 1:
                    act.wait_ge(s_inner, b * (g["chunks"] - 1) + (g["inner0"] + s + 1))
                else:
                    act.wait_ge(s_tile, b * 4 + (g["t0"] + 4))
                sc.copy(w_hi[slot][:, :, :], raw[slot][:, :, :]).then_inc(s_hi, 1)

            def linear(name, evict, after=None):
                g = plan[name]
                for b in blocks(act, name, loop=after is None):
                    for s in range(g["chunks"] - 1):
                        split(name, b, s)
                    evict(g, b)
                    split(name, b, g["chunks"] - 1)
                    if after:
                        after(b)

            def evicted(g, b, m, *instructions):
                act.wait_ge(s_tile, b * 4 + (g["t0"] + m + 1))
                for f in instructions[:-1]:
                    f()
                instructions[-1]().then_inc(s_free["act"], 1)

            def nothing(g, b):
                pass

            def norm(ready, src, n_mean=D):
                for k in range(KT):
                    ready(k)
                    if k >= 2:
                        n.take(s_sqd)
                    n.give(sc.activation(tmp[:, k % 2, :], src[:, k, :], ACT.Square), s_sq)
                n.take(s_sqd, 2)
                n.give(sc.activation(rstd[:, 0, :], X[:, 0, 0:TB], ACT.Sqrt, bias=EPS, scale=1.0 / n_mean), s_std)

            def to_u(scale, shift=None):
                for k in range(KT):
                    n.take(s_n)
                    if k >= 2:
                        n.take(s_u)
                    kw = dict(scale=scale(k), bias=0.0 if shift is None else shift(k))
                    sc.activation(tmp[:, 4 + k % 2, :], tmp[:, 2 + k % 2, :], ACT.Identity, **kw)
                    n.give(sc.activation(u_hi[:, k, :], tmp[:, 2 + k % 2, :], ACT.Identity, **kw), s_uhi)
                n.take(s_u, 2)

            def split_tiles(src, hi, s_done, ready=None):
                for k in range(KT):
                    if ready:
                        ready(k)
                    n.give(sc.copy(hi[:, k, :], src[:, k, :]), s_done)

            def freed_by_dve(name):
                g = plan[name]
                return lambda k: act.wait_ge(s_free["dve"], g["mine"] + k + 1)

            n.take(d2a)
            n.give(sc.activation(cond[:, :], cols_a[:, 96:104], ACT.Silu), a2d)
            n.give(sc.activation(lbc[:, 1, :], lbc[:, 0, :], ACT.Exp), a2d)
            for s in range(2):
                act.wait_ge(s_raw[s], 32)
                sc.copy(w_hi[s][:, :, :], raw[s][:, :, :]).then_inc(s_hi, 1)
            sc.sem_inc(s_free["act"], 4)

            def first_norm(l, q, ready, src):
                norm(ready, src)
                to_u(lambda k: mix[:, 32 * l + 16 * q + k:32 * l + 16 * q + k + 1],
                     lambda k: mod[:, 48 * l + 24 * q + k:48 * l + 24 * q + k + 1])

            def h_ready(k):
                n.take(s_h)

            def hgrn_sigmoids(name, b):
                for h in decay_heads(name, b):
                    if h == 0:
                        act.wait_ge(s_free["act"], plan["hg_f"]["mine"] + 8)
                    else:
                        n.take(d2a)
                    sc.activation(tmp[:, 0, :], hg_f[:, h, :], ACT.Sigmoid)
                    n.give(sc.activation(tmp[:, 1, :], hg_f[:, h, :], ACT.Sigmoid, scale=-1.0), a2d)

            def hgrn():
                for h in range(-1, HG_HEADS + 1):
                    if h >= 1:
                        n.take(hs["sums"])
                        n.give(sc.activation(rstd[:, 0, :], G[:, 3, 0:TB], ACT.Sqrt, bias=EPS, scale=1.0 / P), hs["std"])
                    if h + 1 < HG_HEADS:
                        n.take(hs["k_end_transposed"])
                        n.give(sc.copy(tmp[:, 1, :], G[:, 1, :]), hs["k_end_copied"])
                    if 0 <= h < HG_HEADS:
                        n.take(hs["output"])
                        n.give(sc.activation(tmp[:, 4, :], G[:, 2, :], ACT.Square), hs["squares"])
                        if h >= 2:
                            n.take(hs["done"])
                        n.give(sc.activation(tmp[:, 5 + 2 * (h % 2), :], G[:, 2, :], ACT.Identity,
                                             scale=cols_a[:, HNG + h:HNG + h + 1]), hs["output_copied"])
                n.take(hs["done"], 2)

            def attention(p):
                for t in range(-1, 9):
                    e = t + 1
                    if e < 8:
                        i, B = e % TB, banks[e % 2]
                        w, w0 = (i + 1) * P, 256 if i else P
                        n.take(d2a)
                    if 0 <= t < 8:
                        n.take(p2a)
                    if e < 8:
                        sc.activation(att_p[:, 0:2 * w].rearrange("p (a n) -> p a n", a=2), B[:, 0:2, 0:w], ACT.Exp,
                                      bias=stat[:, 2:3], scale=ATT_SCALE, accum_out=stat[:, 3:4])
                        n.give(sc.activation(att_p[:, 2 * w:2 * w + w0], B[:, 2, 0:w0], ACT.Exp,
                                             bias=stat[:, 2:3], scale=ATT_SCALE, accum_out=stat[:, 4:5]), a2d)
                    if 0 <= t < 8:
                        nb = att_blocks(t) * P
                        n.give(sc.copy(att_pt[t % 2][:, 0:nb], banksf[t % 2][:, 0:nb]), a2p)
                    if t % TB == 0 and t > 0:
                        hh = t // TB - 1
                        n.take(p2a)
                        n.give(sc.copy(yT[:, 2 * p + hh, :], banks[hh][:, 3, :]), a2p)

            def window_attention(l):
                n.give(sc.activation(tmp[:, 4, :], z_k[:, 0, :], ACT.Square), a2p)
                n.take(p2a)
                n.give(sc.activation(tmp[:, 4, :], X[:, 0, :], ACT.Sqrt, bias=EPS, scale=1.0 / SW_DIM), a2d)
                n.take(d2a)
                n.give(sc.activation(tmp[:, 4:8, :], z_q[:, :, :], ACT.Square), a2p)
                n.take(p2a)
                n.give(sc.activation(tmp[:, 4:8, :], X[:, :, :], ACT.Sqrt, bias=EPS, scale=1.0 / SW_DIM), a2d)
                n.take(p2a)
                n.give(sc.copy(tmp[:, 0:4, :], X[:, :, :]), a2p)
                for t in range(-1, 9):
                    h = t + 1
                    if h < SW_HEADS:
                        sink = sinks[:, 8 * l + h:8 * l + h + 1]
                        n.take(d2a)
                    if 0 <= t < SW_HEADS:
                        n.take(p2a)
                    if h < SW_HEADS:
                        for i in range(TB):
                            sc.activation(win_p[:, 256 * i:256 * i + 256], banksf[h % 2][:, 256 * i:256 * i + 256], ACT.Exp,
                                          bias=stat[:, 8 + i:9 + i], scale=SW_DIM ** -0.5, accum_out=stat[:, 12 + i:13 + i])
                        n.give(sc.activation(stat[:, 16:20], stat[:, 8:12], ACT.Exp, bias=sink), a2d)
                    if 0 <= t < SW_HEADS:
                        n.give(sc.copy(win_pt[t % 2][:, 0:7 * P], banksf[t % 2][:, 0:7 * P]), a2p)
                    if t > 0 and t % 2 == 0:
                        n.take(p2a)
                        n.give(sc.copy(yT[:, t // 2 - 1, :], banks[(t // 2 - 1) % 2][:, 2, :]), a2p)

            def mlstm(l):
                gi, gf = z_if[:, 0, :], z_if[:, 1, :]
                n.own(s_free["act"])
                n.give(sc.activation(row[:, 0, :], gf, ACT.Abs), s_act)
                n.own(s_act)
                n.give(sc.activation(row[:, 0, :], row[:, 0, :], ACT.Exp, scale=-1.0), s_act)
                n.own(s_act)
                n.give(sc.activation(row[:, 0, :], row[:, 0, :], ACT.Ln, bias=1.0), a2d)
                n.take(d2a)
                sc.activation(row[:, 1, :], row[:, 1, :], ACT.Exp)
                sc.activation(row[:, 0, :], row[:, 0, :], ACT.Exp)
                sc.activation(row[:, 3, :], row[:, 3, :], ACT.Exp, scale=-1.0)
                n.give(sc.activation(srow[:, 6, :], srow[:, 5, :], ACT.Exp), a2p)
                for pr in range(2):
                    n.take(ms["k_transposed"])
                    n.give(sc.copy(tmp[:, (4, 6)[pr], :], X[:, 2 + pr, :]), ms["k_copied"])
                for h in range(-1, M_HEADS):
                    if h + 1 < M_HEADS:
                        n.take(ms["exponents"])
                        if h == -1:
                            n.take(ms["columns_copied"])
                        for j in range(TB):
                            ins = sc.activation(tmp[:, (0, 5)[(h + 1) % 2], blk(j)], X[:, 0, blk(j)], ACT.Exp,
                                                bias=mcol[:, 4 * j + h + 1:4 * j + h + 2])
                        n.give(ins, ms["weights_exp"])
                    if h >= 0:
                        n.take(ms["output"])
                        for j in range(TB):
                            ins = sc.activation(yT[:, 4 + h, blk(j)], out_view[:, j, 0:P], ACT.Square, accum_out=stat[:, 12 + j:13 + j])
                        n.give(ins, ms["squares"])
                        n.take(ms["variance"])
                        n.give(sc.activation(stat[:, 16:20], stat[:, 12:16], ACT.Sqrt), ms["std"])
                n.take(ms["done"], 4)

            first_norm(0, 0, h_ready, hT)

            for name in order:
                l = int(name[-2]) if name.startswith(("ffn", "ff_")) else 0
                if name == "hg_q":
                    linear(name, lambda g, b: [evicted(g, b, m, lambda: sc.activation(hg_q[:, b * 4 + m, :], G[:, m, :], ACT.Silu)) for m in range(4)])
                elif name == "hg_f":
                    linear(name, lambda g, b: [evicted(g, b, m, lambda: sc.copy(hg_f[:, b * 4 + m, :], G[:, m, :])) for m in range(4)],
                           after=lambda b: hgrn_sigmoids("hg_f", b))
                elif name == "hg_v":
                    linear(name, lambda g, b: [evicted(g, b, m, lambda: sc.copy(hg_v[:, m, bass.ds(b * 512, 512)], G[:, m, :])) for m in range(4)],
                           after=lambda b: hgrn_sigmoids("hg_v", b))
                elif name == "hg_g":
                    linear(name, lambda g, b: [evicted(g, b, m, lambda: sc.activation(hg_g[:, b * 4 + m, :], G[:, m, :], ACT.Silu)) for m in range(4)],
                           after=lambda b: hgrn_sigmoids("hg_g", b))
                    n.made(s_free["act"], plan["hg_g"]["mine"] + 8)
                    n.own(s_free["act"])
                    hgrn()
                    split_tiles(hg_g, u_hi, s_uhi)
                elif name == "hg_out":
                    linear(name, nothing)
                    norm(freed_by_dve(name), yT)
                    first_norm(0, 1, h_ready, hT)
                elif name.startswith("ffn_in"):
                    def gates(g, b):
                        for m in range(2):
                            act.wait_ge(s_tile, b * 4 + (g["t0"] + m + 1))
                            act.wait_ge(s_free["dve"], b * 4 + (g["mine"] - 1 + m))
                            sc.activation(silu_g[:, m, :], G[:, m, :], ACT.Silu).then_inc(s_silu, 1)
                        for m in range(2):
                            act.wait_ge(s_free["dve"], b * 4 + (g["mine"] + 3 + m))
                            sc.copy(hid_hi[:, b * 2 + m, :], hid_f[:, m, :]).then_inc(s_fhi, 1)
                    linear(name, gates)
                elif name.startswith("ffn_out"):
                    linear(name, nothing)
                    if name[-1] == "1":
                        norm(freed_by_dve(name), yT)
                        if l == 0:
                            first_norm(1, 0, h_ready, hT)
                        else:
                            norm(h_ready, hT)
                            to_u(lambda k: cols_b[:, NMIX + k:NMIX + k + 1])
                elif name == "at_v":
                    linear(name, lambda g, b: [evicted(g, b, m, lambda: sc.copy(at_v[:, m, b * 512:b * 512 + 512], G[:, m, :])) for m in range(4)])
                    n.take(d2a)
                    n.give(sc.activation(sinT[:, :], tmp[:, 2, :], ACT.Sin), a2d)
                    n.give(sc.activation(tmp[:, 3, :], tmp[:, 2, :], ACT.Abs), s_act)
                    n.own(s_act)
                    n.give(sc.activation(cosT[:, :], tmp[:, 3, :], ACT.Sin, scale=-1.0, bias=float(np.pi / 2)), a2d)
                elif name.startswith("at_qk"):
                    linear(name, nothing)
                    attention(int(name[-1]))
                    if name[-1] == "3":
                        n.own(a2p)
                        split_tiles(yT, u_hi, s_uhi)
                elif name == "at_out":
                    linear(name, nothing)
                    norm(freed_by_dve(name), yT)
                    first_norm(1, 1, h_ready, hT)
                elif name.startswith("zg"):
                    linear(name, lambda g, b: [evicted(g, b, m, lambda: sc.activation(gate[:, b * 4 + m, :], G[:, m, :], ACT.Sigmoid)) for m in range(4)])
                    l = int(name[-1])
                    n.made(s_free["act"], plan[name]["mine"] + 16 - n.given.get(s_free["act"], 0))
                    n.own(s_free["act"])
                    window_attention(l)
                    mlstm(l)
                    n.own(s_act)
                    split_tiles(yT, u_hi, s_uhi)
                elif name.startswith("z"):
                    n.take(d2a)
                    zl = int(name[-1])

                    def z_evict(g, b):
                        if b == 0:
                            for m in range(4):
                                evicted(g, b, m, lambda: sc.copy(z_q[:, m, :], G[:, m, :]))
                        elif b == 1:
                            evicted(g, b, 0, lambda: sc.copy(z_k[:, 0, :], G[:, 0, :]))
                            v = G[:, 1, :].rearrange("p (j v d) -> p j v d", j=TB, v=2)
                            evicted(g, b, 1, lambda: sc.copy(vpad[:, :, :, 0, 0:64], v), lambda: sc.copy(vpad[:, :, :, 1, 64:128], v))
                            for m in (2, 3):
                                evicted(g, b, m, lambda: sc.copy(z_qm[:, m - 2, :], G[:, m, :]))
                        elif b == 2:
                            for m in range(4):
                                evicted(g, b, m, lambda: sc.copy(z_km[:, m, :], G[:, m, 0:256]),
                                        lambda: sc.copy(z_vm[:, m, 0:2, 0:P], G[:, m, 256:512].rearrange("p (h d) -> p h d", h=2)))
                        elif b == 3:
                            for m in range(2):
                                evicted(g, b, m, *[lambda j=j: sc.copy(z_vm[:, 2 * m + j, 2:4, 0:P],
                                                                       G[:, m, 256 * j:256 * j + 256].rearrange("p (h d) -> p h d", h=2))
                                                   for j in range(2)])
                            for m in (2, 3):
                                evicted(g, b, m, lambda: sc.activation(z_om[:, m - 2, :], G[:, m, :], ACT.Sigmoid))
                        else:
                            for m in range(2):
                                evicted(g, b, m, lambda: sc.activation(z_om[:, 2 + m, :], G[:, m, :], ACT.Sigmoid))
                            for m in (2, 3):
                                evicted(g, b, m, lambda: sc.activation(z_if[:, m - 2, :], G[0:4, m, :], ACT.Identity,
                                                                       bias=gbias[:, 2 * zl + m - 2:2 * zl + m - 1]))
                    linear(name, z_evict)
                elif name.startswith("br"):
                    linear(name, nothing)
                    for k in range(KT):
                        n.take(d2a)
                        n.give(sc.copy(mx_hi[:, k, :], gate[:, k, :]), s_uhi)
                elif name.startswith("mo"):
                    linear(name, nothing)
                    l = int(name[-1])
                    norm(freed_by_dve(name), hT)
                    to_u(lambda k: cols_b[:, NFFN + 8 * l + k:NFFN + 8 * l + k + 1])
                elif name.startswith("ff_in"):
                    gff = n.at(s_ff)

                    def relu2(g, b):
                        def hi(m):
                            act.wait_ge(s_ff, b * 4 + (gff + 2 + m + 1))
                            sc.copy(ff_hi[:, b * 4 + m, :], sq_f[:, m % 2, :]).then_inc(s_fhi, 1)
                        for m in range(4):
                            act.wait_ge(s_ff, b * 4 + (gff + m + 1))
                            evicted(g, b, m, lambda: sc.activation(relu_f[:, m % 2, :], G[:, m, :], ACT.Relu))
                            if m >= 1:
                                hi(m - 1)
                        hi(3)
                    linear(name, relu2)
                    n.skip(s_ff, 16)
                elif name.startswith("ff_out"):
                    linear(name, nothing)
                    if name == "ff_out01":
                        norm(freed_by_dve(name), hT)
                        to_u(lambda k: cols_b[:, NMIX + 8 + k:NMIX + 8 + k + 1])

        @block.vector
        def _(dve):
            n = Counts(dve)
            v = nc.vector
            tt, ts, stt = v.tensor_tensor, v.tensor_scalar, v.scalar_tensor_tensor

            def link(ins):
                n.give(ins, s_dve)
                n.own(s_dve)

            def split(name, b, s):
                g = plan[name]
                if isinstance(b, int) and g["c0"] + b * g["chunks"] + s + 2 >= n_chunks:
                    return
                slot = slot_of(name, b, s)
                dve.wait_ge(s_hi, b * g["chunks"] + (g["c0"] + s + 3))
                tt(w_lo[slot][:, :, :], raw[slot][:, :, :], w_hi[slot][:, :, :].bitcast(F32), ALU.subtract).then_inc(s_lo, 1)

            def linear(name, evict, ada=None, after=None):
                g = plan[name]
                for b in blocks(dve, name, loop=after is None):
                    for s in range(g["chunks"] - 1):
                        split(name, b, s)
                    if ada is not None and with_ada(name, b):
                        ada_products(b + ada)
                    evict(g, b)
                    if ada is not None and with_ada(name, b):
                        ada_add(b + ada)
                    split(name, b, g["chunks"] - 1)
                    if after is not None:
                        after(b)

            def evicted(g, b, m, f):
                dve.wait_ge(s_tile, b * 4 + (g["t0"] + m + 1))
                f().then_inc(s_free["dve"], 1)

            def nothing(g, b):
                pass

            def ada_products(i):
                for s in range(2):
                    dve.wait_ge(s_ada[s], i * 16 + 16)
                    for k in range(4):
                        c = cond[:, 4 * s + k:4 * s + k + 1]
                        if s == k == 0:
                            ins = ts(acc[:, :], ada_raw[:, 0, 0, :], c, None, ALU.mult)
                        else:
                            dve.wait_ge(s_astep, i * 8 + (4 * s + k))
                            ins = stt(acc[:, :], ada_raw[:, s, k, :], c, acc[:, :], ALU.mult, ALU.add)
                        ins.then_inc(s_astep, 1)

            def ada_add(i):
                dve.wait_ge(s_asum, i + 1)
                tt(mod[:, bass.ds(i * 4, 4)], X[:, 3, 0:4], cols_a[:, bass.ds(i * 4, 4)], ALU.add).then_inc(s_mod, 1)

            def norm_tail():
                n.take(s_std)
                link(v.reciprocal(rstd[:, 1, :], rstd[:, 0, :]))
                n.give(tt(tmp[:, 7, :].rearrange("p (j c) -> p j c", j=TB), ident.unsqueeze(1).broadcast_to([P, TB, P]),
                          rstd[:, 1, :].unsqueeze(2).broadcast_to([P, TB, P]), ALU.mult), s_diag)
                n.take(s_spread)

            def to_u(src):
                def lo(k):
                    n.take(s_uhi)
                    n.give(tt(u_lo[:, k, :], tmp[:, 4 + k % 2, :], u_hi[:, k, :].bitcast(F32), ALU.subtract), s_u)
                for k in range(KT):
                    n.give(tt(tmp[:, 2 + k % 2, :], src[:, k, :], X[:, 1, :], ALU.mult), s_n)
                    if k >= 1:
                        lo(k - 1)
                lo(KT - 1)

            def split_lo(src, hi, lo, s_done):
                for k in range(KT):
                    n.take(s_done)
                    n.give(tt(lo[:, k, :], src[:, k, :], hi[:, k, :].bitcast(F32), ALU.subtract), s_u)

            def add_to_h(l, q):
                norm_tail()
                n.give(tt(tmp[:, 2, :], yT[:, 0, :], X[:, 1, :], ALU.mult), s_dve)
                for k in range(KT):
                    if k + 1 < KT:
                        if k:
                            n.own(s_h)
                        n.give(tt(tmp[:, 2 + (k + 1) % 2, :], yT[:, k + 1, :], X[:, 1, :], ALU.mult), s_dve)
                        dve.wait_ge(s_dve, n.given[s_dve] - 1)
                    else:
                        n.own(s_dve)
                    c = mix[:, 32 * l + 16 * q + 8 + k:32 * l + 16 * q + 9 + k]
                    n.give(stt(hT[:, k, :], tmp[:, 2 + k % 2, :], c, hT[:, k, :], ALU.mult, ALU.add), s_h)

            def mixing(l, q):
                m0, c0, g0 = 48 * l + 24 * q, 32 * l + 16 * q, 32 * l + 16 * q
                stt(mix[:, c0:c0 + 8], mod[:, m0 + 8:m0 + 16], 1.0, cols_b[:, g0:g0 + 8], ALU.add, ALU.mult)
                return stt(mix[:, c0 + 8:c0 + 16], mod[:, m0 + 16:m0 + 24], 1.0, cols_b[:, g0 + 8:g0 + 16], ALU.add, ALU.mult)

            v.sem_inc(s_free["dve"], 4)
            v.sem_inc(s_ff, 2)
            v.sem_inc(s_fr, 2)
            n.take(p2d)
            v.tensor_copy(cols_a[:, :], X[:, 0, 0:P])
            link(v.tensor_copy(cols_b[:, 0:100], X[:, 1, 0:100]))
            n.give(tt(lbc[:, 0, :], cols_a[:, LBC:LBC + 8], cols_a[:, LBC:LBC + 8], ALU.subtract), d2a)
            for k in range(KT):
                n.take(p2d)
                n.give(v.tensor_copy(hT[:, k, :], (G if k < 4 else X)[:, k % 4, :]), s_h)
            n.take(a2d, 2)
            link(v.reciprocal(lbc[:, 2, :], lbc[:, 1, :]))
            link(tt(lbc[:, 1, :], lbc[:, 1, :], lbc[:, 2, :], ALU.mult))
            link(tt(lbc[:, 0, :], lbc[:, 1, :], lbc[:, 1, :], ALU.subtract))
            link(ts(lbc[:, 1, :], lbc[:, 0, :], -1.0, 1.0, ALU.mult, ALU.add))
            for s in range(2):
                dve.wait_ge(s_hi, s + 1)
                tt(w_lo[s][:, :, :], raw[s][:, :, :], w_hi[s][:, :, :].bitcast(F32), ALU.subtract).then_inc(s_lo, 1)
            norm_tail()
            for i in range(ADA_FIRST):
                ada_products(i)
                ada_add(i)
            dve.wait_ge(s_mod, ADA_FIRST)
            link(stt(mix[:, 0:8], mod[:, 8:16], 1.0, cols_b[:, 0:8], ALU.add, ALU.mult))
            to_u(hT)

            def hgrn_decays(name, b):
                F, K, F1, Dc, Di = (tmp[:, i, :] for i in (2, 1, 3, 4, 5))
                for h in decay_heads(name, b):
                    if h == 0:
                        link(v.memset(F1, 0.0))
                    n.take(a2d)
                    ts(F, tmp[:, 0, :], lbc[:, 1, h:h + 1], lbc[:, 0, h:h + 1], ALU.mult, ALU.add)
                    link(ts(K, K, lbc[:, 1, h:h + 1], None, ALU.mult))
                    link(v.tensor_copy(F1[:, ::HG_CHUNK], F[:, ::HG_CHUNK]))
                    link(v.memset(F[:, ::HG_CHUNK], 0.0))
                    link(v.tensor_tensor_scan(Dc, F, F1, 0.0, ALU.mult, ALU.add))
                    v.reciprocal(Di, Dc)
                    v.tensor_copy(decay[:, h, :], Dc[:, HG_CHUNK - 1::HG_CHUNK])
                    link(tt(hg_q[:, h, :], hg_q[:, h, :], Dc, ALU.mult))
                    link(tt(hg_f[:, h, :], K, Di, ALU.mult))
                    if h < HG_HEADS - 1:
                        v.sem_inc(d2a, 1)
                        n.made(d2a, 1)

            def hgrn():
                dve.wait_ge(s_free["act"], plan["hg_g"]["mine"] + 8)
                chunks = lambda t: t.rearrange("p (n c) -> p n c", c=HG_CHUNK)
                by4 = lambda t: t.rearrange("p (j c) -> p j c", j=TB)

                def k_end(h):
                    if h:
                        n.take(hs["k_end_transposed"])
                    n.give(tt(chunks(tmp[:, 0, :]), chunks(hg_f[:, h, :]),
                              decay[:, h, :].unsqueeze(2).broadcast_to([P, 16, HG_CHUNK]), ALU.mult), hs["k_end"])

                k_end(0)
                for h in range(-1, HG_HEADS + 1):
                    if 0 <= h < HG_HEADS:
                        n.take(hs["updates"])
                        link(v.tensor_copy(hg_state[:, 1, :], X[:, 0, 0:P]))
                        for c in range(1, 15):
                            ins = stt(hg_state[:, c + 1, :], hg_state[:, c, :], decay[:, h, c:c + 1],
                                      X[:, c % 4, blk(c // 4)], ALU.mult, ALU.add)
                            if c < 14:
                                link(ins)
                        n.give(ins, hs["states"])
                    if h >= 1:
                        n.take(hs["std"])
                        link(v.reciprocal(rstd[:, 1, :], rstd[:, 0, :]))
                        n.give(tt(by4(tmp[:, 6, :]), ident.unsqueeze(1).broadcast_to([P, TB, P]),
                                  rstd[:, 1, :].unsqueeze(2).broadcast_to([P, TB, P]), ALU.mult), hs["diagonal"])
                    if h + 1 < HG_HEADS:
                        n.take(hs["scores"])
                        n.give(tt(by4(tmp[:, 2 + (h + 1) % 2, :]), by4(G[:, 0, :]),
                                  mask32[:, :].unsqueeze(1).broadcast_to([P, TB, P]), ALU.mult), hs["masked"])
                    if h + 2 < HG_HEADS:
                        k_end(h + 2)
                    if h >= 1:
                        n.take(hs["output_copied"])
                        n.take(hs["spread"])
                        o = tmp[:, 5 + 2 * ((h - 1) % 2), :]
                        link(tt(o, o, G[:, 3, :], ALU.mult))
                        n.give(tt(hg_g[:, h - 1, :], hg_g[:, h - 1, :], o, ALU.mult), hs["done"])
                n.own(hs["done"])
                split_lo(hg_g, u_hi, u_lo, s_uhi)

            def rope_tables():
                n.take(s_con, 64)
                two_pi = 2 * np.pi
                c_a = float(np.float32(6.28125))
                c_b = float((np.array([two_pi - c_a], np.float32).view(np.uint32) & np.uint32(0xFFFFF000)).view(np.float32)[0])
                c_c = float(np.float32(two_pi - c_a - c_b))
                magic = float(1.5 * 2 ** 23)
                link(v.tensor_copy(tmp[:, 0, :], sinT[:, :].bitcast(I32)))
                link(ts(tmp[:, 0, :], tmp[:, 0, :], freq, None, ALU.mult))
                link(ts(tmp[:, 1, :], tmp[:, 0, :], float(1 / two_pi), magic, ALU.mult, ALU.add))
                link(ts(tmp[:, 1, :], tmp[:, 1, :], -magic, None, ALU.add))
                for c in (c_a, c_b, c_c):
                    link(stt(tmp[:, 0, :], tmp[:, 1, :], -c, tmp[:, 0, :], ALU.mult, ALU.add))
                n.give(ts(tmp[:, 2, :], tmp[:, 0, :], 3.1415925, -3.1415925, ALU.min, ALU.max), d2a)
                n.take(a2d)
                link(ts(sinT[:, :], sinT[:, :], sign, None, ALU.mult))
                n.take(a2d)

            def rope(x, rot, mask, parts, tiles):
                wide = lambda t: t[0:parts, :].unsqueeze(1).broadcast_to([parts, tiles, S])
                link(v.stream_shuffle(rot, x, mask))
                tt(rot, rot, wide(sinT), ALU.mult)
                link(tt(x, x, wide(cosT), ALU.mult))
                return tt(x, x, rot, ALU.add)

            def attention(p):
                v.sem_inc(d2p, 1)
                n.made(d2p, 1)
                for t in range(8):
                    i, B = t % TB, banks[t % 2]
                    w, w0 = (i + 1) * P, 256 if i else P
                    n.take(p2d)
                    v.tensor_reduce(stat[:, 0:1], B[:, 0:2, 0:w], mybir.AxisListType.XY, ALU.max)
                    link(v.tensor_reduce(stat[:, 1:2], B[:, 2, 0:w0], AX, ALU.max))
                    n.give(ts(stat[:, 2:3], stat[:, 0:1], stat[:, 1:2], -ATT_SCALE, ALU.max, ALU.mult), d2a)
                    n.take(a2d)
                    link(tt(stat[:, 5:6], stat[:, 3:4], stat[:, 4:5], ALU.add))
                    link(v.reciprocal(stat[:, 6:7], stat[:, 5:6]))
                    n.give(ts(att_p[:, 0:2 * w + w0], att_p[:, 0:2 * w + w0], stat[:, 6:7], None, ALU.mult), d2p)

            def window_attention(l):
                swap = [i + 8 if i < 8 else i - 8 if i < 16 else i for i in range(32)]
                if l == 0:
                    n.take(s_con2, 32)
                for z, k, gain in ((z_k, 1, KN), (z_q, 4, QN)):
                    n.take(a2d)
                    ra = tmp[:, 4:4 + k, :]
                    link(v.reciprocal(ra, ra))
                    for t in range(k):
                        ins = stt(z[:, t, :], z[:, t, :], cols_b[:, gain + l:gain + l + 1], ra[:, t, :], ALU.mult, ALU.mult)
                    link(ins)
                    n.give(rope(z[:, 0:k, :], ra, swap, P, k), d2a if k == 1 else d2p)
                Pb = win_p.rearrange("p (i k) -> p i k", i=TB)
                for h in range(SW_HEADS):
                    sink = sinks[:, 8 * l + h:8 * l + h + 1]
                    n.take(p2d)
                    link(v.tensor_reduce(stat[:, 0:4], banksf[h % 2][:, 0:1024].rearrange("p (i k) -> p i k", i=TB), AX, ALU.max))
                    link(ts(stat[:, 4:8], stat[:, 0:4], SW_DIM ** -0.5, sink, ALU.mult, ALU.max))
                    n.give(ts(stat[:, 8:12], stat[:, 4:8], -1.0, None, ALU.mult), d2a)
                    n.take(a2d)
                    link(tt(stat[:, 20:24], stat[:, 12:16], stat[:, 16:20], ALU.add))
                    link(v.reciprocal(stat[:, 8:12], stat[:, 20:24]))
                    n.give(tt(Pb, Pb, stat[:, 8:12].unsqueeze(2).broadcast_to([P, TB, 256]), ALU.mult), d2p)

            def mlstm(l):
                R = [row[:, i, :] for i in range(4)]
                gi, gf = z_if[:, 0, :], z_if[:, 1, :]
                ch = lambda t: t.rearrange("p (n c) -> p n c", c=M_CHUNK)
                wide = lambda t: t.unsqueeze(2).broadcast_to([M_HEADS, 8, M_CHUNK])
                n.take(a2d)
                link(ts(R[1], gf, 0.0, None, ALU.min))
                v.memset(R[3], 1.0)
                link(tt(gf, R[1], R[0], ALU.subtract))
                link(v.memset(R[3][:, ::M_CHUNK], 0.0))
                link(v.tensor_tensor_scan(R[0], R[3], gf, 0.0, ALU.mult, ALU.add))
                g = srow[:, 0, :]
                v.tensor_copy(g, R[0][:, M_CHUNK - 1::M_CHUNK])
                link(tt(gi, gi, R[0], ALU.subtract))
                link(tt(ch(R[1]), ch(gi), wide(g), ALU.add))
                link(v.tensor_reduce(srow[:, 1, :], ch(R[1]), AX, ALU.max))
                v.memset(srow[:, 3, 0:1], 0.0)
                link(v.tensor_tensor_scan(srow[:, 2, :], g, srow[:, 1, :], 0.0, ALU.add, ALU.max))
                link(v.tensor_copy(srow[:, 3, 1:8], srow[:, 2, 0:7]))
                tt(ch(R[1]), ch(R[1]), wide(srow[:, 2, :]), ALU.subtract)
                tt(srow[:, 4, :], g, srow[:, 3, :], ALU.add)
                v.tensor_copy(R[2], gi)
                link(v.memset(R[3], 0.0))
                tt(srow[:, 5, :], srow[:, 4, :], srow[:, 2, :], ALU.subtract)
                v.memset(R[3][:, ::M_CHUNK], -3.0e38)
                link(tt(R[2][:, ::M_CHUNK], gi[:, ::M_CHUNK], srow[:, 3, :], ALU.max))
                link(v.tensor_tensor_scan(gf, R[3], R[2], 0.0, ALU.add, ALU.max))
                ts(R[2], gf, -1.0, None, ALU.mult)
                link(tt(R[3], R[0], gf, ALU.add))
                n.give(tt(ch(R[0]), wide(srow[:, 3, :]), ch(gf), ALU.subtract), d2a)
                n.take(ms["columns"])
                n.give(v.tensor_copy(mcol[:, :], X[:, 0, 0:80]), ms["columns_copied"])
                n.own(ms["columns_copied"])

                def q_alone(h):
                    n.give(ts(tmp[:, 1, :], z_qm[:, h // 2, :], q8[:, h % 2:h % 2 + 1], None, ALU.mult), ms["q_alone"])

                def k_end(h):
                    pr = h // 2
                    for j in range(TB):
                        ins = ts(tmp[:, 3, blk(j)], z_km[:, j, pr * P:(pr + 1) * P], mcol[:, 16 + 4 * j + h:17 + 4 * j + h], None, ALU.mult)
                    n.give(ins, ms["k_end"])

                q_alone(0)
                k_end(0)
                for h in range(-1, M_HEADS + 1):
                    if 0 <= h < M_HEADS:
                        n.take(ms["updates"])
                        link(v.tensor_copy(m_state[:, 0, :], G[:, 0, 0:P + 1]))
                        for c in range(1, 7):
                            bank, i = m_bank(c)
                            ins = stt(m_state[:, c, :], m_state[:, c - 1, :], mcol[:, 32 + 8 * h + c:33 + 8 * h + c],
                                      G[:, bank, (P + 1) * i:(P + 1) * (i + 1)], ALU.mult, ALU.add)
                            if c < 6:
                                link(ins)
                        n.give(ins, ms["states"])
                        if h + 1 < M_HEADS:
                            k_end(h + 1)
                    if h >= 1:
                        n.take(ms["transposed"])
                        n.give(stt(yT[:, 3 + h, :], G[:, 3, :], cols_a[:, MHN + 4 * l + h - 1:MHN + 4 * l + h], z_om[:, h - 1, :],
                                   ALU.mult, ALU.mult), ms["done"])
                    if h + 1 < M_HEADS:
                        W, qs = tmp[:, (0, 5)[(h + 1) % 2], :], tmp[:, (2, 7)[(h + 1) % 2], :]
                        n.take(ms["weights_exp"])
                        n.take(ms["scores"])
                        n.give(tt(W, W, X[:, 1, :], ALU.mult), ms["weights"])
                        n.take(ms["decay"])
                        n.own(ms["q_alone"])
                        n.give(tt(qs, tmp[:, 1, :], G[:, 3, :], ALU.mult), ms["q_decayed"])
                        if h + 2 < M_HEADS:
                            n.own(ms["q_decayed"])
                            q_alone(h + 2)
                    if 0 <= h < M_HEADS:
                        n.take(ms["squares"])
                        den = out_view[:, :, P:P + 1].rearrange("p j o -> p (j o)")
                        link(ts(stat[:, 0:4], den, -1.0, None, ALU.mult))
                        link(tt(stat[:, 4:8], den, stat[:, 0:4], ALU.max))
                        link(tt(stat[:, 4:8], stat[:, 4:8], mcol[:, 64 + h:80:4], ALU.max))
                        link(stt(stat[:, 8:12], stat[:, 4:8], EPS, stat[:, 4:8], ALU.mult, ALU.mult))
                        n.give(stt(stat[:, 12:16], stat[:, 12:16], 1.0 / P, stat[:, 8:12], ALU.mult, ALU.add), ms["variance"])
                        n.take(ms["std"])
                        link(v.reciprocal(stat[:, 20:24], stat[:, 16:20]))
                        n.give(tt(yT[:, 4 + h, :].rearrange("p (j c) -> p j c", j=TB), out_view[:, :, 0:P],
                                  stat[:, 20:24].unsqueeze(2).broadcast_to([P, TB, P]), ALU.mult), ms["normed"])
                n.own(ms["done"])
                split_lo(yT, u_hi, u_lo, s_uhi)

            def copy_out(g, b):
                for m in range(4):
                    evicted(g, b, m, lambda: v.tensor_copy(yT[:, b * 4 + m, :], G[:, m, :]))

            def add_out(dst):
                def f(g, b):
                    for m in range(4):
                        evicted(g, b, m, lambda: tt(dst[:, b * 4 + m, :], dst[:, b * 4 + m, :], G[:, m, :], ALU.add))
                return f

            for name in order:
                if name in ("hg_q", "hg_f", "hg_v", "hg_g"):
                    linear(name, nothing, ada=ADA_FIRST + 2 * ("hg_q", "hg_f", "hg_v", "hg_g").index(name),
                           after=None if name == "hg_q" else lambda b: hgrn_decays(name, b))
                    if name == "hg_g":
                        hgrn()
                elif name == "hg_out":
                    linear(name, copy_out, ada=ADA_FIRST + 7)
                    dve.wait_ge(s_mod, ADA_BLOCKS)
                    mixing(0, 0)
                    link(mixing(0, 1))
                    add_to_h(0, 0)
                    norm_tail()
                    to_u(hT)
                elif name.startswith("ffn_in"):
                    l, hf = int(name[-2]), int(name[-1])
                    fr, fhi, silu = n.at("fr"), n.at("fhi"), n.at("silu")

                    def product(g, b):
                        for m in range(2):
                            dve.wait_ge(s_silu, b * 2 + (silu + m + 1))
                            v.sem_inc(s_free["dve"], 1)
                        for m in range(2):
                            dve.wait_ge(s_fr, b * 2 + (fr + 2))
                            evicted(g, b, 2 + m, lambda: tt(hid_f[:, m, :], silu_g[:, m, :], G[:, 2 + m, :], ALU.mult))
                        for m in range(2):
                            dve.wait_ge(s_fhi, b * 2 + (fhi + m + 1))
                            dve.wait_ge(s_free["dve"], b * 4 + (g["mine"] + 3 + m))
                            tt(hid_lo[:, b * 2 + m, :], hid_f[:, m, :], hid_hi[:, b * 2 + m, :].bitcast(F32), ALU.subtract).then_inc(s_fr, 1)
                    linear(name, product, ada=(ADA_FIRST + 9 + 6 * hf) if l == 0 else None)
                    for q in ("fr", "fhi", "silu"):
                        n.skip(q, 2 * plan[name]["blocks"])
                elif name.startswith("ffn_out"):
                    l, hf = int(name[-2]), int(name[-1])
                    if hf == 0:
                        linear(name, copy_out)
                    else:
                        linear(name, add_out(yT))
                        if l == 0:
                            dve.wait_ge(s_mod, 24)
                            mixing(1, 0)
                            link(mixing(1, 1))
                        add_to_h(l, 1)
                        norm_tail()
                        to_u(hT)
                elif name == "at_v":
                    linear(name, nothing)
                    rope_tables()
                elif name.startswith("at_qk"):
                    def qk(g, b):
                        for m in range(4):
                            evicted(g, b, m, lambda: v.tensor_copy(at_qk[:, b, m, :], G[:, m, :]))

                    base = n.given[s_dve]

                    def rotate(b):
                        swap = [(i + 16) % 32 for i in range(32)]
                        x, rot = at_qk[0:32, b, :, :], tmp[0:32, 0:4, :]
                        wide = lambda t: t[0:32, :].unsqueeze(1).broadcast_to([32, 4, S])
                        dve.wait_ge(s_free["dve"], b * 4 + (plan[name]["mine"] + 4))
                        if b:
                            dve.wait_ge(s_dve, b * 3 + base)
                        v.stream_shuffle(rot, x, swap).then_inc(s_dve, 1)
                        dve.wait_ge(s_dve, b * 3 + (base + 1))
                        tt(rot, rot, wide(sinT), ALU.mult)
                        tt(x, x, wide(cosT), ALU.mult).then_inc(s_dve, 1)
                        dve.wait_ge(s_dve, b * 3 + (base + 2))
                        tt(x, x, rot, ALU.add).then_inc(s_dve, 1)
                    linear(name, qk, after=rotate)
                    n.made(s_dve, 9)
                    n.own(s_dve)
                    attention(int(name[-1]))
                    if name[-1] == "3":
                        v.sem_inc(s_rope1, 1)
                        split_lo(yT, u_hi, u_lo, s_uhi)
                elif name == "at_out":
                    linear(name, copy_out)
                    add_to_h(1, 0)
                    norm_tail()
                    to_u(hT)
                elif name.startswith("zg"):
                    linear(name, nothing)
                    window_attention(int(name[-1]))
                    mlstm(int(name[-1]))
                elif name.startswith("z"):
                    v.memset(z_vm[:, :, :, P:P + 1], 1.0)
                    n.give(v.memset(vpad[:, :, :, :, :].rearrange("p a b c d -> p (a b c d)"), 0.0), d2a)
                    linear(name, nothing)
                elif name.startswith("br"):
                    def branch(g, b):
                        for m in range(4):
                            t = b * 4 + m
                            evicted(g, b, m, lambda: tt(gate[:, t, :], gate[:, t, :], G[:, m, :], ALU.mult))
                    linear(name, branch)
                    dve.wait_ge(s_free["dve"], plan[name]["mine"] + 16)
                    for k in range(KT):
                        n.give(tt(gate[:, k, :], gate[:, k, :], gate[:, 8 + k, :], ALU.add), d2a)
                    for k in range(KT):
                        n.take(s_uhi)
                        n.give(tt(mx_lo[:, k, :], gate[:, k, :], mx_hi[:, k, :].bitcast(F32), ALU.subtract), s_u)
                elif name.startswith("mo"):
                    linear(name, add_out(hT))
                    norm_tail()
                    to_u(hT)
                elif name.startswith("ff_in"):
                    fr, fhi = n.at("fr"), n.at("fhi")
                    gff = n.at("ff")

                    def square(g, b):
                        def lo(m):
                            dve.wait_ge(s_fhi, b * 4 + (fhi + m + 1))
                            tt(ff_lo[:, b * 4 + m, :], sq_f[:, m % 2, :], ff_hi[:, b * 4 + m, :].bitcast(F32), ALU.subtract).then_inc(s_fr, 1)
                        for m in range(4):
                            dve.wait_ge(s_free["act"], b * 4 + (g["mine"] + m + 1))
                            dve.wait_ge(s_fr, b * 4 + (fr + 2 + m - 1))
                            tt(sq_f[:, m % 2, :], relu_f[:, m % 2, :], relu_f[:, m % 2, :], ALU.mult).then_inc(s_ff, 1)
                            if m >= 1:
                                lo(m - 1)
                        lo(3)
                    linear(name, square)
                    n.skip("fr", 16)
                    n.skip("fhi", 16)
                elif name.startswith("ff_out"):
                    linear(name, add_out(hT))
                    if name == "ff_out01":
                        norm_tail()
                        to_u(hT)
            for q in range(8):
                n.take(p2d)
                v.tensor_copy(x_view[:, q // 2, (q % 2) * 512:(q % 2) * 512 + 512], (G if q < 4 else X)[:, q % 4, :]).then_inc(s_res, 1)

        @block.tensor
        def _(pe):
            n = Counts(pe)
            mm, tr = nc.tensor.matmul, nc.tensor.transpose

            def linear(name, x_hi, x_lo, tiles=None, ada=None, x0=lambda b: 0):
                g = plan[name]
                other = "dve" if g["evictor"] == "act" else "act"
                pe.wait_ge(s_free[other], g["other"])
                for b in blocks(pe, name):
                    for s in range(g["chunks"]):
                        slot = slot_of(name, b, s)
                        pe.wait_ge(s_lo, b * g["chunks"] + (g["c0"] + s + 1))
                        nk = min(4, g["ktiles"] - 4 * s)
                        w, xs = (w_hi[slot], w_lo[slot]), (x_hi, x_lo)
                        for m in range(4):
                            if s == 0:
                                pe.wait_ge(s_free[g["evictor"]], b * 4 + (g["mine"] + m - 3))
                            spec = tiles(b, m) if tiles else None
                            last_k = g["ktiles"] - 1
                            for part in (spec if isinstance(spec, list) else [None]):
                                for k in range(nk):
                                    kk = 4 * s + k
                                    if m == 0 and name in u_base and part in (None, (spec or [0])[0]):
                                        pe.wait_ge(s_u, u_base[name] + x0(b) + kk + 1)
                                    for iw, ix in PASSES:
                                        first = kk == 0 and (iw, ix) == (0, 0) and (part is None or part is spec[0])
                                        last = kk == last_k and (iw, ix) == (1, 0)
                                        if part is None:
                                            c0, c1_ = spec or (m * P, m * P + P)
                                            ins = mm(G[0:c1_ - c0, m, :], w[iw][:, k, c0:c1_], xs[ix][:, x0(b) + kk, :],
                                                     start=first, stop=last, skip_group_check=True)
                                        else:
                                            tok, (c0, c1_), (o0, o1) = part
                                            ins = mm(G[:, m, o0:o1], xs[ix][:, kk, blk(tok)], w[iw][:, k, c0:c1_],
                                                     start=first, stop=last, skip_group_check=True)
                            if s == g["chunks"] - 1:
                                ins.then_inc(s_tile, 1)
                            elif m == 3:
                                ins.then_inc(s_inner, 1)
                    if ada is not None and with_ada(name, b):
                        ada_sum(b + ada)

            def ada_sum(i):
                pe.wait_ge(s_astep, i * 8 + 8)
                if not isinstance(i, int) or i > 0:
                    pe.wait_ge(s_mod, i)
                for q in range(4):
                    ins = mm(X[:, 3, q:q + 1], acc[:, blk(q)], ones[:, 0:1], start=True, stop=True, skip_group_check=True)
                ins.then_inc(s_asum, 1)

            def norm():
                for k in range(KT):
                    n.take(s_sq)
                    for j in range(TB):
                        ins = mm(X[:, 0, j:j + 1], tmp[:, k % 2, blk(j)], ones[:, 0:1],
                                 start=k == 0 and j == 0, stop=k == KT - 1, skip_group_check=True)
                    n.give(ins, s_sqd)
                n.take(s_diag)
                n.give(mm(X[:, 1, :], ones, tmp[:, 7, :], start=True, stop=True), s_spread)

            def transposes(out_bank, src, count, sem_, dst0=0):
                for j in range(count):
                    ins = tr(out_bank[:, blk(dst0 + j)], src(j), ident)
                if sem_ is not None:
                    n.give(ins, sem_)
                return ins

            n.take(s_in, 16 * 20)
            tr(X[:, 0, 0:P], rhs_a, ident)
            n.give(tr(X[:, 1, 0:100], rows_b[0:100, :], ident[0:100, 0:100]), p2d)
            for k in range(KT):
                if k == 4:
                    n.take(s_h, 1)
                transposes((G if k < 4 else X)[:, k % 4, :], lambda j: x_view[:, j, blk(k)], TB, p2d)
            n.take(s_h, 7)
            norm()
            for i in range(ADA_FIRST):
                ada_sum(i)

            def hgrn():
                pe.wait_ge(s_free["act"], plan["hg_g"]["mine"] + 8)
                for h in range(-1, HG_HEADS + 1):
                    if 0 <= h < HG_HEADS:
                        n.take(hs["k_end_copied"])
                        for c in range(15):
                            r = slice(32 * (c % 4), 32 * (c % 4) + 32)
                            ins = mm(X[:, c % 4, blk(c // 4)], tmp[r, 1, blk(c // 4)], hg_v[r, c // 4, blk(h)],
                                     start=True, stop=True, skip_group_check=True)
                        n.give(ins, hs["updates"])
                    if h >= 1:
                        n.take(hs["squares"])
                        if h >= 2:
                            n.take(hs["done"])
                        for j in range(TB):
                            ins = mm(G[:, 3, j:j + 1], tmp[:, 4, blk(j)], ones[:, 0:1], start=j == 0, stop=True, skip_group_check=True)
                        n.give(ins, hs["sums"])
                    if h + 1 < HG_HEADS:
                        if h >= 0:
                            n.take(hs["masked"])
                        for j in range(TB):
                            ins = mm(G[:, 0, blk(j)], hg_f[:, h + 1, blk(j)], hg_q[:, h + 1, blk(j)], start=True, stop=True, skip_group_check=True)
                        n.give(ins, hs["scores"])
                        n.take(hs["k_end"])
                        transposes(G[:, 1, :], lambda j: tmp[:, 0, blk(j)], TB, hs["k_end_transposed"])
                    if 0 <= h < HG_HEADS:
                        n.take(hs["states"])
                        if h == HG_HEADS - 1:
                            n.take(hs["masked"])
                        if h >= 1:
                            n.take(hs["output_copied"])
                        for j in range(TB):
                            mm(G[:, 2, blk(j)], hg_v[:, j, blk(h)], tmp[:, 2 + h % 2, blk(j)], start=j == 0, stop=False, skip_group_check=True)
                        for c in range(1, 16):
                            ins = mm(G[:, 2, 32 * c:32 * c + 32], hg_state[:, c, :], hg_q[:, h, 32 * c:32 * c + 32],
                                     start=False, stop=c == 15, skip_group_check=True)
                        n.give(ins, hs["output"])
                    if h >= 1:
                        n.take(hs["diagonal"])
                        n.give(mm(G[:, 3, :], ones, tmp[:, 6, :], start=True, stop=True), hs["spread"])

            def attention(p):
                n.take(d2p)
                for t in range(-1, 9):
                    if t >= 1:
                        n.take(a2p)
                    if t == TB + 2:
                        n.take(a2p)
                    if t + 1 < 8:
                        hh, i = divmod(t + 1, TB)
                        w, w0 = (i + 1) * P, 256 if i else P
                        for bank, (g, lo, hi) in enumerate(((1, 512 - w, 512), (2, 1024 - w, 1024), (0, 1280 - w0, 1280))):
                            o = banks[(t + 1) % 2][:, bank, 0:hi - lo]
                            mm(o, identb, mk("dil", lo, hi), start=True, stop=False)
                            ins = mm(o, at_qk[:, g, hh, blk(i)], at_qk[:, g, 2 + hh, (i + 1) * P - (hi - lo):(i + 1) * P],
                                     start=False, stop=True)
                        n.give(ins, p2d)
                    if 0 <= t < 8:
                        n.take(d2p)
                        transposes(banksf[t % 2], lambda j: att_p[:, blk(j)], att_blocks(t), p2a)
                    if t >= 1:
                        hh, i = divmod(t - 1, TB)
                        h = 2 * p + hh
                        where = [(1, j) for j in range(i + 1)] + [(2, j) for j in range(i + 1)] + [(0, j) for j in range(max(i - 1, 0), i + 1)]
                        for c, (g, j) in enumerate(where):
                            ins = mm(banks[hh][:, 3, blk(i)], at_v[:, j, g * D + h * P:g * D + (h + 1) * P], att_pt[(t - 1) % 2][:, blk(c)],
                                     start=i == 0 and c == 0, stop=c == len(where) - 1, skip_group_check=True)
                        if i == TB - 1:
                            n.give(ins, p2a)
                n.take(a2p)

            def window_attention(l):
                n.take(a2p)
                n.give(mm(X[:, 0, :], half, tmp[:, 4, :], start=True, stop=True), p2a)
                n.take(a2p)
                for t in range(4):
                    ins = mm(X[:, t, :], half, tmp[:, 4 + t, :], start=True, stop=True)
                n.give(ins, p2a)
                n.take(d2p)
                for t in range(4):
                    ins = mm(X[:, t, :], selk[:, t, :], z_k[:, 0, :], start=True, stop=True)
                n.give(ins, p2a)
                n.take(a2p)
                for step in range(-1, 9):
                    if step >= 1:
                        n.take(a2p)
                    if step >= 4 and step % 2 == 0:
                        n.take(a2p)
                    h = step + 1
                    if h < SW_HEADS:
                        t, hf, kv = h // 2, h % 2, h // 4
                        kp = tmp[:, 2 * kv + hf, :]
                        B = banks[h % 2]
                        for bank in range(2):
                            mm(B[:, bank, :], identb, mk("sw", 512 * bank, 512 * bank + 512), start=True, stop=False, skip_group_check=True)
                        for i in range(TB):
                            c0 = 256 * (i % 2)
                            lo = (i - 1) * P if i else 0
                            o = B[:, i // 2, c0 + (0 if i else P):c0 + 256]
                            ins = mm(o, z_q[:, t, blk(i)], kp[:, lo:(i + 1) * P], start=False, stop=True, skip_group_check=True)
                        n.give(ins, p2d)
                    if 0 <= step < SW_HEADS:
                        n.take(d2p)
                        transposes(banksf[step % 2], lambda j: win_p[:, blk(j + 1)], 7, p2a)
                    if step >= 1:
                        h = step - 1
                        t, hf, kv = h // 2, h % 2, h // 4
                        for j in range(7):
                            i, cur = (j + 1) // 2, (j + 1) % 2
                            ins = mm(banks[t % 2][:, 2, blk(i)], vpad[:, i if cur else i - 1, kv, hf, :], win_pt[h % 2][:, blk(j)],
                                     start=hf == 0 and j == 0, stop=hf == 1, skip_group_check=True)
                        if hf:
                            n.give(ins, p2a)
                n.take(a2p)

            def mlstm(l):
                gi = z_if[:, 0, :]
                n.take(a2p)
                for j in range(TB):
                    mm(X[:, 0, 4 * j:4 * j + 4], gi[:, blk(j)], ident[0:4, 0:4], start=j == 0, stop=True, skip_group_check=True)
                    mm(X[:, 0, 16 + 4 * j:20 + 4 * j], row[:, 1, blk(j)], ident[0:4, 0:4], start=False, stop=True, skip_group_check=True)
                    mm(X[:, 0, 64 + 4 * j:68 + 4 * j], row[:, 3, blk(j)], ident[0:4, 0:4], start=False, stop=True, skip_group_check=True)
                for h in range(M_HEADS):
                    ins = mm(X[:, 0, 32 + 8 * h:40 + 8 * h], sel4[0:4, blk(h)], srow[:, 6, :], start=False, stop=True, skip_group_check=True)
                n.give(ins, ms["columns"])
                for pr in range(2):
                    transposes(X[:, 2 + pr, :], lambda j: z_km[:, j, pr * P:(pr + 1) * P], TB, ms["k_transposed"])
                n.take(ms["columns_copied"])
                n.take(ms["k_copied"], 2)
                for h in range(-1, M_HEADS + 1):
                    if 0 <= h < M_HEADS:
                        n.take(ms["k_end"])
                        for c in range(7):
                            r = slice(64 * (c % 2), 64 * (c % 2) + 64)
                            bank, i = m_bank(c)
                            ins = mm(G[:, bank, (P + 1) * i:(P + 1) * (i + 1)], tmp[r, 3, blk(c // 2)], z_vm[r, c // 2, h, :],
                                     start=True, stop=True, skip_group_check=True)
                        n.give(ins, ms["updates"])
                    if h >= 1:
                        n.take(ms["normed"])
                        transposes(G[:, 3, :], lambda j: yT[:, 3 + h, blk(j)], TB, ms["transposed"])
                    if h + 1 < M_HEADS:
                        pr, sel = (h + 1) // 2, sel4[0:4, blk(h + 1)]
                        if h >= 0:
                            n.take(ms["weights"])
                        mm(X[:, 0, :], identb, mk("ml", 0, 512), start=True, stop=False)
                        n.give(mm(X[:, 0, :], sel, row[:, 2, :], start=False, stop=True), ms["exponents"])
                        n.take(ms["q_alone"])
                        for j in range(TB):
                            ins = mm(X[:, 1, blk(j)], tmp[:, (4, 6)[pr], blk(j)], tmp[:, 1, blk(j)], start=True, stop=True, skip_group_check=True)
                        n.give(ins, ms["scores"])
                        if h >= 0:
                            n.take(ms["q_decayed"])
                        if h >= 1:
                            n.take(ms["done"])
                        n.give(mm(G[:, 3, :], sel, row[:, 0, :], start=True, stop=True), ms["decay"])
                    if 0 <= h < M_HEADS:
                        if h == M_HEADS - 1:
                            n.take(ms["weights"])
                            n.take(ms["q_decayed"])
                        n.take(ms["states"])
                        W, qs = tmp[:, (0, 5)[h % 2], :], tmp[:, (2, 7)[h % 2], :]
                        for j in range(TB):
                            mm(out_view[:, j, 0:P + 1], W[:, blk(j)], z_vm[:, j, h, :], start=j % 2 == 0, stop=False, skip_group_check=True)
                        for c in range(1, 8):
                            r = slice(64 * (c % 2), 64 * (c % 2) + 64)
                            ins = mm(out_view[r, c // 2, 0:P + 1], qs[:, 64 * c:64 * c + 64], m_state[:, c - 1, :],
                                     start=False, stop=c == 7, skip_group_check=True)
                        n.give(ins, ms["output"])
                n.take(ms["done"], 2)

            u_base = {}

            def u_ready():
                u_base[name] = n.at(s_u)
                n.skip(s_u, KT)

            n.skip(s_fr, 2)
            fr = [0]

            def token_tiles(b, m):
                return [(m, (0, 512), (0, 512))]

            def z_tiles(b, m):
                if b == 1 and m == 1:
                    return [(j, (P, 2 * P), (j * P, (j + 1) * P)) for j in range(TB)]
                if b == 2:
                    return [(m, (0, 512), (0, 512))]
                if b == 3 and m < 2:
                    return [(2 * m + j, (0, 256), (256 * j, 256 * j + 256)) for j in range(2)]
                if b == 4 and m >= 2:
                    return (256 + 4 * (m - 2), 260 + 4 * (m - 2))
                return None

            for name in order:
                if name in ("hg_q", "hg_f", "hg_v", "hg_g"):
                    if name == "hg_q":
                        u_ready()
                    linear(name, u_hi, u_lo, token_tiles if name == "hg_v" else None,
                           ada=ADA_FIRST + 2 * ("hg_q", "hg_f", "hg_v", "hg_g").index(name))
                    if name == "hg_g":
                        hgrn()
                elif name in ("hg_out", "at_out"):
                    u_ready()
                    linear(name, u_hi, u_lo, ada=ADA_FIRST + 7 if name == "hg_out" else None)
                    norm()
                    norm()
                elif name.startswith("ffn_in"):
                    l, hf = int(name[-2]), int(name[-1])
                    if hf == 0:
                        u_ready()
                    linear(name, u_hi, u_lo, ada=(ADA_FIRST + 9 + 6 * hf) if l == 0 else None)
                    n.take(s_fr, FF1_TILES[hf])
                elif name.startswith("ffn_out"):
                    linear(name, hid_hi, hid_lo)
                    if name[-1] == "1":
                        norm()
                        norm()
                elif name == "at_v":
                    u_ready()
                    linear(name, u_hi, u_lo, token_tiles)
                elif name.startswith("at_qk"):
                    linear(name, u_hi, u_lo)
                    attention(int(name[-1]))
                elif name.startswith("zg"):
                    linear(name, u_hi, u_lo)
                    window_attention(int(name[-1]))
                    mlstm(int(name[-1]))
                elif name.startswith("z"):
                    u_ready()
                    linear(name, u_hi, u_lo, z_tiles)
                elif name.startswith("br"):
                    u_ready()
                    linear(name, u_hi, u_lo, x0=lambda b: 0 if b < 2 else 4)
                elif name.startswith("mo"):
                    u_ready()
                    linear(name, mx_hi, mx_lo)
                    norm()
                elif name.startswith("ff_in"):
                    if name[-1] == "0":
                        u_ready()
                    linear(name, u_hi, u_lo)
                    n.take(s_fr, 16)
                elif name.startswith("ff_out"):
                    linear(name, ff_hi, ff_lo)
                    if name == "ff_out01":
                        norm()
            for e in ("act", "dve"):
                pe.wait_ge(s_free[e], sum(4 * plan[x]["blocks"] for x in order if plan[x]["evictor"] == e) + 4)
            for q in range(8):
                bank = (G if q < 4 else X)[:, q % 4, :]
                transposes(bank, lambda j: hT[:, 4 * (q % 2) + j, blk(q // 2)], 4, p2d)

    return plan


NAMES = ["x", "c", "positions", "ada_w", "ada_b", "norm_g", "hgrn_w_in", "hgrn_lower_bounds", "hgrn_norm_g",
         "hgrn_w_out", "attn_w_in", "attn_w_out", "ffn_w_in", "ffn_w_out", "norm_mix_2", "w_in_2", "att_q_norm_2",
         "att_k_norm_2", "att_sinks_2", "m_gate_bias_2", "m_head_norm_2", "w_att_branch_2", "w_m_branch_2",
         "w_out_2", "norm_ffn_2", "w_ff1_2", "w_ff2_2"]


def make(nc, inputs, stop=None):
    first, second, m = constants()
    con1, where1 = pack(first)
    con2, where2 = pack(second)
    masks, where3 = pack(m)
    arrays = {f"in_{k}": np.ascontiguousarray(inputs[k]) for k in NAMES}
    arrays.update(in_con1=con1, in_con2=con2, in_masks=masks)
    aps = {}
    for k, v in arrays.items():
        aps[k[3:]] = nc.dram_tensor(k, v.shape, mybir.dt.from_np(v.dtype), kind="ExternalInput").ap()
    out = nc.dram_tensor("out", (1, S, D), F32, kind="ExternalOutput").ap()
    build(nc, aps, out, where1, where2, where3, stop)
    return arrays


def kernel(**inputs):
    import concourse.bacc as bacc
    from concourse.bass_utils import run_bass_kernel_spmd

    nc = bacc.Bacc("TRN2", target_bir_lowering=False, num_devices=1, dynamic_dma_scratch_size=4096)
    arrays = make(nc, inputs)
    r = run_bass_kernel_spmd(nc, [arrays], core_ids=[0])
    return r.results[0]["out"]
```

```python
import concourse.bass as bass
import numpy as np
from concourse import mybir
from contextlib import ExitStack

F32 = mybir.dt.float32
F32R = mybir.dt.float32r
BF16 = mybir.dt.bfloat16
U16 = mybir.dt.uint16
I32 = mybir.dt.int32
ACT = mybir.ActivationFunctionType
ALU = mybir.AluOpType
AX = mybir.AxisListType.X

P = 128
S = 512
D = 1024
KT = D // P
TB = S // P
NEG = -1.0e30
EPS = 1e-6

HG_HEADS, HG_CHUNK = 8, 32
ATT_HEADS, GROUPS = 8, 3
ATT_SCALE = 128 ** -0.5
ROPE_THETA = 500000.0
FF1 = 2816
FF1_TILES = (12, 10)
SW_HEADS, SW_DIM = 8, 64
M_HEADS, M_CHUNK, M_DK = 4, 64, 64
FF2 = 4096
Z = {"q_a": 0, "k_a": 512, "v_a": 640, "q_m": 768, "k_m": 1024, "v_m": 1280, "o_m": 1792, "if": 2304, "gate": 2312}
ADA_BLOCKS = 12
ADA_FIRST = 4


def constants():
    r = np.arange(P)
    f = {}
    f["ident"] = np.eye(P)
    f["ones"] = np.ones((P, P))
    f["half"] = (r[:, None] // 64 == r[None, :] // 64)
    s, c = r[:, None], r[None, :]
    mask32 = (s // HG_CHUNK == c // HG_CHUNK) & (s <= c)
    inv = ROPE_THETA ** (-np.arange(0, 32, 2, dtype=np.float32) / np.float32(32))
    freq = np.zeros((P, 1), np.float32)
    freq[:32, 0] = np.tile(inv.astype(np.float32), 2)
    f["freq"] = freq
    sign = np.zeros((P, 1))
    sign[:16], sign[16:32] = -1, 1
    f["sign"] = sign
    q8 = np.zeros((P, 2))
    q8[:64, 0] = q8[64:, 1] = M_DK ** -0.5
    f["q8"] = q8
    first = {k: np.asarray(v, np.float32) for k, v in f.items()}

    g = {"mask32": mask32}
    inv2 = ROPE_THETA ** (-np.arange(0, 16, 2, dtype=np.float32) / np.float32(16))
    ang = np.arange(S, dtype=np.float32)[None, :] * inv2.astype(np.float32)[:, None]
    cos2, sin2 = np.ones((P, S)), np.zeros((P, S))
    for h in (0, 64):
        cos2[h:h + 8] = cos2[h + 8:h + 16] = np.cos(ang)
        sin2[h:h + 8], sin2[h + 8:h + 16] = -np.sin(ang), np.sin(ang)
    g["cos2"], g["sin2"] = cos2, sin2
    sel = []
    for kv in range(2):
        for half in range(2):
            m = np.zeros((P, P))
            m[kv * 64 + np.arange(64), half * 64 + np.arange(64)] = 1
            sel.append(m)
    g["selk"] = np.concatenate(sel, 1)
    sel4 = np.zeros((P, M_HEADS, P))
    for h in range(M_HEADS):
        sel4[h, h] = 1
    g["sel4"] = sel4.reshape(P, -1)
    second = {k: np.asarray(v, np.float32) for k, v in g.items()}

    q, k = r[:, None], r[None, :]
    n = lambda ok: np.where(ok, 0.0, NEG)
    off1, off2 = n((q - k) % 4 == 0), n((q - k) % 16 == 0)
    d1, d2 = n(((q - k) % 4 == 0) & (k <= q)), n(((q - k) % 16 == 0) & (k <= q))
    causal = n(k <= q)
    prev0 = n(k >= q)
    m = {"dil": np.concatenate([off1, off1, off1, d1, off2, off2, off2, d2, prev0, causal], 1)}
    prevw = n(k > q)
    full = np.full((P, P), NEG)
    m["sw"] = np.concatenate([full, causal, prevw, causal, prevw, causal, prevw, causal], 1)
    md = n((q // M_CHUNK == k // M_CHUNK) & (q <= k))
    m["ml"] = np.tile(md, (1, TB))
    m["identb"] = np.eye(P)
    masks = {k2: (np.ascontiguousarray(v, np.float32).view(np.uint32) >> 16).astype(np.uint16) for k2, v in m.items()}
    return first, second, masks


def pack(parts):
    at, where = 0, {}
    for k, v in parts.items():
        where[k] = (at, at + v.shape[1])
        at += v.shape[1]
    return np.ascontiguousarray(np.concatenate(list(parts.values()), 1)), where


class Counts:

    def __init__(self, eng):
        self.eng, self.seen, self.given = eng, {}, {}

    def take(self, sem, n=1):
        self.seen[sem] = self.seen.get(sem, 0) + n
        self.eng.wait_ge(sem, self.seen[sem])

    def skip(self, sem, n):
        self.seen[sem] = self.seen.get(sem, 0) + n

    def at(self, sem):
        return self.seen.get(sem, 0)

    def give(self, ins, sem, n=1):
        ins.then_inc(sem, n)
        self.given[sem] = self.given.get(sem, 0) + n

    def made(self, sem, n):
        self.given[sem] = self.given.get(sem, 0) + n

    def own(self, sem):
        self.eng.wait_ge(sem, self.given[sem])


def gemm_plan():
    plan, order = {}, []

    def add(name, blocks, ktiles, evictor):
        chunks = -(-ktiles // 4)
        order.append(name)
        plan[name] = dict(blocks=blocks, chunks=chunks, ktiles=ktiles, evictor=evictor)

    def ffn1(l):
        for half, n in enumerate(FF1_TILES):
            add(f"ffn_in{l}{half}", n // 2, KT, "dve")
            add(f"ffn_out{l}{half}", 2, n, "dve")

    add("hg_q", 2, KT, "act")
    add("hg_f", 2, KT, "act")
    add("hg_v", 2, KT, "act")
    add("hg_g", 2, KT, "act")
    add("hg_out", 2, KT, "dve")
    ffn1(0)
    add("at_v", 6, KT, "act")
    for p in range(4):
        add(f"at_qk{p}", 3, KT, "dve")
    add("at_out", 2, KT, "dve")
    ffn1(1)
    for l in range(2):
        add(f"z{l}", 5, KT, "act")
        add(f"zg{l}", 4, KT, "act")
        add(f"br{l}", 4, 4, "dve")
        add(f"mo{l}", 2, KT, "dve")
        for half in range(2):
            add(f"ff_in{l}{half}", 4, KT, "act")
            add(f"ff_out{l}{half}", 2, 16, "dve")
    c = t = inner = 0
    freed = {"act": 4, "dve": 4}
    for name in order:
        g = plan[name]
        g.update(c0=c, t0=t, inner0=inner, mine=freed[g["evictor"]], other=freed["dve" if g["evictor"] == "act" else "act"])
        c += g["blocks"] * g["chunks"]
        inner += g["blocks"] * (g["chunks"] - 1)
        t += 4 * g["blocks"]
        freed[g["evictor"]] += 4 * g["blocks"]
    return plan, order, c


def build(nc, a, out, where1, where2, where3, stop=None):
    plan, order, n_chunks = gemm_plan()
    if stop is not None:
        order = order[:order.index(stop) + 1]
        n_chunks = plan[stop]["c0"] + plan[stop]["blocks"] * plan[stop]["chunks"]
    ctx = ExitStack()

    def sb(name, shape, dt=F32, stack=None):
        return (stack or ctx).enter_context(nc.sbuf_tensor(name, shape, dt))

    def sem(name):
        return ctx.enter_context(nc.semaphore(name))

    with ctx:
        hT = sb("hT", [P, KT, S])
        yT = sb("yT", [P, KT, S])
        u_hi, u_lo = sb("u_hi", [P, KT, S], F32R), sb("u_lo", [P, KT, S], F32R)
        raw = [sb(f"raw{i}", [P, 4, 512]) for i in range(2)]
        w_hi = [sb(f"w_hi{i}", [P, 4, 512], F32R) for i in range(2)]
        w_lo = [sb(f"w_lo{i}", [P, 4, 512], F32R) for i in range(2)]
        tmp = sb("tmp", [P, 8, S])
        con1 = sb("con1", [P, max(v[1] for v in where1.values())])
        cols_a, cols_b = sb("cols_a", [P, P]), sb("cols_b", [P, P])
        mod, mix, cond, lbc = sb("mod", [P, 96]), sb("mix", [P, 64]), sb("cond", [P, KT]), sb("lbc", [P, 3, KT])
        sinks, gbias, stat = sb("sinks", [P, 16]), sb("gbias", [4, 4]), sb("stat", [P, 24])
        rstd = sb("rstd", [P, 3, TB])
        with ExitStack() as room:
            masks = sb("masks", [P, max(v[1] for v in where3.values())], U16, room)
            cosT, sinT = sb("cosT", [P, S], F32, room), sb("sinT", [P, S], F32, room)
            sel4, selk = sb("sel4", [P, 512], F32, room), sb("selk", [P, 4, P], F32, room)
        ada_raw = sb("ada_raw", [P, 2, 4, 512])
        ada_room = ExitStack()
        acc, mask32 = sb("acc", [P, 512], F32, ada_room), sb("mask32_sb", [P, P], F32, ada_room)
        with ExitStack() as room:
            hg_q, hg_f, hg_g = (sb(n, [P, 8, S], F32, room) for n in ("hg_q", "hg_f", "hg_g"))
            hg_v = sb("hg_v", [P, TB, D], F32, room)
            decay = sb("decay", [P, HG_HEADS, S // HG_CHUNK], F32, room)
        with ExitStack() as room:
            hid_hi, hid_lo = (sb(n, [P, FF1_TILES[0], S], F32R, room) for n in ("hid_hi", "hid_lo"))
            silu_g, hid_f = (sb(n, [P, 2, S], F32, room) for n in ("silu_g", "hid_f"))
        ada_room.close()
        with ExitStack() as room:
            at_v = sb("at_v", [P, TB, GROUPS * D], F32, room)
            at_qk = sb("at_qk", [P, GROUPS, 4, S], F32, room)
        with ExitStack() as room:
            gate = sb("gate", [P, 16, S], F32, room)
            with ExitStack() as sub:
                z_km, z_vm = sb("z_km", [P, TB, 256], F32, sub), sb("z_vm", [P, TB, M_HEADS, P + 1], F32, sub)
                z_om, z_if = sb("z_om", [P, 4, S], F32, sub), sb("z_if", [M_HEADS, 2, S], F32, sub)
                srow = sb("srow", [M_HEADS, 8, 8], F32, sub)
                with ExitStack() as sub2:
                    z_q = sb("z_q", [P, 4, S], F32, sub2)
                    vpad = sb("vpad", [P, TB, 2, 2, P], F32, sub2)
                with ExitStack() as sub2:
                    m_state = sb("m_state", [P, 7, P + 1], F32, sub2)
            with ExitStack() as sub:
                mx_hi, mx_lo = (sb(n, [P, KT, S], F32R, sub) for n in ("mx_hi", "mx_lo"))
        with ExitStack() as room:
            ff_hi, ff_lo = (sb(n, [P, 16, S], F32R, room) for n in ("ff_hi", "ff_lo"))
            relu_f, sq_f = (sb(n, [P, 2, S], F32, room) for n in ("relu_f", "sq_f"))
        hg_state = yT[:, 0:4, :].rearrange("p a (b c) -> p (a b) c", c=P)
        z_k = yT[:, 4:5, :]
        tmpf = tmp.rearrange("p a s -> p (a s)")
        att_p, att_pt = tmpf[:, 0:1280], [tmpf[:, 1280:2560], tmpf[:, 2560:3840]]
        win_p, win_pt = tmpf[:, 2048:3072], [tmpf[:, 3072:4096], yT[:, 4:6, :].rearrange("p a s -> p (a s)")]
        row = [cosT[0:M_HEADS, :], tmp[0:M_HEADS, 5, :], sinT[0:M_HEADS, :], masks[0:M_HEADS, 0:2 * S].bitcast(F32)]
        mcol = mod[:, 0:80]
        z_qm = yT[:, 6:8, :]

        G = ctx.enter_context(nc.psum_tensor("G", [P, 4, 512], F32))
        X = ctx.enter_context(nc.psum_tensor("X", [P, 4, 512], F32))

        s_raw = [sem("raw_landed0"), sem("raw_landed1")]
        s_hi, s_lo = sem("w_hi_ready"), sem("w_lo_ready")
        s_inner, s_tile = sem("inner_chunk_used"), sem("tile_summed")
        s_free = {"act": sem("act_freed_tile"), "dve": sem("dve_freed_tile")}
        s_in, s_con, s_con2 = sem("inputs_landed"), sem("masks_landed"), sem("rope_tables_landed")
        s_ada, s_ada_first = [sem("ada_landed0"), sem("ada_landed1")], sem("first_ada_landed1")
        s_astep, s_asum, s_mod = sem("ada_product_added"), sem("ada_summed"), sem("mod_ready")
        s_dve, s_act = sem("dve_order"), sem("act_order")
        s_sq, s_sqd, s_std = sem("square_ready"), sem("square_summed"), sem("std_ready")
        s_diag, s_spread = sem("rstd_on_diagonal"), sem("rstd_spread")
        s_h, s_n, s_uhi, s_u = sem("h_tile_ready"), sem("normed_tile_ready"), sem("u_hi_ready"), sem("u_ready")
        s_silu, s_ff, s_fhi, s_fr = sem("silu_ready"), sem("hidden_ready"), sem("hidden_hi_ready"), sem("hidden_split")
        d2p, d2a = sem("dve_made_for_pe"), sem("dve_made_for_act")
        a2d, a2p = sem("act_made_for_dve"), sem("act_made_for_pe")
        p2d, p2a = sem("pe_made_for_dve"), sem("pe_made_for_act")
        hs = {k: sem("hgrn_" + k) for k in ("scores", "masked", "k_end", "k_end_transposed", "k_end_copied", "updates",
                                            "states", "output", "squares", "std", "normed", "transposed", "done")}
        ms = {k: sem("mlstm_" + k) for k in ("softplus", "rows", "rows_exp", "columns", "columns_copied", "k_transposed", "k_copied", "exponents", "weights_exp",
                                             "q_alone", "k_end", "scores", "decay", "weights", "q_decayed", "updates", "states",
                                             "output", "squares", "variance", "std", "normed", "transposed", "done")}
        ws = {k: sem("window_" + k) for k in ("squares", "q_sums", "k_sums", "q_std", "k_std", "rotated", "k_spread", "k_ready")}
        s_rope1, s_res, s_out = sem("first_rope_done"), sem("result_ready"), sem("result_written")

        c1 = lambda k: con1[:, where1[k][0]:where1[k][1]]
        ident, ones, half, freq, sign, q8 = (c1(k) for k in ("ident", "ones", "half", "freq", "sign", "q8"))
        mk = lambda k, lo, hi: masks[:, where3[k][0] + lo:where3[k][0] + hi].bitcast(BF16)
        identb = mk("identb", 0, P)
        rhs_a, rows_b = tmp[:, 0, 0:P], tmp[:, 0, P:2 * P]
        flat = lambda t: t.rearrange("p a s -> p (a s)")
        x_view = flat(yT[:, :, :]).rearrange("p (b n) -> p b n", b=TB)
        Xf = flat(X[:, :, :])
        out_view = X[:, 2:4, :].rearrange("p b (i c) -> p (b i) c", c=256)
        banks, banksf = (X, G), (Xf, flat(G[:, :, :]))
        LBC, HNG, MHN = 104, 112, 120
        NMIX, NFFN, QN, KN = 64, 80, 96, 98
        A1, C1, A2, C2 = 0, 8, 16, 24
        blk = lambda j: slice(j * P, (j + 1) * P)
        PASSES = ((0, 0), (0, 1), (1, 0))

        def att_blocks(t):
            i = t % TB
            return 2 * (i + 1) + (2 if i else 1)

        def rolled(name):
            g = plan[name]
            return g["chunks"] % 2 == 0 and name not in ("hg_out", "z0", "z1", "at_v") and name != order[-1]

        def m_bank(c):
            return (2, c // 2) if c % 2 else (c // 6, c // 2 % 3)

        def decay_heads(name, b):
            first = {"hg_f": -2, "hg_v": 2, "hg_g": 6}[name] + 2 * b
            return range(first, first + 2) if 0 <= first < HG_HEADS else ()

        def with_ada(name, b):
            return name != "hg_out" or b == 1

        def blocks(eng, name, loop=True):
            if rolled(name) and loop:
                with eng.Fori(0, plan[name]["blocks"]) as b:
                    yield b
            else:
                yield from range(plan[name]["blocks"])

        def slot_of(name, b, s):
            g = plan[name]
            return (s if rolled(name) else b * g["chunks"] + s) % 2

        def half_count(name, b, s, ahead):
            g = plan[name]
            if rolled(name):
                return b * (g["chunks"] // 2) + (g["c0"] + s + ahead) // 2
            return (g["c0"] + b * g["chunks"] + s + ahead) // 2

        def source(name, s, b, k0, k1):
            rows = lambda w: w.rearrange("(t p) n -> p t n", p=P)[:, k0:k1, :]
            one = lambda w, n=512, off=0: [(0, rows(w)[:, :, bass.ds(b * 512 + off, n)])]
            if name in ("hg_q", "hg_f", "hg_v", "hg_g"):
                return one(a["hgrn_w_in"][0], off=D * ("hg_q", "hg_f", "hg_v", "hg_g").index(name))
            if name == "hg_out":
                return one(a["hgrn_w_out"][0])
            if name == "at_out":
                return one(a["attn_w_out"][0])
            if name == "at_v":
                return [(0, rows(a["attn_w_in"][0])[:, :, (b // 2) * 3 * D + 2 * D + (b % 2) * 512:][:, :, 0:512])]
            if name.startswith("at_qk"):
                w, p = rows(a["attn_w_in"][0]), int(name[-1])
                return [(256 * i, w[:, :, bass.ds(b * 3 * D + (i * D + p * 256), 256)]) for i in range(2)]
            if name.startswith("ffn_in"):
                l, base = int(name[-2]), int(name[-1]) * FF1_TILES[0] * P
                w = rows(a["ffn_w_in"][l])
                return [(256 * i, w[:, :, bass.ds(b * 256 + (i * FF1 + base), 256)]) for i in range(2)]
            if name.startswith("ffn_out"):
                return one(a["ffn_w_out"][int(name[-2])])
            if name.startswith("zg"):
                return one(a["w_in_2"][int(name[-1])], off=Z["gate"])
            if name.startswith("z"):
                return one(a["w_in_2"][int(name[-1])], n=512 if b < 4 else 264)
            if name.startswith("br"):
                w = a["w_att_branch_2" if b < 2 else "w_m_branch_2"][int(name[-1])]
                return [(0, rows(w)[:, :, (b % 2) * 512:(b % 2) * 512 + 512])]
            if name.startswith("mo"):
                return one(a["w_out_2"][int(name[-1])])
            if name.startswith("ff_in"):
                return one(a["w_ff1_2"][int(name[-2])], off=int(name[-1]) * 2048)
            return one(a["w_ff2_2"][int(name[-2])])

        def first_row_tile(name):
            if name.startswith("ffn_out"):
                return int(name[-1]) * FF1_TILES[0]
            return int(name[-1]) * 16 if name.startswith("ff_out") else 0

        block = ctx.enter_context(nc.Block())

        @block.sync
        def _(sp):
            def chunk(name, s, b):
                g = plan[name]
                nk, k0 = min(4, g["ktiles"] - 4 * s), first_row_tile(name) + 4 * s
                slot = slot_of(name, b, s)
                if name.startswith(("at_qk", "ffn_in")):
                    for col, src in source(name, s, b, k0, k0 + nk):
                        sp.dma_start(raw[slot][:, 0:nk, col:col + 256], src).then_inc(s_raw[slot], 16)
                else:
                    for i in range(2):
                        (_, src), = source(name, s, b, k0 + i * nk // 2, k0 + (i + 1) * nk // 2)
                        sp.dma_start(raw[slot][:, i * nk // 2:(i + 1) * nk // 2, 0:src.shape[-1]],
                                     src).then_inc(s_raw[slot], 16)

            small = [(con1[:, :], a["con1"]),
                     (mask32[:, :], a["con2"][:, where2["mask32"][0]:where2["mask32"][1]]),
                     (rhs_a[0:96, :], a["ada_b"].rearrange("l (c p) -> (l c) p", p=P)),
                     (rhs_a[96:104, :], a["c"].rearrange("o (c p) -> (o c) p", p=P)),
                     (rhs_a[104:112, :], a["hgrn_lower_bounds"].rearrange("o (c p) -> (o c) p", p=P)),
                     (rhs_a[112:120, :], a["hgrn_norm_g"].rearrange("o (c p) -> (o c) p", p=P)),
                     (rhs_a[120:128, :], a["m_head_norm_2"].rearrange("o (c p) -> (o c) p", p=P)),
                     (rows_b[0:64, :], a["norm_g"].rearrange("l q (c p) -> (l q c) p", p=P)),
                     (rows_b[64:80, :], a["norm_mix_2"].rearrange("l (c p) -> (l c) p", p=P)),
                     (rows_b[80:96, :], a["norm_ffn_2"].rearrange("l (c p) -> (l c) p", p=P))]
            for r0, nm in ((QN, "att_q_norm_2"), (KN, "att_k_norm_2")):
                small += [(rows_b[r0:r0 + 2, 64 * i:64 * i + 64], a[nm]) for i in range(2)]
            small += [(sinks[:, :], a["att_sinks_2"].rearrange("l h -> (l h)").partition_broadcast(P))]
            for dst, src in small:
                sp.dma_start(dst, src).then_inc(s_in, 16)
            with nc.allow_non_contiguous_dma(reason="sixteen gate biases"):
                for l in range(2):
                    for i in range(2):
                        sp.dma_start(gbias[:, 2 * l + i:2 * l + i + 1],
                                     a["m_gate_bias_2"][l:l + 1, 4 * i:4 * i + 4].rearrange("o h -> h o")).then_inc(s_in, 16)
            sp.dma_start(x_view, a["x"][0].rearrange("(b p) n -> p b n", p=P)).then_inc(s_in, 16)
            for name in order:
                g = plan[name]
                if name == "at_v":
                    sp.wait_ge(s_mod, 2 * ADA_BLOCKS)
                    sp.dma_start(masks[:, :], a["masks"]).then_inc(s_con, 16)
                    sp.dma_start(sel4[:, :], a["con2"][:, where2["sel4"][0]:where2["sel4"][1]]).then_inc(s_con, 16)
                    sp.dma_start(flat(selk[:, :, :]), a["con2"][:, where2["selk"][0]:where2["selk"][1]]).then_inc(s_con, 16)
                    sp.dma_start(sinT[:, :].bitcast(I32), a["positions"][0].partition_broadcast(P)).then_inc(s_con, 16)
                if name in ("z0", "z1"):
                    if name == "z0":
                        sp.wait_ge(s_rope1, 1)
                    else:
                        sp.wait_ge(ms["decay"], M_HEADS)
                    sp.dma_start(cosT[:, :], a["con2"][:, where2["cos2"][0]:where2["cos2"][1]]).then_inc(s_con2, 16)
                    sp.dma_start(sinT[:, :], a["con2"][:, where2["sin2"][0]:where2["sin2"][1]]).then_inc(s_con2, 16)
                if name == order[0]:
                    for s in range(2):
                        chunk(name, s, 0)
                    w = a["ada_w"][0].rearrange("(s k p) n -> s p k n", p=P, k=4)
                    for b in range(ADA_FIRST):
                        if b:
                            sp.wait_ge(s_astep, 8 * b)
                        sp.dma_start(ada_raw[:, 1, :, :], w[1][:, :, 512 * b:512 * b + 512]).then_inc(s_ada_first, 16)
                    with sp.Fori(1, g["blocks"]) as b:
                        for s in range(2):
                            sp.wait_ge(s_lo, 2 * b + (s - 1))
                            chunk(name, s, b)
                    continue
                for b in blocks(sp, name):
                    for s in range(g["chunks"]):
                        sp.wait_ge(s_lo, b * g["chunks"] + (g["c0"] + s - 1))
                        chunk(name, s, b)
            sp.wait_ge(s_res, 8)
            sp.dma_start(out[0].rearrange("(b p) n -> p b n", p=P), x_view).then_inc(s_out, 16)
            sp.wait_ge(s_out, 16)

        @block.gpsimd
        def _(pool):
            for l in range(2):
                w = a["ada_w"][l].rearrange("(s k p) n -> s p k n", p=P, k=4)

                def load(b, slots=(0, 1)):
                    for s in slots:
                        if l or not isinstance(b, int) or b:
                            pool.wait_ge(s_astep, b * 8 + (8 * ADA_BLOCKS * l - 8 + 4 * (s + 1)))
                        pool.dma_start(ada_raw[:, s, :, :], w[s][:, :, bass.ds(b * 512, 512)]).then_inc(s_ada[s], 16)

                if l == 0:
                    for b in range(ADA_FIRST):
                        load(b, slots=(0,))
                with pool.Fori(0 if l else ADA_FIRST, ADA_BLOCKS) as b:
                    load(b)

        @block.scalar
        def _(act):
            n = Counts(act)
            sc = nc.scalar

            def split(name, b, s):
                g = plan[name]
                if isinstance(b, int) and g["c0"] + b * g["chunks"] + s + 2 >= n_chunks:
                    return
                slot = slot_of(name, b, s)
                act.wait_ge(s_raw[slot], half_count(name, b, s, 2) * 32 + 32)
                if s < g["chunks"] - 1:
                    act.wait_ge(s_inner, b * (g["chunks"] - 1) + (g["inner0"] + s + 1))
                else:
                    act.wait_ge(s_tile, b * 4 + (g["t0"] + 4))
                sc.copy(w_hi[slot][:, :, :], raw[slot][:, :, :]).then_inc(s_hi, 1)

            def linear(name, evict, after=None):
                g = plan[name]
                for b in blocks(act, name, loop=after is None):
                    for s in range(g["chunks"] - 1):
                        split(name, b, s)
                    evict(g, b)
                    split(name, b, g["chunks"] - 1)
                    if after:
                        after(b)

            def evicted(g, b, m, *instructions):
                act.wait_ge(s_tile, b * 4 + (g["t0"] + m + 1))
                for f in instructions[:-1]:
                    f()
                instructions[-1]().then_inc(s_free["act"], 1)

            def nothing(g, b):
                pass

            def squares(ready, src, ks, slots=2):
                for k in ks:
                    ready(k)
                    if k >= slots:
                        n.take(s_sqd)
                    n.give(sc.activation(tmp[:, k % slots, :], src[:, k, :], ACT.Square), s_sq)

            def deviation(slots):
                n.take(s_sqd, slots)
                n.give(sc.activation(rstd[:, 0, :], X[:, 0, 0:TB], ACT.Sqrt, bias=EPS, scale=1.0 / D), s_std)

            def norm(ready, src):
                squares(ready, src, range(KT))
                deviation(2)

            def norm_first_half(name, src):
                def f(b):
                    if b == 0:
                        sc.activation(rstd[:, 2, 0:1], ones[:, 0:1], ACT.Sqrt)
                        squares(freed_by_dve(name), src, range(4), slots=4)
                return f

            def norm_second_half(name, src):
                def f(g, b):
                    if b == 1:
                        squares(freed_by_dve(name), src, range(4, KT), slots=4)
                return f

            def to_u(scale, shift=None):
                for k in range(KT):
                    n.take(s_n)
                    if k >= 2:
                        n.take(s_u)
                    kw = dict(scale=scale(k), bias=0.0 if shift is None else shift(k))
                    sc.activation(tmp[:, 4 + k % 2, :], tmp[:, 2 + k % 2, :], ACT.Identity, **kw)
                    n.give(sc.activation(u_hi[:, k, :], tmp[:, 2 + k % 2, :], ACT.Identity, **kw), s_uhi)
                n.take(s_u, 2)

            def split_tiles(src, hi, s_done, ready=None):
                for k in range(KT):
                    if ready:
                        ready(k)
                    n.give(sc.copy(hi[:, k, :], src[:, k, :]), s_done)

            def freed_by_dve(name):
                g = plan[name]
                return lambda k: act.wait_ge(s_free["dve"], g["mine"] + k + 1)

            n.take(d2a)
            n.give(sc.activation(cond[:, :], cols_a[:, 96:104], ACT.Silu), a2d)
            n.give(sc.activation(lbc[:, 1, :], lbc[:, 0, :], ACT.Exp), a2d)
            for s in range(2):
                act.wait_ge(s_raw[s], 32)
                sc.copy(w_hi[s][:, :, :], raw[s][:, :, :]).then_inc(s_hi, 1)
            sc.sem_inc(s_free["act"], 4)

            def first_norm(l, q, ready, src):
                norm(ready, src)
                to_u(lambda k: mix[:, 32 * l + 16 * q + k:32 * l + 16 * q + k + 1],
                     lambda k: mod[:, 48 * l + 24 * q + k:48 * l + 24 * q + k + 1])

            def h_ready(k):
                n.take(s_h)

            def hgrn_sigmoids(name, b):
                for h in decay_heads(name, b):
                    if h == 0:
                        act.wait_ge(s_free["act"], plan["hg_f"]["mine"] + 8)
                    else:
                        n.take(d2a)
                    sc.activation(tmp[:, 0, :], hg_f[:, h, :], ACT.Sigmoid)
                    n.give(sc.activation(tmp[:, 1, :], hg_f[:, h, :], ACT.Sigmoid, scale=-1.0), a2d)

            def hgrn():
                for h in range(-1, HG_HEADS + 1):
                    if h + 1 < HG_HEADS:
                        n.take(hs["k_end_transposed"])
                        n.give(sc.copy(tmp[:, 1, :], G[:, 1, :]), hs["k_end_copied"])
                    if 0 <= h < HG_HEADS:
                        n.take(hs["output"])
                        for j in range(TB):
                            ins = sc.activation(tmp[:, 4, blk(j)], G[:, 2, blk(j)], ACT.Square, accum_out=stat[:, j:j + 1])
                        n.give(ins, hs["squares"])
                        n.own(hs["squares"])
                        n.give(sc.activation(rstd[:, 0, :], stat[:, 0:TB], ACT.Sqrt, bias=EPS, scale=1.0 / P), hs["std"])
                n.take(hs["done"], HG_HEADS)

            def attention(p):
                for t in range(-1, 9):
                    e = t + 1
                    if 0 <= t < 8:
                        n.take(p2a)
                        nb = att_blocks(t) * P
                        n.give(sc.copy(att_pt[t % 2][:, 0:nb], banksf[t % 2][:, 0:nb]), a2p)
                    if e < 8:
                        i, B = e % TB, banks[e % 2]
                        w, w0 = (i + 1) * P, 256 if i else P
                        n.take(d2a)
                        sc.activation(att_p[:, 0:2 * w].rearrange("p (a n) -> p a n", a=2), B[:, 0:2, 0:w], ACT.Exp,
                                      bias=stat[:, 2:3], scale=ATT_SCALE, accum_out=stat[:, 3:4])
                        n.give(sc.activation(att_p[:, 2 * w:2 * w + w0], B[:, 2, 0:w0], ACT.Exp,
                                             bias=stat[:, 2:3], scale=ATT_SCALE, accum_out=stat[:, 4:5]), a2d)
                    if t % TB == 0 and t > 0:
                        hh = t // TB - 1
                        n.take(p2a)
                        n.give(sc.copy(yT[:, 2 * p + hh, :], banks[hh][:, 3, :]), a2p)

            def window_keys(name, b):
                stage = (name[:-1], b)
                if stage == ("z", 1):
                    act.wait_ge(s_free["act"], plan[name]["mine"] + 8)
                    sc.activation(tmp[:, 0:4, :], z_q[:, :, :], ACT.Square)
                    n.give(sc.activation(tmp[:, 4, :], z_k[:, 0, :], ACT.Square), ws["squares"])
                elif stage == ("z", 2):
                    n.take(ws["q_sums"])
                    n.give(sc.activation(tmp[:, 0:4, :], X[:, :, :], ACT.Sqrt, bias=EPS, scale=1.0 / SW_DIM), ws["q_std"])
                elif stage == ("z", 3):
                    n.take(ws["k_sums"])
                    n.give(sc.activation(tmp[:, 4, :], X[:, 0, :], ACT.Sqrt, bias=EPS, scale=1.0 / SW_DIM), ws["k_std"])
                elif stage == ("zg", 0):
                    act.wait_ge(s_free["act"], plan[name]["mine"])
                    n.take(ws["k_spread"])
                    n.give(sc.copy(tmp[:, 0:4, :], X[:, :, :]), ws["k_ready"])

            def window_attention(l):
                for t in range(-1, 9):
                    h = t + 1
                    if 0 <= t < SW_HEADS:
                        n.take(p2a)
                        n.give(sc.copy(win_pt[t % 2][:, 0:7 * P], banksf[t % 2][:, 0:7 * P]), a2p)
                    if h < SW_HEADS:
                        sink = sinks[:, 8 * l + h:8 * l + h + 1]
                        n.take(d2a)
                        for i in range(TB):
                            sc.activation(win_p[:, 256 * i:256 * i + 256], banksf[h % 2][:, 256 * i:256 * i + 256], ACT.Exp,
                                          bias=stat[:, 8 + i:9 + i], scale=SW_DIM ** -0.5, accum_out=stat[:, 12 + i:13 + i])
                        n.give(sc.activation(stat[:, 16:20], stat[:, 8:12], ACT.Exp, bias=sink), a2d)
                    if t > 0 and t % 2 == 0:
                        n.take(p2a)
                        n.give(sc.copy(yT[:, t // 2 - 1, :], banks[(t // 2 - 1) % 2][:, 2, :]), a2p)

            def m_gates(b):
                if b == 0:
                    n.give(sc.activation(row[0], z_if[:, 1, :], ACT.Abs), s_act)
                    n.own(s_act)
                    n.give(sc.activation(row[0], row[0], ACT.Exp, scale=-1.0), s_act)
                    n.own(s_act)
                    n.give(sc.activation(row[0], row[0], ACT.Ln, bias=1.0), ms["softplus"])
                elif b == 2:
                    n.take(ms["rows"])
                    sc.activation(row[1], row[1], ACT.Exp)
                    sc.activation(row[0], row[0], ACT.Exp)
                    sc.activation(row[3], row[3], ACT.Exp, scale=-1.0)
                    n.give(sc.activation(srow[:, 6, :], srow[:, 5, :], ACT.Exp), ms["rows_exp"])

            def mlstm(l):
                for pr in range(2):
                    n.take(ms["k_transposed"])
                    n.give(sc.copy(tmp[:, (4, 6)[pr], :], X[:, 2 + pr, :]), ms["k_copied"])
                for h in range(-1, M_HEADS):
                    if h + 1 < M_HEADS:
                        n.take(ms["exponents"])
                        for j in range(TB):
                            ins = sc.activation(tmp[:, (0, 5)[(h + 1) % 2], blk(j)], X[:, 0, blk(j)], ACT.Exp,
                                                bias=mcol[:, 4 * j + h + 1:4 * j + h + 2])
                        n.give(ins, ms["weights_exp"])
                    if h >= 0:
                        n.take(ms["output"])
                        for j in range(TB):
                            ins = sc.activation(yT[:, 4 + h, blk(j)], out_view[:, j, 0:P], ACT.Square, accum_out=stat[:, 12 + j:13 + j])
                        n.give(ins, ms["squares"])
                        n.take(ms["variance"])
                        n.give(sc.activation(stat[:, 16:20], stat[:, 12:16], ACT.Sqrt), ms["std"])
                n.take(ms["done"], 4)

            first_norm(0, 0, h_ready, hT)

            for name in order:
                l = int(name[-2]) if name.startswith(("ffn", "ff_")) else 0
                if name == "hg_q":
                    linear(name, lambda g, b: [evicted(g, b, m, lambda: sc.activation(hg_q[:, b * 4 + m, :], G[:, m, :], ACT.Silu)) for m in range(4)])
                elif name == "hg_f":
                    linear(name, lambda g, b: [evicted(g, b, m, lambda: sc.copy(hg_f[:, b * 4 + m, :], G[:, m, :])) for m in range(4)],
                           after=lambda b: hgrn_sigmoids("hg_f", b))
                elif name == "hg_v":
                    linear(name, lambda g, b: [evicted(g, b, m, lambda: sc.copy(hg_v[:, m, bass.ds(b * 512, 512)], G[:, m, :])) for m in range(4)],
                           after=lambda b: hgrn_sigmoids("hg_v", b))
                elif name == "hg_g":
                    linear(name, lambda g, b: [evicted(g, b, m, lambda: sc.activation(hg_g[:, b * 4 + m, :], G[:, m, :], ACT.Silu)) for m in range(4)],
                           after=lambda b: hgrn_sigmoids("hg_g", b))
                    n.made(s_free["act"], plan["hg_g"]["mine"] + 8)
                    n.own(s_free["act"])
                    hgrn()
                    split_tiles(hg_g, u_hi, s_uhi)
                elif name == "hg_out":
                    linear(name, norm_second_half(name, yT), after=norm_first_half(name, yT))
                    deviation(4)
                    first_norm(0, 1, h_ready, hT)
                elif name.startswith("ffn_in"):
                    def gates(g, b):
                        for m in range(2):
                            act.wait_ge(s_tile, b * 4 + (g["t0"] + m + 1))
                            act.wait_ge(s_free["dve"], b * 4 + (g["mine"] - 1 + m))
                            sc.activation(silu_g[:, m, :], G[:, m, :], ACT.Silu).then_inc(s_silu, 1)
                        for m in range(2):
                            act.wait_ge(s_free["dve"], b * 4 + (g["mine"] + 3 + m))
                            sc.copy(hid_hi[:, b * 2 + m, :], hid_f[:, m, :]).then_inc(s_fhi, 1)
                    linear(name, gates)
                elif name.startswith("ffn_out"):
                    linear(name, norm_second_half(name, yT) if name[-1] == "1" else nothing,
                           after=norm_first_half(name, yT) if name[-1] == "1" else None)
                    if name[-1] == "1":
                        deviation(4)
                        if l == 0:
                            first_norm(1, 0, h_ready, hT)
                        else:
                            norm(h_ready, hT)
                            to_u(lambda k: cols_b[:, NMIX + k:NMIX + k + 1])
                elif name == "at_v":
                    linear(name, lambda g, b: [evicted(g, b, m, lambda: sc.copy(at_v[:, m, b * 512:b * 512 + 512], G[:, m, :])) for m in range(4)])
                    n.take(d2a)
                    n.give(sc.activation(sinT[:, :], tmp[:, 2, :], ACT.Sin), a2d)
                    n.give(sc.activation(tmp[:, 3, :], tmp[:, 2, :], ACT.Abs), s_act)
                    n.own(s_act)
                    n.give(sc.activation(cosT[:, :], tmp[:, 3, :], ACT.Sin, scale=-1.0, bias=float(np.pi / 2)), a2d)
                elif name.startswith("at_qk"):
                    linear(name, nothing)
                    attention(int(name[-1]))
                    if name[-1] == "3":
                        n.own(a2p)
                        split_tiles(yT, u_hi, s_uhi)
                elif name == "at_out":
                    linear(name, norm_second_half(name, yT), after=norm_first_half(name, yT))
                    deviation(4)
                    first_norm(1, 1, h_ready, hT)
                elif name.startswith("zg"):
                    linear(name, lambda g, b: [evicted(g, b, m, lambda: sc.activation(gate[:, b * 4 + m, :], G[:, m, :], ACT.Sigmoid)) for m in range(4)],
                           after=lambda b: [window_keys(name, b), m_gates(b)])
                    l = int(name[-1])
                    n.made(s_free["act"], plan[name]["mine"] + 16 - n.given.get(s_free["act"], 0))
                    n.own(s_free["act"])
                    window_attention(l)
                    mlstm(l)
                    n.own(s_act)
                    split_tiles(yT, u_hi, s_uhi)
                elif name.startswith("z"):
                    n.take(d2a)
                    zl = int(name[-1])

                    def z_evict(g, b):
                        if b == 0:
                            for m in range(4):
                                evicted(g, b, m, lambda: sc.copy(z_q[:, m, :], G[:, m, :]))
                        elif b == 1:
                            evicted(g, b, 0, lambda: sc.copy(z_k[:, 0, :], G[:, 0, :]))
                            v = G[:, 1, :].rearrange("p (j v d) -> p j v d", j=TB, v=2)
                            evicted(g, b, 1, lambda: sc.copy(vpad[:, :, :, 0, 0:64], v), lambda: sc.copy(vpad[:, :, :, 1, 64:128], v))
                            for m in (2, 3):
                                evicted(g, b, m, lambda: sc.copy(z_qm[:, m - 2, :], G[:, m, :]))
                        elif b == 2:
                            for m in range(4):
                                evicted(g, b, m, lambda: sc.copy(z_km[:, m, :], G[:, m, 0:256]),
                                        lambda: sc.copy(z_vm[:, m, 0:2, 0:P], G[:, m, 256:512].rearrange("p (h d) -> p h d", h=2)))
                        elif b == 3:
                            for m in range(2):
                                evicted(g, b, m, *[lambda j=j: sc.copy(z_vm[:, 2 * m + j, 2:4, 0:P],
                                                                       G[:, m, 256 * j:256 * j + 256].rearrange("p (h d) -> p h d", h=2))
                                                   for j in range(2)])
                            for m in (2, 3):
                                evicted(g, b, m, lambda: sc.activation(z_om[:, m - 2, :], G[:, m, :], ACT.Sigmoid))
                        else:
                            for m in range(2):
                                evicted(g, b, m, lambda: sc.activation(z_om[:, 2 + m, :], G[:, m, :], ACT.Sigmoid))
                            for m in (2, 3):
                                evicted(g, b, m, lambda: sc.activation(z_if[:, m - 2, :], G[0:4, m, :], ACT.Identity,
                                                                       bias=gbias[:, 2 * zl + m - 2:2 * zl + m - 1]))
                    linear(name, z_evict, after=lambda b: window_keys(name, b))
                elif name.startswith("br"):
                    def mixed_hi(g, b):
                        for k in range(4 * (b - 2), 4 * (b - 1)) if b >= 2 else ():
                            n.take(d2a)
                            n.give(sc.copy(mx_hi[:, k, :], gate[:, k, :]), s_uhi)
                    linear(name, mixed_hi)
                elif name.startswith("mo"):
                    linear(name, norm_second_half(name, hT), after=norm_first_half(name, hT))
                    l = int(name[-1])
                    deviation(4)
                    to_u(lambda k: cols_b[:, NFFN + 8 * l + k:NFFN + 8 * l + k + 1])
                elif name.startswith("ff_in"):
                    gff = n.at(s_ff)

                    def relu2(g, b):
                        def hi(m):
                            act.wait_ge(s_ff, b * 4 + (gff + 2 + m + 1))
                            sc.copy(ff_hi[:, b * 4 + m, :], sq_f[:, m % 2, :]).then_inc(s_fhi, 1)
                        for m in range(4):
                            act.wait_ge(s_ff, b * 4 + (gff + m + 1))
                            evicted(g, b, m, lambda: sc.activation(relu_f[:, m % 2, :], G[:, m, :], ACT.Relu))
                            if m >= 1:
                                hi(m - 1)
                        hi(3)
                    linear(name, relu2)
                    n.skip(s_ff, 16)
                elif name.startswith("ff_out"):
                    linear(name, norm_second_half(name, hT) if name == "ff_out01" else nothing,
                           after=norm_first_half(name, hT) if name == "ff_out01" else None)
                    if name == "ff_out01":
                        deviation(4)
                        to_u(lambda k: cols_b[:, NMIX + 8 + k:NMIX + 8 + k + 1])

        @block.vector
        def _(dve):
            n = Counts(dve)
            v = nc.vector
            tt, ts, stt = v.tensor_tensor, v.tensor_scalar, v.scalar_tensor_tensor

            def link(ins):
                n.give(ins, s_dve)
                n.own(s_dve)

            def split(name, b, s):
                g = plan[name]
                if isinstance(b, int) and g["c0"] + b * g["chunks"] + s + 2 >= n_chunks:
                    return
                slot = slot_of(name, b, s)
                dve.wait_ge(s_hi, b * g["chunks"] + (g["c0"] + s + 3))
                tt(w_lo[slot][:, :, :], raw[slot][:, :, :], w_hi[slot][:, :, :].bitcast(F32), ALU.subtract).then_inc(s_lo, 1)

            def linear(name, evict, ada=None, after=None, hold_last=False):
                g = plan[name]
                for b in blocks(dve, name, loop=after is None):
                    for s in range(g["chunks"] - 1):
                        split(name, b, s)
                    if ada is not None and with_ada(name, b):
                        ada_products(b + ada)
                    evict(g, b)
                    if ada is not None and with_ada(name, b):
                        ada_add(b + ada)
                    if not hold_last or b < g["blocks"] - 1:
                        split(name, b, g["chunks"] - 1)
                    if after is not None:
                        after(b)

            def evicted(g, b, m, f):
                dve.wait_ge(s_tile, b * 4 + (g["t0"] + m + 1))
                f().then_inc(s_free["dve"], 1)

            def nothing(g, b):
                pass

            def ada_products(i):
                for s in range(2):
                    if s == 0:
                        dve.wait_ge(s_ada[0], i * 16 + 16)
                    elif isinstance(i, int) and i < ADA_FIRST:
                        dve.wait_ge(s_ada_first, i * 16 + 16)
                    else:
                        dve.wait_ge(s_ada[1], i * 16 + (16 - 16 * ADA_FIRST))
                    for k in range(4):
                        c = cond[:, 4 * s + k:4 * s + k + 1]
                        if s == k == 0:
                            ins = ts(acc[:, :], ada_raw[:, 0, 0, :], c, None, ALU.mult)
                        else:
                            dve.wait_ge(s_astep, i * 8 + (4 * s + k))
                            ins = stt(acc[:, :], ada_raw[:, s, k, :], c, acc[:, :], ALU.mult, ALU.add)
                        ins.then_inc(s_astep, 1)

            def ada_add(i):
                dve.wait_ge(s_asum, i + 1)
                tt(mod[:, bass.ds(i * 4, 4)], X[:, 3, 0:4], cols_a[:, bass.ds(i * 4, 4)], ALU.add).then_inc(s_mod, 1)

            def norm_tail():
                n.take(s_std)
                link(v.reciprocal(rstd[:, 1, :], rstd[:, 0, :]))
                n.give(tt(tmp[:, 7, :].rearrange("p (j c) -> p j c", j=TB), ident.unsqueeze(1).broadcast_to([P, TB, P]),
                          rstd[:, 1, :].unsqueeze(2).broadcast_to([P, TB, P]), ALU.mult), s_diag)
                n.take(s_spread)

            def to_u(src):
                def lo(k):
                    n.take(s_uhi)
                    n.give(tt(u_lo[:, k, :], tmp[:, 4 + k % 2, :], u_hi[:, k, :].bitcast(F32), ALU.subtract), s_u)
                for k in range(KT):
                    n.give(tt(tmp[:, 2 + k % 2, :], src[:, k, :], X[:, 1, :], ALU.mult), s_n)
                    if k >= 1:
                        lo(k - 1)
                lo(KT - 1)

            def split_lo(src, hi, lo, s_done):
                for k in range(KT):
                    n.take(s_done)
                    n.give(tt(lo[:, k, :], src[:, k, :], hi[:, k, :].bitcast(F32), ALU.subtract), s_u)

            def add_to_h(l, q):
                norm_tail()
                n.give(tt(tmp[:, 2, :], yT[:, 0, :], X[:, 1, :], ALU.mult), s_dve)
                for k in range(KT):
                    if k + 1 < KT:
                        if k:
                            n.own(s_h)
                        n.give(tt(tmp[:, 2 + (k + 1) % 2, :], yT[:, k + 1, :], X[:, 1, :], ALU.mult), s_dve)
                        dve.wait_ge(s_dve, n.given[s_dve] - 1)
                    else:
                        n.own(s_dve)
                    c = mix[:, 32 * l + 16 * q + 8 + k:32 * l + 16 * q + 9 + k]
                    n.give(stt(hT[:, k, :], tmp[:, 2 + k % 2, :], c, hT[:, k, :], ALU.mult, ALU.add), s_h)

            def mixing(l, q):
                m0, c0, g0 = 48 * l + 24 * q, 32 * l + 16 * q, 32 * l + 16 * q
                stt(mix[:, c0:c0 + 8], mod[:, m0 + 8:m0 + 16], 1.0, cols_b[:, g0:g0 + 8], ALU.add, ALU.mult)
                return stt(mix[:, c0 + 8:c0 + 16], mod[:, m0 + 16:m0 + 24], 1.0, cols_b[:, g0 + 8:g0 + 16], ALU.add, ALU.mult)

            v.sem_inc(s_free["dve"], 4)
            v.sem_inc(s_ff, 2)
            v.sem_inc(s_fr, 2)
            n.take(p2d)
            v.tensor_copy(cols_a[:, :], X[:, 0, 0:P])
            link(v.tensor_copy(cols_b[:, 0:100], X[:, 1, 0:100]))
            n.give(tt(lbc[:, 0, :], cols_a[:, LBC:LBC + 8], cols_a[:, LBC:LBC + 8], ALU.subtract), d2a)
            n.take(a2d)
            ada_products(0)
            for k in range(KT):
                n.take(p2d)
                n.give(v.tensor_copy(hT[:, k, :], (G if k < 4 else X)[:, k % 4, :]), s_h)
            n.take(a2d)
            link(v.reciprocal(lbc[:, 2, :], lbc[:, 1, :]))
            link(tt(lbc[:, 1, :], lbc[:, 1, :], lbc[:, 2, :], ALU.mult))
            link(tt(lbc[:, 0, :], lbc[:, 1, :], lbc[:, 1, :], ALU.subtract))
            link(ts(lbc[:, 1, :], lbc[:, 0, :], -1.0, 1.0, ALU.mult, ALU.add))
            for s in range(2):
                dve.wait_ge(s_hi, s + 1)
                tt(w_lo[s][:, :, :], raw[s][:, :, :], w_hi[s][:, :, :].bitcast(F32), ALU.subtract).then_inc(s_lo, 1)
            ada_add(0)
            for i in range(1, ADA_FIRST):
                ada_products(i)
                if i == 1:
                    norm_tail()
                ada_add(i)
            dve.wait_ge(s_mod, ADA_FIRST)
            link(stt(mix[:, 0:8], mod[:, 8:16], 1.0, cols_b[:, 0:8], ALU.add, ALU.mult))
            to_u(hT)

            def hgrn_decays(name, b):
                F, K, F1, Dc, Di = (tmp[:, i, :] for i in (2, 1, 3, 4, 5))
                for h in decay_heads(name, b):
                    if h == 0:
                        link(v.memset(F1, 0.0))
                    n.take(a2d)
                    ts(F, tmp[:, 0, :], lbc[:, 1, h:h + 1], lbc[:, 0, h:h + 1], ALU.mult, ALU.add)
                    link(ts(K, K, lbc[:, 1, h:h + 1], None, ALU.mult))
                    link(v.tensor_copy(F1[:, ::HG_CHUNK], F[:, ::HG_CHUNK]))
                    link(v.memset(F[:, ::HG_CHUNK], 0.0))
                    link(v.tensor_tensor_scan(Dc, F, F1, 0.0, ALU.mult, ALU.add))
                    v.reciprocal(Di, Dc)
                    v.tensor_copy(decay[:, h, :], Dc[:, HG_CHUNK - 1::HG_CHUNK])
                    link(tt(hg_q[:, h, :], hg_q[:, h, :], Dc, ALU.mult))
                    link(tt(hg_f[:, h, :], K, Di, ALU.mult))
                    if h < HG_HEADS - 1:
                        v.sem_inc(d2a, 1)
                        n.made(d2a, 1)

            def hgrn():
                dve.wait_ge(s_free["act"], plan["hg_g"]["mine"] + 8)
                chunks = lambda t: t.rearrange("p (n c) -> p n c", c=HG_CHUNK)
                by4 = lambda t: t.rearrange("p (j c) -> p j c", j=TB)

                def k_end(h):
                    if h:
                        n.take(hs["k_end_transposed"])
                    n.give(tt(chunks(tmp[:, 0, :]), chunks(hg_f[:, h, :]),
                              decay[:, h, :].unsqueeze(2).broadcast_to([P, 16, HG_CHUNK]), ALU.mult), hs["k_end"])

                k_end(0)
                for h in range(-1, HG_HEADS + 1):
                    if 0 <= h < HG_HEADS:
                        n.take(hs["updates"])
                        link(v.tensor_copy(hg_state[:, 1, :], X[:, 0, 0:P]))
                        for c in range(1, 15):
                            ins = stt(hg_state[:, c + 1, :], hg_state[:, c, :], decay[:, h, c:c + 1],
                                      X[:, c % 4, blk(c // 4)], ALU.mult, ALU.add)
                            if c < 14:
                                link(ins)
                        n.give(ins, hs["states"])
                    if h + 1 < HG_HEADS:
                        n.take(hs["scores"])
                        n.give(tt(by4(tmp[:, 2 + (h + 1) % 2, :]), by4(G[:, 0, :]),
                                  mask32[:, :].unsqueeze(1).broadcast_to([P, TB, P]), ALU.mult), hs["masked"])
                    if h + 2 < HG_HEADS:
                        k_end(h + 2)
                    if h >= 1:
                        n.take(hs["transposed"])
                        n.give(stt(hg_g[:, h - 1, :], G[:, 3, :], cols_a[:, HNG + h - 1:HNG + h], hg_g[:, h - 1, :],
                                   ALU.mult, ALU.mult), hs["done"])
                    if 0 <= h < HG_HEADS:
                        n.take(hs["std"])
                        link(v.reciprocal(rstd[:, 1, :], rstd[:, 0, :]))
                        n.give(tt(by4(tmp[:, 5, :]), by4(G[:, 2, :]), rstd[:, 1, :].unsqueeze(2).broadcast_to([P, TB, P]), ALU.mult),
                               hs["normed"])
                n.own(hs["done"])
                split_lo(hg_g, u_hi, u_lo, s_uhi)

            def rope_tables():
                n.take(s_con, 64)
                two_pi = 2 * np.pi
                c_a = float(np.float32(6.28125))
                c_b = float((np.array([two_pi - c_a], np.float32).view(np.uint32) & np.uint32(0xFFFFF000)).view(np.float32)[0])
                c_c = float(np.float32(two_pi - c_a - c_b))
                magic = float(1.5 * 2 ** 23)
                link(v.tensor_copy(tmp[:, 0, :], sinT[:, :].bitcast(I32)))
                link(ts(tmp[:, 0, :], tmp[:, 0, :], freq, None, ALU.mult))
                link(ts(tmp[:, 1, :], tmp[:, 0, :], float(1 / two_pi), magic, ALU.mult, ALU.add))
                link(ts(tmp[:, 1, :], tmp[:, 1, :], -magic, None, ALU.add))
                for c in (c_a, c_b, c_c):
                    link(stt(tmp[:, 0, :], tmp[:, 1, :], -c, tmp[:, 0, :], ALU.mult, ALU.add))
                n.give(ts(tmp[:, 2, :], tmp[:, 0, :], 3.1415925, -3.1415925, ALU.min, ALU.max), d2a)
                n.take(a2d)
                link(ts(sinT[:, :], sinT[:, :], sign, None, ALU.mult))
                n.take(a2d)

            def rope(x, rot, mask, parts, tiles):
                wide = lambda t: t[0:parts, :].unsqueeze(1).broadcast_to([parts, tiles, S])
                link(v.stream_shuffle(rot, x, mask))
                tt(rot, rot, wide(sinT), ALU.mult)
                link(tt(x, x, wide(cosT), ALU.mult))
                return tt(x, x, rot, ALU.add)

            def attention(name, second_head):
                v.sem_inc(d2p, 1)
                n.made(d2p, 1)
                for t in range(8):
                    i, B = t % TB, banks[t % 2]
                    w, w0 = (i + 1) * P, 256 if i else P
                    n.take(p2d)
                    v.tensor_reduce(stat[:, 0:1], B[:, 0:2, 0:w], mybir.AxisListType.XY, ALU.max)
                    link(v.tensor_reduce(stat[:, 1:2], B[:, 2, 0:w0], AX, ALU.max))
                    n.give(ts(stat[:, 2:3], stat[:, 0:1], stat[:, 1:2], -ATT_SCALE, ALU.max, ALU.mult), d2a)
                    n.take(a2d)
                    link(tt(stat[:, 5:6], stat[:, 3:4], stat[:, 4:5], ALU.add))
                    link(v.reciprocal(stat[:, 6:7], stat[:, 5:6]))
                    n.give(ts(att_p[:, 0:2 * w + w0], att_p[:, 0:2 * w + w0], stat[:, 6:7], None, ALU.mult), d2p)
                    if t < 3:
                        next(second_head)
                    if t == 2:
                        n.own(s_dve)
                        v.sem_inc(d2p, 1)
                        n.made(d2p, 1)
                    if t == 4:
                        split(name, 2, 1)

            def window_keys(name, b):
                swap = [i + 8 if i < 8 else i - 8 if i < 16 else i for i in range(32)]
                stage, l = (name[:-1], b), int(name[-1])
                if stage == ("z", 2):
                    n.take(ws["q_std"])
                    link(v.reciprocal(tmp[:, 0:4, :], tmp[:, 0:4, :]))
                elif stage == ("z", 3):
                    n.take(s_con2, 32)
                    for t in range(4):
                        ins = stt(z_q[:, t, :], z_q[:, t, :], cols_b[:, QN + l:QN + l + 1], tmp[:, t, :], ALU.mult, ALU.mult)
                    link(ins)
                    link(rope(z_q[:, :, :], tmp[:, 0:4, :], swap, P, 4))
                elif stage == ("z", 4):
                    n.take(ws["k_std"])
                    ra = tmp[:, 4:5, :]
                    link(v.reciprocal(ra, ra))
                    link(stt(z_k[:, 0, :], z_k[:, 0, :], cols_b[:, KN + l:KN + l + 1], tmp[:, 4, :], ALU.mult, ALU.mult))
                    n.give(rope(z_k[:, 0:1, :], ra, swap, P, 1), ws["rotated"])

            def window_attention(l):
                Pb = win_p.rearrange("p (i k) -> p i k", i=TB)
                for h in range(SW_HEADS):
                    sink = sinks[:, 8 * l + h:8 * l + h + 1]
                    n.take(p2d)
                    link(v.tensor_reduce(stat[:, 0:4], banksf[h % 2][:, 0:1024].rearrange("p (i k) -> p i k", i=TB), AX, ALU.max))
                    link(ts(stat[:, 4:8], stat[:, 0:4], SW_DIM ** -0.5, sink, ALU.mult, ALU.max))
                    n.give(ts(stat[:, 8:12], stat[:, 4:8], -1.0, None, ALU.mult), d2a)
                    n.take(a2d)
                    link(tt(stat[:, 20:24], stat[:, 12:16], stat[:, 16:20], ALU.add))
                    link(v.reciprocal(stat[:, 8:12], stat[:, 20:24]))
                    n.give(tt(Pb, Pb, stat[:, 8:12].unsqueeze(2).broadcast_to([P, TB, 256]), ALU.mult), d2p)

            def m_gates():
                R = row
                gi, gf = z_if[:, 0, :], z_if[:, 1, :]
                ch = lambda t: t.rearrange("p (n c) -> p n c", c=M_CHUNK)
                wide = lambda t: t.unsqueeze(2).broadcast_to([M_HEADS, 8, M_CHUNK])
                n.take(ms["softplus"])
                link(ts(R[1], gf, 0.0, None, ALU.min))
                v.memset(R[3], 1.0)
                link(tt(gf, R[1], R[0], ALU.subtract))
                link(v.memset(R[3][:, ::M_CHUNK], 0.0))
                link(v.tensor_tensor_scan(R[0], R[3], gf, 0.0, ALU.mult, ALU.add))
                g = srow[:, 0, :]
                v.tensor_copy(g, R[0][:, M_CHUNK - 1::M_CHUNK])
                link(tt(gi, gi, R[0], ALU.subtract))
                link(tt(ch(R[1]), ch(gi), wide(g), ALU.add))
                link(v.tensor_reduce(srow[:, 1, :], ch(R[1]), AX, ALU.max))
                v.memset(srow[:, 3, 0:1], 0.0)
                link(v.tensor_tensor_scan(srow[:, 2, :], g, srow[:, 1, :], 0.0, ALU.add, ALU.max))
                link(v.tensor_copy(srow[:, 3, 1:8], srow[:, 2, 0:7]))
                tt(ch(R[1]), ch(R[1]), wide(srow[:, 2, :]), ALU.subtract)
                tt(srow[:, 4, :], g, srow[:, 3, :], ALU.add)
                v.tensor_copy(R[2], gi)
                link(v.memset(R[3], 0.0))
                tt(srow[:, 5, :], srow[:, 4, :], srow[:, 2, :], ALU.subtract)
                v.memset(R[3][:, ::M_CHUNK], -3.0e38)
                link(tt(R[2][:, ::M_CHUNK], gi[:, ::M_CHUNK], srow[:, 3, :], ALU.max))
                link(v.tensor_tensor_scan(gf, R[3], R[2], 0.0, ALU.add, ALU.max))
                ts(R[2], gf, -1.0, None, ALU.mult)
                link(tt(R[3], R[0], gf, ALU.add))
                n.give(tt(ch(R[0]), wide(srow[:, 3, :]), ch(gf), ALU.subtract), ms["rows"])

            def columns():
                n.take(ms["columns"])
                n.give(v.tensor_copy(mcol[:, :], X[:, 0, 0:80]), ms["columns_copied"])

            def mlstm(l):
                n.own(ms["columns_copied"])

                def q_alone(h):
                    n.give(ts(tmp[:, 1, :], z_qm[:, h // 2, :], q8[:, h % 2:h % 2 + 1], None, ALU.mult), ms["q_alone"])

                def k_end(h):
                    pr = h // 2
                    for j in range(TB):
                        ins = ts(tmp[:, 3, blk(j)], z_km[:, j, pr * P:(pr + 1) * P], mcol[:, 16 + 4 * j + h:17 + 4 * j + h], None, ALU.mult)
                    n.give(ins, ms["k_end"])

                q_alone(0)
                k_end(0)
                for h in range(-1, M_HEADS + 1):
                    if 0 <= h < M_HEADS:
                        n.take(ms["updates"])
                        link(v.tensor_copy(m_state[:, 0, :], G[:, 0, 0:P + 1]))
                        for c in range(1, 7):
                            bank, i = m_bank(c)
                            ins = stt(m_state[:, c, :], m_state[:, c - 1, :], mcol[:, 32 + 8 * h + c:33 + 8 * h + c],
                                      G[:, bank, (P + 1) * i:(P + 1) * (i + 1)], ALU.mult, ALU.add)
                            if c < 6:
                                link(ins)
                        n.give(ins, ms["states"])
                        if h + 1 < M_HEADS:
                            k_end(h + 1)
                    if h >= 1:
                        n.take(ms["transposed"])
                        n.give(stt(yT[:, 3 + h, :], G[:, 3, :], cols_a[:, MHN + 4 * l + h - 1:MHN + 4 * l + h], z_om[:, h - 1, :],
                                   ALU.mult, ALU.mult), ms["done"])
                    if h + 1 < M_HEADS:
                        W, qs = tmp[:, (0, 5)[(h + 1) % 2], :], tmp[:, (2, 7)[(h + 1) % 2], :]
                        n.take(ms["weights_exp"])
                        n.take(ms["scores"])
                        n.give(tt(W, W, X[:, 1, :], ALU.mult), ms["weights"])
                        n.take(ms["decay"])
                        n.own(ms["q_alone"])
                        n.give(tt(qs, tmp[:, 1, :], G[:, 3, :], ALU.mult), ms["q_decayed"])
                        if h + 2 < M_HEADS:
                            n.own(ms["q_decayed"])
                            q_alone(h + 2)
                    if 0 <= h < M_HEADS:
                        n.take(ms["squares"])
                        den = out_view[:, :, P:P + 1].rearrange("p j o -> p (j o)")
                        link(ts(stat[:, 0:4], den, -1.0, None, ALU.mult))
                        link(tt(stat[:, 4:8], den, stat[:, 0:4], ALU.max))
                        link(tt(stat[:, 4:8], stat[:, 4:8], mcol[:, 64 + h:80:4], ALU.max))
                        link(stt(stat[:, 8:12], stat[:, 4:8], EPS, stat[:, 4:8], ALU.mult, ALU.mult))
                        n.give(stt(stat[:, 12:16], stat[:, 12:16], 1.0 / P, stat[:, 8:12], ALU.mult, ALU.add), ms["variance"])
                        n.take(ms["std"])
                        link(v.reciprocal(stat[:, 20:24], stat[:, 16:20]))
                        n.give(tt(yT[:, 4 + h, :].rearrange("p (j c) -> p j c", j=TB), out_view[:, :, 0:P],
                                  stat[:, 20:24].unsqueeze(2).broadcast_to([P, TB, P]), ALU.mult), ms["normed"])
                n.own(ms["done"])
                split_lo(yT, u_hi, u_lo, s_uhi)

            def copy_out(g, b):
                for m in range(4):
                    evicted(g, b, m, lambda: v.tensor_copy(yT[:, b * 4 + m, :], G[:, m, :]))

            def add_out(dst):
                def f(g, b):
                    for m in range(4):
                        evicted(g, b, m, lambda: tt(dst[:, b * 4 + m, :], dst[:, b * 4 + m, :], G[:, m, :], ALU.add))
                return f

            for name in order:
                if name in ("hg_q", "hg_f", "hg_v", "hg_g"):
                    linear(name, nothing, ada=ADA_FIRST + 2 * ("hg_q", "hg_f", "hg_v", "hg_g").index(name),
                           after=None if name == "hg_q" else lambda b: hgrn_decays(name, b))
                    if name == "hg_g":
                        hgrn()
                elif name == "hg_out":
                    linear(name, copy_out, ada=ADA_FIRST + 7)
                    dve.wait_ge(s_mod, ADA_BLOCKS)
                    mixing(0, 0)
                    link(mixing(0, 1))
                    add_to_h(0, 0)
                    norm_tail()
                    to_u(hT)
                elif name.startswith("ffn_in"):
                    l, hf = int(name[-2]), int(name[-1])
                    fr, fhi, silu = n.at("fr"), n.at("fhi"), n.at("silu")

                    def product(g, b):
                        for m in range(2):
                            dve.wait_ge(s_silu, b * 2 + (silu + m + 1))
                            v.sem_inc(s_free["dve"], 1)
                        for m in range(2):
                            dve.wait_ge(s_fr, b * 2 + (fr + 2))
                            evicted(g, b, 2 + m, lambda: tt(hid_f[:, m, :], silu_g[:, m, :], G[:, 2 + m, :], ALU.mult))
                        for m in range(2):
                            dve.wait_ge(s_fhi, b * 2 + (fhi + m + 1))
                            dve.wait_ge(s_free["dve"], b * 4 + (g["mine"] + 3 + m))
                            tt(hid_lo[:, b * 2 + m, :], hid_f[:, m, :], hid_hi[:, b * 2 + m, :].bitcast(F32), ALU.subtract).then_inc(s_fr, 1)
                    linear(name, product, ada=(ADA_FIRST + 9 + 6 * hf) if l == 0 else None)
                    for q in ("fr", "fhi", "silu"):
                        n.skip(q, 2 * plan[name]["blocks"])
                elif name.startswith("ffn_out"):
                    l, hf = int(name[-2]), int(name[-1])
                    if hf == 0:
                        linear(name, copy_out)
                    else:
                        linear(name, add_out(yT))
                        if l == 0:
                            dve.wait_ge(s_mod, 24)
                            mixing(1, 0)
                            link(mixing(1, 1))
                        add_to_h(l, 1)
                        norm_tail()
                        to_u(hT)
                elif name == "at_v":
                    linear(name, nothing)
                    rope_tables()
                elif name.startswith("at_qk"):
                    pair = int(name[-1])

                    def qk(g, b):
                        for m in range(4):
                            evicted(g, b, m, lambda: v.tensor_copy(at_qk[:, b, m, :], G[:, m, :]))

                    def rotate(b, heads=slice(None), room=tmp[0:32, 0:4, :]):
                        swap = [(i + 16) % 32 for i in range(32)]
                        pick = lambda t: t.rearrange("p (w h) s -> p w h s", h=2)[:, :, heads, :]
                        x, rot = pick(at_qk[0:32, b, :, :]), room.rearrange("p (w h) s -> p w h s", w=2)
                        rot = rot[:, :, 0:x.shape[2], :]
                        wide = lambda t: t[0:32, :].unsqueeze(1).unsqueeze(1).broadcast_to(list(x.shape))
                        dve.wait_ge(s_free["dve"], b * 4 + (plan[name]["mine"] + 4))
                        if n.given.get(s_dve):
                            n.own(s_dve)
                        link(v.stream_shuffle(rot, x, swap))
                        yield
                        tt(rot, rot, wide(sinT), ALU.mult)
                        link(tt(x, x, wide(cosT), ALU.mult))
                        yield
                        n.give(tt(x, x, rot, ALU.add), s_dve)
                        yield

                    def rotate_group(b):
                        for _ in rotate(b, slice(None) if b < 2 else slice(0, 1)):
                            pass
                    linear(name, qk, after=rotate_group, hold_last=True)
                    n.own(s_dve)
                    attention(name, rotate(2, slice(1, 2), room=yT[0:32, 2 * pair:2 * pair + 2, :]))
                    if name[-1] == "3":
                        v.sem_inc(s_rope1, 1)
                        split_lo(yT, u_hi, u_lo, s_uhi)
                elif name == "at_out":
                    linear(name, copy_out)
                    add_to_h(1, 0)
                    norm_tail()
                    to_u(hT)
                elif name.startswith("zg"):
                    linear(name, nothing, after=lambda b: m_gates() if b == 0 else columns() if b == 3 else None)
                    window_attention(int(name[-1]))
                    mlstm(int(name[-1]))
                elif name.startswith("z"):
                    v.memset(z_vm[:, :, :, P:P + 1], 1.0)
                    n.give(v.memset(vpad[:, :, :, :, :].rearrange("p a b c d -> p (a b c d)"), 0.0), d2a)
                    linear(name, nothing, after=lambda b: window_keys(name, b))
                elif name.startswith("br"):
                    def branch(g, b):
                        for m in range(4):
                            t = b * 4 + m
                            evicted(g, b, m, lambda: tt(gate[:, t, :], gate[:, t, :], G[:, m, :], ALU.mult))
                        if b < 2:
                            return
                        ks = range(4 * (b - 2), 4 * (b - 1))
                        for k in ks:
                            dve.wait_ge(s_free["dve"], g["mine"] + 8 + k + 1)
                            n.give(tt(gate[:, k, :], gate[:, k, :], gate[:, 8 + k, :], ALU.add), d2a)
                        for k in ks:
                            n.take(s_uhi)
                            n.give(tt(mx_lo[:, k, :], gate[:, k, :], mx_hi[:, k, :].bitcast(F32), ALU.subtract), s_u)
                    linear(name, branch)
                elif name.startswith("mo"):
                    linear(name, add_out(hT))
                    norm_tail()
                    to_u(hT)
                elif name.startswith("ff_in"):
                    fr, fhi = n.at("fr"), n.at("fhi")
                    gff = n.at("ff")

                    def square(g, b):
                        def lo(m):
                            dve.wait_ge(s_fhi, b * 4 + (fhi + m + 1))
                            tt(ff_lo[:, b * 4 + m, :], sq_f[:, m % 2, :], ff_hi[:, b * 4 + m, :].bitcast(F32), ALU.subtract).then_inc(s_fr, 1)
                        for m in range(4):
                            dve.wait_ge(s_free["act"], b * 4 + (g["mine"] + m + 1))
                            dve.wait_ge(s_fr, b * 4 + (fr + 2 + m - 1))
                            tt(sq_f[:, m % 2, :], relu_f[:, m % 2, :], relu_f[:, m % 2, :], ALU.mult).then_inc(s_ff, 1)
                            if m >= 1:
                                lo(m - 1)
                        lo(3)
                    linear(name, square)
                    n.skip("fr", 16)
                    n.skip("fhi", 16)
                elif name.startswith("ff_out"):
                    linear(name, add_out(hT))
                    if name == "ff_out01":
                        norm_tail()
                        to_u(hT)
            for q in range(8):
                n.take(p2d)
                v.tensor_copy(x_view[:, q // 2, (q % 2) * 512:(q % 2) * 512 + 512], (G if q < 4 else X)[:, q % 4, :]).then_inc(s_res, 1)

        @block.tensor
        def _(pe):
            n = Counts(pe)
            mm, tr = nc.tensor.matmul, nc.tensor.transpose

            def linear(name, x_hi, x_lo, tiles=None, ada=None, x0=lambda b: 0, after=None, mid=None):
                g = plan[name]
                other = "dve" if g["evictor"] == "act" else "act"
                pe.wait_ge(s_free[other], g["other"])
                for b in blocks(pe, name, loop=after is None and mid is None):
                    for s in range(g["chunks"]):
                        slot = slot_of(name, b, s)
                        pe.wait_ge(s_lo, b * g["chunks"] + (g["c0"] + s + 1))
                        nk = min(4, g["ktiles"] - 4 * s)
                        w, xs = (w_hi[slot], w_lo[slot]), (x_hi, x_lo)
                        for m in range(4):
                            if s == 0:
                                pe.wait_ge(s_free[g["evictor"]], b * 4 + (g["mine"] + m - 3))
                            spec = tiles(b, m) if tiles else None
                            last_k = g["ktiles"] - 1
                            for part in (spec if isinstance(spec, list) else [None]):
                                for k in range(nk):
                                    kk = 4 * s + k
                                    if m == 0 and name in operand and part in (None, (spec or [0])[0]):
                                        split_done, base = operand[name]
                                        pe.wait_ge(split_done, base + x0(b) + kk + 1)
                                    for iw, ix in PASSES:
                                        first = kk == 0 and (iw, ix) == (0, 0) and (part is None or part is spec[0])
                                        last = kk == last_k and (iw, ix) == (1, 0)
                                        if part is None:
                                            c0, c1_ = spec or (m * P, m * P + P)
                                            ins = mm(G[0:c1_ - c0, m, :], w[iw][:, k, c0:c1_], xs[ix][:, x0(b) + kk, :],
                                                     start=first, stop=last, skip_group_check=True)
                                        else:
                                            tok, (c0, c1_), (o0, o1) = part
                                            ins = mm(G[:, m, o0:o1], xs[ix][:, kk, blk(tok)], w[iw][:, k, c0:c1_],
                                                     start=first, stop=last, skip_group_check=True)
                            if s == g["chunks"] - 1:
                                ins.then_inc(s_tile, 1)
                            elif m == 3:
                                ins.then_inc(s_inner, 1)
                        if mid is not None:
                            mid(b, s)
                    if ada is not None and with_ada(name, b):
                        ada_sum(b + ada)
                    if after is not None:
                        after(b)

            def ada_sum(i):
                pe.wait_ge(s_astep, i * 8 + 8)
                if not isinstance(i, int) or i > 0:
                    pe.wait_ge(s_mod, i)
                for q in range(4):
                    ins = mm(X[:, 3, q:q + 1], acc[:, blk(q)], ones[:, 0:1], start=True, stop=True, skip_group_check=True)
                ins.then_inc(s_asum, 1)

            def square_sums(ks, slots):
                for k in ks:
                    n.take(s_sq)
                    for j in range(TB):
                        ins = mm(X[:, 0, j:j + 1], tmp[:, k % slots, blk(j)], ones[:, 0:1],
                                 start=k == 0 and j == 0, stop=k == KT - 1, skip_group_check=True)
                    n.give(ins, s_sqd)

            def spread():
                n.take(s_diag)
                n.give(mm(X[:, 1, :], ones, tmp[:, 7, :], start=True, stop=True), s_spread)

            def norm():
                square_sums(range(KT), 2)
                spread()

            def norm_first_half(b, s):
                if b == 1 and s == 0:
                    square_sums(range(4), 4)

            def norm_second_half():
                square_sums(range(4, KT), 4)
                spread()

            def transposes(out_bank, src, count, sem_, dst0=0):
                for j in range(count):
                    ins = tr(out_bank[:, blk(dst0 + j)], src(j), ident)
                if sem_ is not None:
                    n.give(ins, sem_)
                return ins

            n.take(s_in, 16 * 20)
            tr(X[:, 0, 0:P], rhs_a, ident)
            n.give(tr(X[:, 1, 0:100], rows_b[0:100, :], ident[0:100, 0:100]), p2d)
            for k in range(KT):
                if k == 4:
                    n.take(s_h, 1)
                transposes((G if k < 4 else X)[:, k % 4, :], lambda j: x_view[:, j, blk(k)], TB, p2d)
            n.take(s_h, 7)
            ada_sum(0)
            norm()
            for i in range(1, ADA_FIRST):
                ada_sum(i)

            def hgrn():
                pe.wait_ge(s_free["act"], plan["hg_g"]["mine"] + 8)
                for h in range(-1, HG_HEADS + 1):
                    if 0 <= h < HG_HEADS:
                        n.take(hs["k_end_copied"])
                        for c in range(15):
                            r = slice(32 * (c % 4), 32 * (c % 4) + 32)
                            ins = mm(X[:, c % 4, blk(c // 4)], tmp[r, 1, blk(c // 4)], hg_v[r, c // 4, blk(h)],
                                     start=True, stop=True, skip_group_check=True)
                        n.give(ins, hs["updates"])
                    if h >= 1:
                        n.take(hs["normed"])
                        if h >= 2:
                            n.take(hs["done"])
                        transposes(G[:, 3, :], lambda j: tmp[:, 5, blk(j)], TB, hs["transposed"])
                    if h + 1 < HG_HEADS:
                        if h >= 0:
                            n.take(hs["masked"])
                        for j in range(TB):
                            ins = mm(G[:, 0, blk(j)], hg_f[:, h + 1, blk(j)], hg_q[:, h + 1, blk(j)], start=True, stop=True, skip_group_check=True)
                        n.give(ins, hs["scores"])
                        n.take(hs["k_end"])
                        transposes(G[:, 1, :], lambda j: tmp[:, 0, blk(j)], TB, hs["k_end_transposed"])
                    if 0 <= h < HG_HEADS:
                        n.take(hs["states"])
                        if h == HG_HEADS - 1:
                            n.take(hs["masked"])
                        for j in range(TB):
                            mm(G[:, 2, blk(j)], tmp[:, 2 + h % 2, blk(j)], hg_v[:, j, blk(h)], start=j == 0, stop=False, skip_group_check=True)
                        for c in range(1, 16):
                            r = slice(32 * (c % 4), 32 * (c % 4) + 32)
                            ins = mm(G[r, 2, blk(c // 4)], hg_q[:, h, 32 * c:32 * c + 32], hg_state[:, c, :],
                                     start=False, stop=c == 15, skip_group_check=True, tile_position=(0, 32 * (c % 4)))
                        n.give(ins, hs["output"])
                n.take(hs["done"])

            def attention(p):
                n.take(d2p)
                for t in range(-1, 9):
                    if t >= 1:
                        n.take(a2p)
                    if t == TB + 2:
                        n.take(a2p)
                    if t + 1 == TB:
                        n.take(d2p)
                    if t + 1 < 8:
                        hh, i = divmod(t + 1, TB)
                        w, w0 = (i + 1) * P, 256 if i else P
                        for bank, (g, lo, hi) in enumerate(((1, 512 - w, 512), (2, 1024 - w, 1024), (0, 1280 - w0, 1280))):
                            o = banks[(t + 1) % 2][:, bank, 0:hi - lo]
                            mm(o, identb, mk("dil", lo, hi), start=True, stop=False)
                            ins = mm(o, at_qk[:, g, hh, blk(i)], at_qk[:, g, 2 + hh, (i + 1) * P - (hi - lo):(i + 1) * P],
                                     start=False, stop=True)
                        n.give(ins, p2d)
                    if 0 <= t < 8:
                        n.take(d2p)
                        transposes(banksf[t % 2], lambda j: att_p[:, blk(j)], att_blocks(t), p2a)
                    if t >= 1:
                        hh, i = divmod(t - 1, TB)
                        h = 2 * p + hh
                        where = [(1, j) for j in range(i + 1)] + [(2, j) for j in range(i + 1)] + [(0, j) for j in range(max(i - 1, 0), i + 1)]
                        for c, (g, j) in enumerate(where):
                            ins = mm(banks[hh][:, 3, blk(i)], at_v[:, j, g * D + h * P:g * D + (h + 1) * P], att_pt[(t - 1) % 2][:, blk(c)],
                                     start=i == 0 and c == 0, stop=c == len(where) - 1, skip_group_check=True)
                        if i == TB - 1:
                            n.give(ins, p2a)
                n.take(a2p)

            def window_keys(name, b):
                stage = (name[:-1], b)
                if stage == ("z", 2):
                    n.take(ws["squares"])
                    for t in range(4):
                        ins = mm(X[:, t, :], half, tmp[:, t, :], start=True, stop=True)
                    n.give(ins, ws["q_sums"])
                elif stage == ("z", 3):
                    n.take(ws["q_std"])
                    n.give(mm(X[:, 0, :], half, tmp[:, 4, :], start=True, stop=True), ws["k_sums"])
                elif stage == ("zg", 0):
                    n.take(ws["k_std"])
                    n.take(ws["rotated"])
                    for t in range(4):
                        ins = mm(X[:, t, :], selk[:, t, :], z_k[:, 0, :], start=True, stop=True)
                    n.give(ins, ws["k_spread"])

            def window_attention(l):
                n.take(ms["columns_copied"])
                pe.wait_ge(s_free["act"], plan[f"zg{l}"]["mine"] + 16)
                for step in range(-1, 9):
                    if step >= 1:
                        n.take(a2p)
                    if step >= 4 and step % 2 == 0:
                        n.take(a2p)
                    h = step + 1
                    if h < SW_HEADS:
                        t, hf, kv = h // 2, h % 2, h // 4
                        kp = tmp[:, 2 * kv + hf, :]
                        B = banks[h % 2]
                        for bank in range(2):
                            mm(B[:, bank, :], identb, mk("sw", 512 * bank, 512 * bank + 512), start=True, stop=False, skip_group_check=True)
                        for i in range(TB):
                            c0 = 256 * (i % 2)
                            lo = (i - 1) * P if i else 0
                            o = B[:, i // 2, c0 + (0 if i else P):c0 + 256]
                            ins = mm(o, z_q[:, t, blk(i)], kp[:, lo:(i + 1) * P], start=False, stop=True, skip_group_check=True)
                        n.give(ins, p2d)
                    if 0 <= step < SW_HEADS:
                        n.take(d2p)
                        transposes(banksf[step % 2], lambda j: win_p[:, blk(j + 1)], 7, p2a)
                    if step >= 1:
                        h = step - 1
                        t, hf, kv = h // 2, h % 2, h // 4
                        for j in range(7):
                            i, cur = (j + 1) // 2, (j + 1) % 2
                            ins = mm(banks[t % 2][:, 2, blk(i)], vpad[:, i if cur else i - 1, kv, hf, :], win_pt[h % 2][:, blk(j)],
                                     start=hf == 0 and j == 0, stop=hf == 1, skip_group_check=True)
                        if hf:
                            n.give(ins, p2a)
                n.take(a2p)

            def gate_columns():
                n.take(ws["k_ready"])
                gi = z_if[:, 0, :]
                n.take(ms["rows_exp"])
                for j in range(TB):
                    mm(X[:, 0, 4 * j:4 * j + 4], gi[:, blk(j)], ident[0:4, 0:4], start=j == 0, stop=True, skip_group_check=True)
                    mm(X[:, 0, 16 + 4 * j:20 + 4 * j], row[1][:, blk(j)], ident[0:4, 0:4], start=False, stop=True, skip_group_check=True)
                    mm(X[:, 0, 64 + 4 * j:68 + 4 * j], row[3][:, blk(j)], ident[0:4, 0:4], start=False, stop=True, skip_group_check=True)
                for h in range(M_HEADS):
                    ins = mm(X[:, 0, 32 + 8 * h:40 + 8 * h], sel4[0:4, blk(h)], srow[:, 6, :], start=False, stop=True, skip_group_check=True)
                n.give(ins, ms["columns"])

            def mlstm(l):
                for pr in range(2):
                    transposes(X[:, 2 + pr, :], lambda j: z_km[:, j, pr * P:(pr + 1) * P], TB, ms["k_transposed"])
                n.take(ms["k_copied"], 2)
                for h in range(-1, M_HEADS + 1):
                    if 0 <= h < M_HEADS:
                        n.take(ms["k_end"])
                        for c in range(7):
                            r = slice(64 * (c % 2), 64 * (c % 2) + 64)
                            bank, i = m_bank(c)
                            ins = mm(G[:, bank, (P + 1) * i:(P + 1) * (i + 1)], tmp[r, 3, blk(c // 2)], z_vm[r, c // 2, h, :],
                                     start=True, stop=True, skip_group_check=True)
                        n.give(ins, ms["updates"])
                    if h >= 1:
                        n.take(ms["normed"])
                        transposes(G[:, 3, :], lambda j: yT[:, 3 + h, blk(j)], TB, ms["transposed"])
                    if h + 1 < M_HEADS:
                        pr, sel = (h + 1) // 2, sel4[0:4, blk(h + 1)]
                        if h >= 0:
                            n.take(ms["weights"])
                        mm(X[:, 0, :], identb, mk("ml", 0, 512), start=True, stop=False)
                        n.give(mm(X[:, 0, :], sel, row[2], start=False, stop=True), ms["exponents"])
                        n.take(ms["q_alone"])
                        for j in range(TB):
                            ins = mm(X[:, 1, blk(j)], tmp[:, (4, 6)[pr], blk(j)], tmp[:, 1, blk(j)], start=True, stop=True, skip_group_check=True)
                        n.give(ins, ms["scores"])
                        if h >= 0:
                            n.take(ms["q_decayed"])
                        if h >= 1:
                            n.take(ms["done"])
                        n.give(mm(G[:, 3, :], sel, row[0], start=True, stop=True), ms["decay"])
                    if 0 <= h < M_HEADS:
                        if h == M_HEADS - 1:
                            n.take(ms["weights"])
                            n.take(ms["q_decayed"])
                        n.take(ms["states"])
                        W, qs = tmp[:, (0, 5)[h % 2], :], tmp[:, (2, 7)[h % 2], :]
                        for j in range(TB):
                            mm(out_view[:, j, 0:P + 1], W[:, blk(j)], z_vm[:, j, h, :], start=j % 2 == 0, stop=False, skip_group_check=True)
                        for c in range(1, 8):
                            r = slice(64 * (c % 2), 64 * (c % 2) + 64)
                            ins = mm(out_view[r, c // 2, 0:P + 1], qs[:, 64 * c:64 * c + 64], m_state[:, c - 1, :],
                                     start=False, stop=c == 7, skip_group_check=True)
                        n.give(ins, ms["output"])
                n.take(ms["done"], 2)

            operand = {}

            def u_ready():
                operand[name] = (s_u, n.at(s_u))
                n.skip(s_u, KT)

            n.skip(s_fr, 2)
            fr = [0]

            def token_tiles(b, m):
                return [(m, (0, 512), (0, 512))]

            def z_tiles(b, m):
                if b == 1 and m == 1:
                    return [(j, (P, 2 * P), (j * P, (j + 1) * P)) for j in range(TB)]
                if b == 2:
                    return [(m, (0, 512), (0, 512))]
                if b == 3 and m < 2:
                    return [(2 * m + j, (0, 256), (256 * j, 256 * j + 256)) for j in range(2)]
                if b == 4 and m >= 2:
                    return (256 + 4 * (m - 2), 260 + 4 * (m - 2))
                return None

            for name in order:
                if name in ("hg_q", "hg_f", "hg_v", "hg_g"):
                    if name == "hg_q":
                        u_ready()
                    linear(name, u_hi, u_lo, token_tiles if name == "hg_v" else None,
                           ada=ADA_FIRST + 2 * ("hg_q", "hg_f", "hg_v", "hg_g").index(name))
                    if name == "hg_g":
                        hgrn()
                elif name in ("hg_out", "at_out"):
                    u_ready()
                    linear(name, u_hi, u_lo, ada=ADA_FIRST + 7 if name == "hg_out" else None, mid=norm_first_half)
                    norm_second_half()
                    norm()
                elif name.startswith("ffn_in"):
                    l, hf = int(name[-2]), int(name[-1])
                    if hf == 0:
                        u_ready()
                    linear(name, u_hi, u_lo, ada=(ADA_FIRST + 9 + 6 * hf) if l == 0 else None)
                    operand[f"ffn_out{l}{hf}"] = (s_fr, n.at(s_fr))
                    n.skip(s_fr, FF1_TILES[hf])
                elif name.startswith("ffn_out"):
                    linear(name, hid_hi, hid_lo, mid=norm_first_half if name[-1] == "1" else None)
                    if name[-1] == "1":
                        norm_second_half()
                        norm()
                elif name == "at_v":
                    u_ready()
                    linear(name, u_hi, u_lo, token_tiles)
                elif name.startswith("at_qk"):
                    linear(name, u_hi, u_lo)
                    attention(int(name[-1]))
                elif name.startswith("zg"):
                    linear(name, u_hi, u_lo, after=lambda b: gate_columns() if b == 3 else window_keys(name, b))
                    window_attention(int(name[-1]))
                    mlstm(int(name[-1]))
                elif name.startswith("z"):
                    u_ready()
                    linear(name, u_hi, u_lo, z_tiles, after=lambda b: window_keys(name, b))
                elif name.startswith("br"):
                    u_ready()
                    linear(name, u_hi, u_lo, x0=lambda b: 0 if b < 2 else 4)
                elif name.startswith("mo"):
                    u_ready()
                    linear(name, mx_hi, mx_lo, mid=norm_first_half)
                    norm_second_half()
                elif name.startswith("ff_in"):
                    if name[-1] == "0":
                        u_ready()
                    linear(name, u_hi, u_lo)
                    operand[f"ff_out{name[-2:]}"] = (s_fr, n.at(s_fr))
                    n.skip(s_fr, 16)
                elif name.startswith("ff_out"):
                    linear(name, ff_hi, ff_lo, mid=norm_first_half if name == "ff_out01" else None)
                    if name == "ff_out01":
                        norm_second_half()
            for e in ("act", "dve"):
                pe.wait_ge(s_free[e], sum(4 * plan[x]["blocks"] for x in order if plan[x]["evictor"] == e) + 4)
            for q in range(8):
                bank = (G if q < 4 else X)[:, q % 4, :]
                transposes(bank, lambda j: hT[:, 4 * (q % 2) + j, blk(q // 2)], 4, p2d)

    return plan


NAMES = ["x", "c", "positions", "ada_w", "ada_b", "norm_g", "hgrn_w_in", "hgrn_lower_bounds", "hgrn_norm_g",
         "hgrn_w_out", "attn_w_in", "attn_w_out", "ffn_w_in", "ffn_w_out", "norm_mix_2", "w_in_2", "att_q_norm_2",
         "att_k_norm_2", "att_sinks_2", "m_gate_bias_2", "m_head_norm_2", "w_att_branch_2", "w_m_branch_2",
         "w_out_2", "norm_ffn_2", "w_ff1_2", "w_ff2_2"]


def make(nc, inputs, stop=None):
    first, second, m = constants()
    con1, where1 = pack(first)
    con2, where2 = pack(second)
    masks, where3 = pack(m)
    arrays = {f"in_{k}": np.ascontiguousarray(inputs[k]) for k in NAMES}
    arrays.update(in_con1=con1, in_con2=con2, in_masks=masks)
    aps = {}
    for k, v in arrays.items():
        aps[k[3:]] = nc.dram_tensor(k, v.shape, mybir.dt.from_np(v.dtype), kind="ExternalInput").ap()
    out = nc.dram_tensor("out", (1, S, D), F32, kind="ExternalOutput").ap()
    build(nc, aps, out, where1, where2, where3, stop)
    return arrays


def kernel(**inputs):
    import concourse.bacc as bacc
    from concourse.bass_utils import run_bass_kernel_spmd

    nc = bacc.Bacc("TRN2", target_bir_lowering=False, num_devices=1, dynamic_dma_scratch_size=4096)
    arrays = make(nc, inputs)
    r = run_bass_kernel_spmd(nc, [arrays], core_ids=[0])
    return r.results[0]["out"]
```
